# Optimizing a Trainium2 kernel written in Bass

```python
import jax, jax.numpy as jnp
from jax import lax
import numpy as np
import math

D_MODEL = 1024
BATCH = 1
SEQ = 256
DEPTH = 2

GRID_W = 64
CTX_LEN = 256
HEAD_DIM = 64
NORM_EPS = 1e-6
POOL_WIDTH = D_MODEL // 4
POOL_WINDOWS = (2, 4, 8, 16)
POOL_GROUP = POOL_WIDTH // 4
GLA_WIDTH = D_MODEL // 4
GLA_DK = 64
GLA_DV = 64
GLA_HEADS = GLA_WIDTH // GLA_DV
GLA_GATE_RANK = 16
GLA_GATE_NORM = 16.0
GLA_CHUNK = 64
ATTN_WIDTH = D_MODEL // 2
ATTN_Q_HEADS = ATTN_WIDTH // HEAD_DIM
ATTN_KV_HEADS = ATTN_Q_HEADS // 4
ATTN_KV_WIDTH = ATTN_KV_HEADS * HEAD_DIM
Q_BLOCK = 128
ROPE_THETA = 10000.0
MLP_HIDDEN = 4 * D_MODEL
IN_SIZES = (POOL_WIDTH,
            GLA_HEADS * GLA_DK, GLA_HEADS * GLA_DK,
            GLA_WIDTH, GLA_WIDTH,
            GLA_GATE_RANK, GLA_GATE_RANK,
            ATTN_WIDTH, ATTN_KV_WIDTH, ATTN_KV_WIDTH)
IN_WIDTH = sum(IN_SIZES)
MIX_WIDTH = POOL_WIDTH + GLA_WIDTH + ATTN_WIDTH


def rmsnorm(x, g):
    xf = x.astype(jnp.float32)
    y = xf * lax.rsqrt(jnp.mean(xf * xf, axis=-1, keepdims=True) + NORM_EPS)
    return (y * g).astype(x.dtype)

def modulation(cvec, w_mod, b_mod):
    m = (jax.nn.silu(cvec) @ w_mod + b_mod)[..., None, :]
    return jnp.split(m, 6, axis=-1)

def split_in(u):
    idx = np.cumsum(np.array(IN_SIZES))[:-1].tolist()
    return jnp.split(u, idx, axis=-1)

def pool_mixer(p, w_pool, s_pool):
    B, N, _ = p.shape
    pg = p.reshape(B, N, 4, POOL_GROUP)
    pf = pg.astype(jnp.float32)
    P = jnp.concatenate([jnp.zeros((B, 1, 4, POOL_GROUP), jnp.float32), jnp.cumsum(pf, axis=1)], axis=1)
    t = np.arange(N)
    outs = []
    for gi, w in enumerate(POOL_WINDOWS):
        lo = np.clip(t - w // 2, 0, N - 1)
        hi = np.clip(t + w // 2 - 1, 0, N - 1)
        cnt = jnp.asarray((hi - lo + 1)[None, :, None], jnp.float32)
        Pg = P[:, :, gi]
        mean = (Pg[:, hi + 1] - Pg[:, lo]) / cnt
        outs.append(mean - pf[:, :, gi])
    m = jnp.stack(outs, axis=2)
    y = jnp.einsum('bngc,gcd->bngd', m, w_pool.astype(jnp.float32))
    return (y.reshape(B, N, POOL_WIDTH) * s_pool).astype(p.dtype)

def gla_features(q, k, v, r_f, r_b, w_gate, b_gate):
    B, N, _ = q.shape
    f32 = jnp.float32
    heads = lambda a: a.astype(f32).reshape(B, N, GLA_HEADS, -1)
    wg = w_gate.astype(f32)
    bg = b_gate.astype(f32)
    la_f = jax.nn.log_sigmoid(r_f.astype(f32) @ wg[0] + bg[0]) / GLA_GATE_NORM
    la_b = jax.nn.log_sigmoid(r_b.astype(f32) @ wg[1] + bg[1]) / GLA_GATE_NORM
    return heads(q) * GLA_DK ** -0.5, heads(k), heads(v), heads(la_f), heads(la_b)

def gla_chunk_scan(q, k, v, la, s0, strict):
    B, N, H, _ = q.shape
    C = GLA_CHUNK
    nc = N // C
    to_chunks = lambda a: a.reshape(B, nc, C, H, a.shape[-1]).transpose(1, 0, 3, 2, 4)
    mask = np.tril(np.ones((C, C), bool), k=-1 if strict else 0)[:, :, None]

    def step(S, inp):
        qc, kc, vc, lc = inp
        b = jnp.cumsum(lc, axis=2)
        o_inter = jnp.einsum('bhid,bhde->bhie', qc * jnp.exp(b), S)
        diff = b[:, :, :, None, :] - b[:, :, None, :, :]
        decay = jnp.exp(jnp.where(mask, diff, -jnp.inf))
        A = jnp.einsum('bhid,bhjd,bhijd->bhij', qc, kc, decay)
        o = o_inter + jnp.einsum('bhij,bhje->bhie', A, vc)
        bl = b[:, :, -1:, :]
        S_new = jnp.exp(bl[:, :, 0, :, None]) * S + jnp.einsum('bhjd,bhje->bhde', kc * jnp.exp(bl - b), vc)
        return S_new, o

    S, o = lax.scan(step, s0, (to_chunks(q), to_chunks(k), to_chunks(v), to_chunks(la)))
    return o.transpose(1, 0, 3, 2, 4).reshape(B, N, H, -1), S

def gla_bidir(q, k, v, la_f, la_b, s_f, s_b):
    o_f, s_f_new = gla_chunk_scan(q, k, v, la_f, s_f, strict=False)
    rev = lambda a: a[:, ::-1]
    o_b, s_b_new = gla_chunk_scan(rev(q), rev(k), rev(v), rev(la_b), s_b, strict=True)
    return o_f + rev(o_b), s_f_new, s_b_new

def gla_output(o, g, g_gla, out_dtype):
    B, N = o.shape[:2]
    gate = jax.nn.silu(g.astype(jnp.float32)).reshape(B, N, GLA_HEADS, GLA_DV)
    return (rmsnorm(o, g_gla) * gate).reshape(B, N, GLA_WIDTH).astype(out_dtype)

def attn_qkv(q, k, v, g_q, g_k):
    B, N, _ = q.shape
    q = rmsnorm(q.reshape(B, N, ATTN_Q_HEADS, HEAD_DIM), g_q)
    k = rmsnorm(k.reshape(B, N, ATTN_KV_HEADS, HEAD_DIM), g_k)
    return q, k, v.reshape(B, N, ATTN_KV_HEADS, HEAD_DIM)

def axial_rope(x, rows, cols):
    half = HEAD_DIM // 2
    inv = ROPE_THETA ** (-jnp.arange(0, half, 2, dtype=jnp.float32) / half)

    def rot(xh, pos):
        ang = pos.astype(jnp.float32)[:, None] * inv
        cos = jnp.cos(ang)[None, :, None, :]
        sin = jnp.sin(ang)[None, :, None, :]
        x1, x2 = jnp.split(xh.astype(jnp.float32), 2, axis=-1)
        return jnp.concatenate([x1 * cos - x2 * sin, x1 * sin + x2 * cos], axis=-1)

    xr, xc = jnp.split(x, 2, axis=-1)
    return jnp.concatenate([rot(xr, rows), rot(xc, cols)], axis=-1).astype(x.dtype)

def gqa_attend(qb, k, v):
    s = jnp.einsum('bqhgd,bkhd->bhgqk', qb, k, preferred_element_type=jnp.float32) * HEAD_DIM ** -0.5
    p = jax.nn.softmax(s, axis=-1)
    return jnp.einsum('bhgqk,bkhd->bqhgd', p.astype(v.dtype), v)

def latent_attention(q, k_all, v_all):
    B, N = q.shape[:2]
    G = ATTN_Q_HEADS // ATTN_KV_HEADS
    nb = N // Q_BLOCK
    qb = q.reshape(B, nb, Q_BLOCK, ATTN_KV_HEADS, G, HEAD_DIM).swapaxes(0, 1)
    ob = lax.map(lambda blk: gqa_attend(blk, k_all, v_all), qb)
    return ob.swapaxes(0, 1).reshape(B, N, ATTN_WIDTH)

def context_attention(q, k, v):
    B, L = q.shape[:2]
    G = ATTN_Q_HEADS // ATTN_KV_HEADS
    return gqa_attend(q.reshape(B, L, ATTN_KV_HEADS, G, HEAD_DIM), k, v).reshape(B, L, ATTN_WIDTH)

def squared_relu_mlp(h, w_up, w_down):
    return jnp.square(jax.nn.relu(h @ w_up)) @ w_down

def trunk_layer(x, cx, c, c_ctx, rows, cols, w_mod, b_mod, g_mix, w_in, w_pool, s_pool, w_gate, b_gate,
                g_gla, g_q, g_k, w_out, g_mlp, w_up, w_down, update_ctx):
    sh1, sc1, ga1, sh2, sc2, ga2 = modulation(c, w_mod, b_mod)
    sh1c, sc1c, ga1c, sh2c, sc2c, ga2c = modulation(c_ctx[None], w_mod, b_mod)

    u = (rmsnorm(x, g_mix) * (1 + sc1) + sh1) @ w_in
    uc = (rmsnorm(cx, g_mix) * (1 + sc1c) + sh1c) @ w_in
    p, gq, gk, gv, gg, rf, rb, aq, ak, av = split_in(u)
    pc, gqc, gkc, gvc, ggc, rfc, rbc, aqc, akc, avc = split_in(uc)

    B = x.shape[0]
    s_zero = jnp.zeros((B, GLA_HEADS, GLA_DK, GLA_DV), jnp.float32)
    o_gc, s_f, s_b = gla_bidir(*gla_features(gqc, gkc, gvc, rfc, rbc, w_gate, b_gate), s_zero, s_zero)
    o_gl, _, _ = gla_bidir(*gla_features(gq, gk, gv, rf, rb, w_gate, b_gate), s_f, s_b)

    qc_, kc_, vc_ = attn_qkv(aqc, akc, avc, g_q, g_k)
    ql, kl, vl = attn_qkv(aq, ak, av, g_q, g_k)
    ql = axial_rope(ql, rows, cols)
    kl = axial_rope(kl, rows, cols)
    k_all = jnp.concatenate([kc_, kl], axis=1)
    v_all = jnp.concatenate([vc_, vl], axis=1)

    mix = jnp.concatenate([pool_mixer(p, w_pool, s_pool),
                           gla_output(o_gl, gg, g_gla, x.dtype),
                           latent_attention(ql, k_all, v_all)], axis=-1) @ w_out
    x = x + ga1 * mix
    x = x + ga2 * squared_relu_mlp(rmsnorm(x, g_mlp) * (1 + sc2) + sh2, w_up, w_down)

    if update_ctx:
        mix_c = jnp.concatenate([pool_mixer(pc, w_pool, s_pool),
                                 gla_output(o_gc, ggc, g_gla, cx.dtype),
                                 context_attention(qc_, kc_, vc_)], axis=-1) @ w_out
        cx = cx + ga1c * mix_c
        cx = cx + ga2c * squared_relu_mlp(rmsnorm(cx, g_mlp) * (1 + sc2c) + sh2c, w_up, w_down)
    return x, cx

def first_inputs(seed: int = 0) -> dict:
    key = jax.random.key(seed)
    ks = jax.random.split(key, 20)
    D = D_MODEL
    nrm = lambda k, shape, scale: jax.random.normal(k, shape, jnp.float32) * scale
    return {
        "x": nrm(ks[0], (BATCH, SEQ, D), 1.0),
        "c": nrm(ks[1], (BATCH, D), 1.0),
        "ctx": nrm(ks[2], (BATCH, CTX_LEN, D), 1.0),
        "c_ctx": nrm(ks[3], (D,), 1.0),
        "w_mod": nrm(ks[4], (DEPTH, D, 6 * D), 0.5 * D ** -0.5),
        "b_mod": nrm(ks[5], (DEPTH, 6 * D), 0.01),
        "g_mix": 1.0 + nrm(ks[6], (DEPTH, D), 0.05),
        "w_in": nrm(ks[7], (DEPTH, D, IN_WIDTH), D ** -0.5),
        "w_pool": nrm(ks[8], (DEPTH, 4, POOL_GROUP, POOL_GROUP), POOL_GROUP ** -0.5),
        "s_pool": 1.0 + nrm(ks[9], (DEPTH, POOL_WIDTH), 0.1),
        "w_gate": nrm(ks[10], (DEPTH, 2, GLA_GATE_RANK, GLA_HEADS * GLA_DK), GLA_GATE_RANK ** -0.5),
        "b_gate": nrm(ks[11], (DEPTH, 2, GLA_HEADS * GLA_DK), 0.1),
        "g_gla": 1.0 + nrm(ks[12], (DEPTH, GLA_DV), 0.05),
        "g_q": 1.0 + nrm(ks[13], (DEPTH, HEAD_DIM), 0.05),
        "g_k": 1.0 + nrm(ks[14], (DEPTH, HEAD_DIM), 0.05),
        "w_out": nrm(ks[15], (DEPTH, MIX_WIDTH, D), MIX_WIDTH ** -0.5),
        "g_mlp": 1.0 + nrm(ks[16], (DEPTH, D), 0.05),
        "w_up": nrm(ks[17], (DEPTH, D, MLP_HIDDEN), D ** -0.5),
        "w_down": nrm(ks[18], (DEPTH, MLP_HIDDEN, D), MLP_HIDDEN ** -0.5),
        "g_final": 1.0 + nrm(ks[19], (D,), 0.05),
    }

def first_block(x, c, ctx, c_ctx, w_mod, b_mod, g_mix, w_in, w_pool, s_pool, w_gate, b_gate,
              g_gla, g_q, g_k, w_out, g_mlp, w_up, w_down, g_final):
    n_tok = x.shape[1]
    ROWS = n_tok // GRID_W
    rows = jnp.repeat(jnp.arange(ROWS, dtype=jnp.int32), GRID_W)
    cols = jnp.tile(jnp.arange(GRID_W, dtype=jnp.int32), ROWS)
    cx = ctx
    for l in range(DEPTH):
        x, cx = trunk_layer(x, cx, c, c_ctx, rows, cols, w_mod[l], b_mod[l], g_mix[l], w_in[l],
                            w_pool[l], s_pool[l], w_gate[l], b_gate[l], g_gla[l], g_q[l], g_k[l],
                            w_out[l], g_mlp[l], w_up[l], w_down[l], update_ctx=(l < DEPTH - 1))
    return rmsnorm(x, g_final)


FOX_HEADS = 4
FOX_HEAD_DIM = 64
MOBA_HEADS = 4
MOBA_HEAD_DIM = 64
MOBA_BLOCK = 256
MOBA_TOPK = 3
MOBA_Q_CHUNK = 32
MLA_HEADS = 8
MLA_NOPE_DIM = 64
MLA_ROPE_DIM = 32
MLA_V_DIM = 64
MLA_Q_RANK = 256
MLA_KV_RANK = 128
T5_BUCKETS = 32
T5_MAX_DISTANCE = 128
D_FF = -(-8 * D_MODEL // (3 * 256)) * 256
RMS_EPS = 1e-6

FOX_W = FOX_HEADS * FOX_HEAD_DIM
MOBA_W = MOBA_HEADS * MOBA_HEAD_DIM
MLA_W = MLA_HEADS * MLA_V_DIM
MIX_WIDTH_2 = FOX_W + MOBA_W + MLA_W
IN_SIZES_2 = (FOX_W, FOX_W, FOX_W, FOX_HEADS, MOBA_W, MOBA_W, MOBA_W, MLA_Q_RANK, MLA_KV_RANK, MLA_ROPE_DIM)
IN_WIDTH_2 = 3 * FOX_W + FOX_HEADS + 3 * MOBA_W + MLA_Q_RANK + MLA_KV_RANK + MLA_ROPE_DIM


def rmsnorm_2(x, g):
    x32 = x.astype(jnp.float32)
    y = x32 * lax.rsqrt(jnp.mean(x32 * x32, axis=-1, keepdims=True) + RMS_EPS)
    return (y * g.astype(jnp.float32)).astype(x.dtype)

def rope(x, pos):
    half = x.shape[-1] // 2
    inv_freq = 1.0 / (ROPE_THETA ** (jnp.arange(half, dtype=jnp.float32) / half))
    ang = pos.astype(jnp.float32)[:, None] * inv_freq[None, :]
    cos, sin = jnp.cos(ang), jnp.sin(ang)
    x32 = x.astype(jnp.float32)
    x1, x2 = x32[..., :half], x32[..., half:]
    return jnp.concatenate([x1 * cos - x2 * sin, x2 * cos + x1 * sin], axis=-1).astype(x.dtype)

def t5_bucket(dist):
    n = jnp.maximum(dist, 0)
    max_exact = T5_BUCKETS // 2
    nf = jnp.maximum(n, max_exact).astype(jnp.float32)
    large = max_exact + (jnp.log(nf / max_exact) / math.log(T5_MAX_DISTANCE / max_exact)
                         * (T5_BUCKETS - max_exact)).astype(jnp.int32)
    large = jnp.minimum(large, T5_BUCKETS - 1)
    return jnp.where(n < max_exact, n, large)

def dense_causal_attention(q, k, v, log_decay_cum=None):
    B, H, S, dk = q.shape
    dv = v.shape[-1]
    nqb = S // Q_BLOCK
    scale = dk ** -0.5
    kpos = jnp.arange(S)
    q_blocks = q.reshape(B, H, nqb, Q_BLOCK, dk).transpose(2, 0, 1, 3, 4)
    starts = jnp.arange(nqb, dtype=jnp.int32) * Q_BLOCK
    if log_decay_cum is None:
        xs = (q_blocks, starts)
    else:
        xs = (q_blocks, starts, log_decay_cum.reshape(B, H, nqb, Q_BLOCK).transpose(2, 0, 1, 3))

    def step(blk):
        q_i, t0 = blk[0], blk[1]
        s = jnp.einsum('bhqd,bhkd->bhqk', q_i, k).astype(jnp.float32) * scale
        if log_decay_cum is not None:
            s = s + blk[2][..., None] - log_decay_cum[:, :, None, :]
        qpos = t0 + jnp.arange(Q_BLOCK)
        s = jnp.where(kpos[None, :] <= qpos[:, None], s, -jnp.inf)
        p = jax.nn.softmax(s, axis=-1)
        return jnp.einsum('bhqk,bhkd->bhqd', p.astype(v.dtype), v)

    out = lax.map(step, xs)
    return out.transpose(1, 2, 0, 3, 4).reshape(B, H, S, dv)

def moba_attention(q, k, v, t5_table):
    B, H, S, d = q.shape
    nb = -(-S // MOBA_BLOCK)
    s_pad = nb * MOBA_BLOCK
    n_sel = min(MOBA_TOPK, nb)
    scale = d ** -0.5
    pad = ((0, 0), (0, 0), (0, s_pad - S), (0, 0))
    k_blocks = jnp.pad(k, pad).reshape(B, H, nb, MOBA_BLOCK, d)
    v_blocks = jnp.pad(v, pad).reshape(B, H, nb, MOBA_BLOCK, d)
    k_mean = jnp.mean(k_blocks.astype(jnp.float32), axis=3)
    qpos = jnp.arange(S)
    gate = jnp.einsum('bhsd,bhnd->bhsn', q.astype(jnp.float32), k_mean)
    past = jnp.arange(nb)[None, :] < (qpos // MOBA_BLOCK)[:, None]
    gate = jnp.where(past, gate, -jnp.inf)
    _, sel = lax.top_k(gate, n_sel)

    nc = S // MOBA_Q_CHUNK
    q_c = q.reshape(B, H, nc, MOBA_Q_CHUNK, d).transpose(2, 0, 1, 3, 4)
    sel_c = sel.reshape(B, H, nc, MOBA_Q_CHUNK, n_sel).transpose(2, 0, 1, 3, 4)
    starts = jnp.arange(nc, dtype=jnp.int32) * MOBA_Q_CHUNK
    table_t = t5_table.T
    b_ix = jnp.arange(B)[:, None, None, None]
    h_ix = jnp.arange(H)[None, :, None, None]
    offs = jnp.arange(MOBA_BLOCK)

    def step(blk):
        q_i, sel_i, t0 = blk
        own = t0 // MOBA_BLOCK
        qp = t0 + jnp.arange(MOBA_Q_CHUNK)
        k_g = k_blocks[b_ix, h_ix, sel_i]
        v_g = v_blocks[b_ix, h_ix, sel_i]
        kp_sel = sel_i[..., None] * MOBA_BLOCK + offs
        bias_sel = table_t[h_ix[..., None], t5_bucket(qp[:, None, None] - kp_sel)]
        s_sel = jnp.einsum('bhqd,bhqnkd->bhqnk', q_i, k_g).astype(jnp.float32) * scale + bias_sel
        s_sel = jnp.where((sel_i < own)[..., None], s_sel, -jnp.inf)
        k_own = lax.dynamic_index_in_dim(k_blocks, own, axis=2, keepdims=False)
        v_own = lax.dynamic_index_in_dim(v_blocks, own, axis=2, keepdims=False)
        dist_own = qp[:, None] - (own * MOBA_BLOCK + offs)[None, :]
        s_own = (jnp.einsum('bhqd,bhkd->bhqk', q_i, k_own).astype(jnp.float32) * scale
                 + table_t[:, t5_bucket(dist_own)])
        s_own = jnp.where(dist_own >= 0, s_own, -jnp.inf)
        n_flat = n_sel * MOBA_BLOCK
        s = jnp.concatenate([s_sel.reshape(B, H, MOBA_Q_CHUNK, n_flat), s_own], axis=-1)
        p = jax.nn.softmax(s, axis=-1).astype(v.dtype)
        p_sel = p[..., :n_flat].reshape(B, H, MOBA_Q_CHUNK, n_sel, MOBA_BLOCK)
        p_own = p[..., n_flat:]
        return (jnp.einsum('bhqnk,bhqnkd->bhqd', p_sel, v_g)
                + jnp.einsum('bhqk,bhkd->bhqd', p_own, v_own))

    out = lax.map(step, (q_c, sel_c, starts))
    return out.transpose(1, 2, 0, 3, 4).reshape(B, H, S, d)

def hybrid_mixer(h, w_in, b_forget, g_q_lat, w_uq, g_kv_lat, w_ukv, g_group, w_out, t5_table):
    B, S, _ = h.shape
    proj = h @ w_in
    split_points = np.cumsum(IN_SIZES_2)[:-1].tolist()
    q_f, k_f, v_f, f_logit, q_m, k_m, v_m, c_q, c_kv, k_r = jnp.split(proj, split_points, axis=-1)

    def heads(t, n):
        return t.reshape(B, S, n, -1).transpose(0, 2, 1, 3)

    def flat(o):
        return o.transpose(0, 2, 1, 3).reshape(B, S, -1)

    pos = jnp.arange(S)
    log_f = jax.nn.log_sigmoid((f_logit + b_forget).astype(jnp.float32))
    F = jnp.cumsum(log_f, axis=1).transpose(0, 2, 1)
    o_f = dense_causal_attention(heads(q_f, FOX_HEADS), heads(k_f, FOX_HEADS), heads(v_f, FOX_HEADS), F)
    o_m = moba_attention(heads(q_m, MOBA_HEADS), heads(k_m, MOBA_HEADS), heads(v_m, MOBA_HEADS), t5_table)
    q_lat = heads(rmsnorm_2(c_q, g_q_lat) @ w_uq, MLA_HEADS)
    q_nope, q_rot = q_lat[..., :MLA_NOPE_DIM], q_lat[..., MLA_NOPE_DIM:]
    kv = heads(rmsnorm_2(c_kv, g_kv_lat) @ w_ukv, MLA_HEADS)
    k_nope, v_c = kv[..., :MLA_NOPE_DIM], kv[..., MLA_NOPE_DIM:]
    k_rot = rope(k_r[:, None], pos)
    q_c = jnp.concatenate([q_nope, rope(q_rot, pos)], axis=-1)
    k_c = jnp.concatenate([k_nope, jnp.broadcast_to(k_rot, (B, MLA_HEADS, S, MLA_ROPE_DIM))], axis=-1)
    o_c = dense_causal_attention(q_c, k_c, v_c)
    g_a, g_b, g_c = jnp.split(g_group, [FOX_W, FOX_W + MOBA_W])
    o = jnp.concatenate([rmsnorm_2(flat(o_f), g_a), rmsnorm_2(flat(o_m), g_b), rmsnorm_2(flat(o_c), g_c)], axis=-1)
    return o @ w_out

def swiglu(h, w_gate_up, w_down):
    g, u = jnp.split(h @ w_gate_up, 2, axis=-1)
    return (jax.nn.silu(g) * u) @ w_down

def second_inputs(seed: int = 0) -> dict:
    key = jax.random.key(seed)
    ks = jax.random.split(key, 20)
    f32 = jnp.float32

    def nrm(k, shape, scale):
        return jax.random.normal(k, shape, f32) * scale

    def gain(k, shape):
        return 1.0 + 0.1 * jax.random.normal(k, shape, f32)

    L = DEPTH
    return {
        'x': nrm(ks[0], (BATCH, SEQ, D_MODEL), 1.0),
        'c': nrm(ks[1], (BATCH, D_MODEL), 1.0),
        't5_table': nrm(ks[2], (T5_BUCKETS, MOBA_HEADS), 0.5),
        'w_ada': nrm(ks[3], (L, D_MODEL, 6 * D_MODEL), D_MODEL ** -0.5),
        'b_ada': nrm(ks[4], (L, 6 * D_MODEL), 0.02),
        'g_mix_pre': gain(ks[5], (L, D_MODEL)),
        'g_mix_post': gain(ks[6], (L, D_MODEL)),
        'w_in': nrm(ks[7], (L, D_MODEL, IN_WIDTH_2), D_MODEL ** -0.5),
        'b_forget': 2.0 + 0.5 * jax.random.normal(ks[8], (L, FOX_HEADS), f32),
        'g_q_lat': gain(ks[9], (L, MLA_Q_RANK)),
        'w_uq': nrm(ks[10], (L, MLA_Q_RANK, MLA_HEADS * (MLA_NOPE_DIM + MLA_ROPE_DIM)), MLA_Q_RANK ** -0.5),
        'g_kv_lat': gain(ks[11], (L, MLA_KV_RANK)),
        'w_ukv': nrm(ks[12], (L, MLA_KV_RANK, MLA_HEADS * (MLA_NOPE_DIM + MLA_V_DIM)), MLA_KV_RANK ** -0.5),
        'g_group': gain(ks[13], (L, MIX_WIDTH_2)),
        'w_out': nrm(ks[14], (L, MIX_WIDTH_2, D_MODEL), MIX_WIDTH_2 ** -0.5),
        'g_ffn_pre': gain(ks[15], (L, D_MODEL)),
        'g_ffn_post': gain(ks[16], (L, D_MODEL)),
        'w_gate_up': nrm(ks[17], (L, D_MODEL, 2 * D_FF), D_MODEL ** -0.5),
        'w_down': nrm(ks[18], (L, D_FF, D_MODEL), D_FF ** -0.5),
    }

def second_block(x, c, t5_table, w_ada, b_ada, g_mix_pre, g_mix_post, w_in, b_forget, g_q_lat, w_uq,
              g_kv_lat, w_ukv, g_group, w_out, g_ffn_pre, g_ffn_post, w_gate_up, w_down):
    c_act = jax.nn.silu(c)
    for l in range(DEPTH):
        mod = (c_act @ w_ada[l] + b_ada[l])[:, None, :]
        shift_a, scale_a, gate_a, shift_f, scale_f, gate_f = jnp.split(mod, 6, axis=-1)
        h = rmsnorm_2(x, g_mix_pre[l]) * (1.0 + scale_a) + shift_a
        y = hybrid_mixer(h, w_in[l], b_forget[l], g_q_lat[l], w_uq[l], g_kv_lat[l], w_ukv[l],
                         g_group[l], w_out[l], t5_table)
        x = x + gate_a * rmsnorm_2(y, g_mix_post[l])
        h = rmsnorm_2(x, g_ffn_pre[l]) * (1.0 + scale_f) + shift_f
        x = x + gate_f * rmsnorm_2(swiglu(h, w_gate_up[l], w_down[l]), g_ffn_post[l])
    return x


def setup_inputs(seed=0):
    out = dict(first_inputs(seed))
    for name, value in second_inputs(seed + 1).items():
        if name != "x":
            out[name + "_2"] = value
    return out


def reference(
    x, c, ctx, c_ctx, w_mod, b_mod, g_mix, w_in, w_pool, s_pool, w_gate, b_gate, g_gla, g_q,
    g_k, w_out, g_mlp, w_up, w_down, g_final, c_2, t5_table_2, w_ada_2, b_ada_2, g_mix_pre_2,
    g_mix_post_2, w_in_2, b_forget_2, g_q_lat_2, w_uq_2, g_kv_lat_2, w_ukv_2, g_group_2,
    w_out_2, g_ffn_pre_2, g_ffn_post_2, w_gate_up_2, w_down_2,
):
    x = first_block(
        x, c, ctx, c_ctx, w_mod, b_mod, g_mix, w_in, w_pool, s_pool, w_gate, b_gate, g_gla, g_q,
        g_k, w_out, g_mlp, w_up, w_down, g_final,
    )
    return second_block(
        x, c_2, t5_table_2, w_ada_2, b_ada_2, g_mix_pre_2, g_mix_post_2, w_in_2, b_forget_2,
        g_q_lat_2, w_uq_2, g_kv_lat_2, w_ukv_2, g_group_2, w_out_2, g_ffn_pre_2, g_ffn_post_2,
        w_gate_up_2, w_down_2,
    )


_drawn_inputs = setup_inputs


def setup_inputs(seed=0):
    import zlib

    import numpy as np

    out = dict(_drawn_inputs(seed))
    spreads = {}
    factors = {'g_mix': 3.351,
     's_pool': 3.046,
     'b_gate': 8.0,
     'g_gla': 8.0,
     'g_q': 8.0,
     'g_k': 8.0,
     'g_q_lat_2': 4.394}
    for name, (base, spread) in spreads.items():
        noise = np.random.default_rng([zlib.crc32(name.encode()), seed]).standard_normal(out[name].shape)
        drawn = base * np.exp(spread * noise) if base else spread * noise
        out[name] = __import__('jax').numpy.asarray(drawn.astype(out[name].dtype))
    for name, factor in factors.items():
        out[name] = (out[name] * factor).astype(out[name].dtype)
    return out
```

```python
import math
import numpy as np
import concourse.bass as bass
from concourse import mybir
from contextlib import ExitStack

D = 1024
P = 128
KT = D // P
L = 2
S = 256
TS = S // P
MODC = 512
F1 = 4096
F2 = 2816
IN1 = 2080
IN2 = 1956
EPS = 1e-6
NEG = -1.0e30
GQ, GK, GV, GG, RF, AQ, AK, AV = 256, 512, 768, 1024, 1280, 1312, 1824, 1952
CH1 = [(0, 512), (512, 1024), (1024, 1312), (1312, 1824), (1824, 2080)]
QF, KF, VF, FL, QM, KM, VM, CQ, CKV, KR = 0, 256, 512, 768, 772, 1028, 1284, 1540, 1796, 1924
CH2 = [(489 * i, 489 * (i + 1)) for i in range(4)]
PAR1 = [("band", 2048), ("wg", 512), ("wpool", 256), ("g_q", 64), ("g_k", 64), ("g_gla", 64)]
PAR2 = [("w_uq", 1536), ("w_ukv", 1024), ("g_q_lat", 256), ("g_kv_lat", 128), ("g_group", 1024), ("b_forget", 4)]
CONST = [("ident", 128), ("up16", 128), ("lo16", 128), ("after16", 128), ("before16", 128), ("up", 128),
         ("ones", 128), ("mask_f", 128), ("mask_b", 32), ("causal", 256), ("rope1", 128), ("rope2", 64),
         ("sel", 256)]
NCONS = 4
RSTDS = 4 * L + 1 + 6 * L
NSLOT = 4
SLOT = 4096
HC2 = [(0, 8), (8, 15), (15, 22)]


def offsets(table):
    at, out = 0, {}
    for name, n in table:
        out[name] = (at, n)
        at += n
    return out, at


def loads():
    out = []
    for l in range(L):
        out += [("mod1", l, k) for k in range(6)]
        out += [("in1", l, c) for c in range(len(CH1))]
        out += [("par1", l, 0)]
        out += [("out1", l, n) for n in range(2)]
        out += [("mod1", l, k) for k in range(6, 12)]
        out += [("up1", l, c) for c in range(F1 // MODC)]
        out += [("down1", l, c) for c in range(8)]
    for l in range(L):
        out += [("mod2", l, k) for k in range(6)]
        out += [("in2", l, c) for c in range(len(CH2))]
        out += [("par2", l, 0)]
        out += [("out2", l, n) for n in range(2)]
        out += [("mod2", l, k) for k in range(6, 12)]
        out += [("up2", l, c) for c in range(F2 // 256)]
        out += [("down2", l, c) for c in range(2 * len(HC2))]
    return out


LOADS = loads()
PLACE = {key: i for i, key in enumerate(LOADS)}


def landed():
    at, out = [0] * NSLOT, {}
    for i, key in enumerate(LOADS):
        at[i % NSLOT] += 32 if key[0] == "up2" else 16
        out[key] = at[i % NSLOT]
    return out


LANDED = landed()


def in1_jobs(l):
    out = []
    for c, (c0, c1) in enumerate(CH1):
        for t in range(4):
            lo, hi = 0, c1 - c0
            if l == L - 1 and t >= 2:
                if c in (0, 3):
                    continue
                if c == 2:
                    lo = RF - c0
            out.append((c, t, lo, hi, "va"[len(out) % 2]))
    return out


def units1(l):
    return [(2 * s + q, h, 256 * s) for s in range(2 if l < L - 1 else 1) for q in range(TS) for h in range(8)]


UNITS2 = [(kind, h, q) for q in range(TS) for kind, n in (("fox", 4), ("moba", 4), ("mla", 8)) for h in range(n)]
STATES = [((2, 3), (3, 2)), ((3, 0), (2, 1)), ((0, 1), (1, 0))]


SCALE2 = {"fox": 1.0, "moba": 0.125, "mla": 96.0 ** -0.5}


def counter():
    seen = {}

    def nth(sem, k=1):
        seen[sem.name] = seen.get(sem.name, 0) + k
        return seen[sem.name]
    return nth


def trunks(nc, a, out):
    f32 = mybir.dt.float32
    ALU = mybir.AluOpType
    ACT = mybir.ActivationFunctionType
    X_AXIS = mybir.AxisListType.X
    ctx = ExitStack()
    with ctx:
        def sb(name, shape):
            return ctx.enter_context(nc.sbuf_tensor(name, shape, f32))

        def sem(name):
            return ctx.enter_context(nc.semaphore(name))

        X = sb("X", [P, 4, D])
        actT = sb("actT", [P, KT, 512])
        ring = sb("ring", [P, NSLOT, SLOT])
        arena = sb("arena", [P, 20480])
        GA = sb("GA", [P, 2, D])
        cons_at, cons_n = offsets(CONST)
        cons = sb("cons", [P, cons_n])
        cols = sb("cols", [P, 92])
        csig = sb("csig", [P, 24])
        cT = sb("cT", [P, 3, KT])
        row = sb("row", [2, 3, MODC])
        modT = sb("modT", [P, 2, KT, 2])
        t5 = sb("t5", [P, 4, S])
        post = GA[0:1, 1, :]
        ms = sb("ms", [P, 64])
        rs = sb("rs", [P, 64])
        neghalf = sb("neghalf", [P, 64])
        ss = sb("ss", [P, 48])
        rsum = sb("rsum", [P, 4])
        mx = sb("mx", [P, 2])
        nm = sb("nm", [P, 2])
        rinv = sb("rinv", [P, 2])

        def const(name):
            at, n = cons_at[name]
            return cons[:, at:at + n]

        ident = const("ident")
        ones = const("ones")
        sel = const("sel").rearrange("p (s q) -> p s q", s=2)
        gcol = cols[:, 24:88].rearrange("p (w l k) -> p w l k", w=4, l=2)
        spool = cols[:, 88:92].rearrange("p (l g) -> p l g", l=2)

        def carve(start, *shape):
            n = int(np.prod(shape))
            v = arena[:, start:start + n]
            assert start + n <= 20480, (start, shape)
            if len(shape) == 2:
                v = v.rearrange("p (a b) -> p a b", a=shape[0])
            elif len(shape) == 3:
                v = v.rearrange("p (a b c) -> p a b c", a=shape[0], b=shape[1])
            return v

        xn = carve(0, 4, D)
        u = carve(0, 4, IN1)
        mixt = carve(8320, 4, 768)
        la = carve(11392, 4, 512)
        qgT = carve(13440, 2, 512)
        kgT = carve(14464, 2, 512)
        zt = carve(15488, 4, 512)
        ke4 = carve(15488, 4, 512)
        bT = carve(15488, 4, P)
        qk64 = carve(16000, 4, P)
        qk32 = carve(16512, 4, P)
        qk96 = carve(16000, 1024)
        qd = carve(17024, 4, P)
        kd = carve(17536, 4, P)
        qi = carve(18048, 4, P)
        AT = carve(18560, 4, P)
        rT = arena[0:33, 18560:19072]
        St = carve(19072, 4, 256)
        atb = carve(20096, 4, 32)
        dec = carve(20224, 16)
        gsq = carve(13440, 4, 256)
        gexp = carve(14464, 4, 256)
        qT = carve(11392, 4, 512)
        kT = carve(13440, 2, 512)
        Pr = carve(14464, 2, 512)
        PT = carve(15488, 2, 512)
        mT = carve(16512, 2, 512)
        tmp = carve(17536, 640)
        kdup = carve(18176, 4, 256)
        hid = carve(0, 32, 512)
        tmpx = carve(16384, 2, 512)
        u2 = carve(0, 2, IN2)
        y2 = carve(0, 2, D)
        qa = carve(3912, 8, 66)
        ka = carve(4440, 8, 66)
        qfT = carve(4968, 4, S)
        kfT = carve(5992, 4, S)
        qmT = carve(7016, 2, S)
        kmT = carve(7528, 2, S)
        cqT = carve(8040, 2, S)
        ckvT = carve(8552, S)
        ql = carve(8808, 2, 768)
        kc = carve(10344, 2, 768)
        vv = carve(11880, 2, 512)
        qcT = carve(12904, 8, S)
        kcT = carve(14952, 8, S)
        S2 = carve(17000, 2, S)
        P2 = carve(17512, 2, S)
        PT2 = carve(18024, 2, S)
        mix2 = carve(8808, 2, D)
        Fc = carve(18536, 2, 4)
        lf = carve(18544, 2, 4)
        lft = carve(18552, 2, 4)
        tmp2 = carve(18560, 1920)
        hid2 = carve(4096, 22, S)
        sg2 = carve(10240, 2, S)

        bank = [ctx.enter_context(nc.psum_tensor(f"bank{i}", [P, 512], f32)) for i in range(8)]
        VB, AB, SB = bank[0:4], bank[4:6], bank[6:8]

        names = """cons_in slot_read post_in t5_stored t5_in out_stored
            v_filled v_emptied a_filled a_emptied s_filled s_emptied v_step a_step
            ms_ready rstd_ready pool_ready cexp_ready cT_ready row_ready
            x_in gf_in x_ready sq_ready xn_ready zlog_ready la_ready exps_in exps_out qk_ready
            ke_ready AT_ready gexp_ready aq_ready nm_ready mixt_ready hid_ready
            fneg_ready flog_ready lf_ready qa_ready lat_ready heads_ready p2_ready sg_ready""".split()
        (cons_in, slot_read, post_in, t5_stored, t5_in, out_stored,
         v_filled, v_emptied, a_filled, a_emptied, s_filled, s_emptied, v_step, a_step,
         ms_ready, rstd_ready, pool_ready, cexp_ready, cT_ready, row_ready,
         x_in, gf_in, x_ready, sq_ready, xn_ready, zlog_ready, la_ready, exps_in, exps_out, qk_ready,
         ke_ready, AT_ready, gexp_ready, aq_ready, nm_ready, mixt_ready, hid_ready,
         fneg_ready, flog_ready, lf_ready, qa_ready, lat_ready, heads_ready,
         p2_ready, sg_ready) = [sem(n) for n in names]
        slot_in = [sem(f"slot_in{i}") for i in range(NSLOT)]
        row_in = [sem(f"row_in{i}") for i in range(3)]
        p1at, p1n = offsets(PAR1)
        p2at, p2n = offsets(PAR2)

        def slot(key):
            return ring[:, PLACE[key] % NSLOT, :]

        def slot_wait(eng, key):
            eng.wait_ge(slot_in[PLACE[key] % NSLOT], LANDED[key])

        def par(at, key, name):
            s, n = at[name]
            return slot(key)[:, s:s + n]

        def par1(l, name):
            return par(p1at, ("par1", l, 0), name)

        def par2(l, name):
            return par(p2at, ("par2", l, 0), name)

        def bc(ap, at, n):
            ap = ap.unsqueeze(at)
            shape = list(ap.shape)
            shape[at] = n
            return ap.broadcast_to(shape)

        t5hot = arena[0:32, 18560:19072]
        t5tab = arena[0:32, 19072:19076]
        t5col = arena[0:32, 11264:11776].rearrange("p (h n) -> p h n", h=4)
        t5rows = carve(9216, 4, 512)
        gf = arena[:, 8192:9216]
        mark = {}

        def tiles1(l):
            return [0, 1, 2, 3] if l < L - 1 else [0, 1]

        block = ctx.enter_context(nc.Block())

        @block.sync
        def _(sp):
            rows = 0
            for i, key in enumerate(LOADS):
                kind, l, c = key
                dst = ring[:, i % NSLOT, :]
                if kind in ("mod1", "mod2"):
                    if rows >= 3:
                        sp.wait_ge(row_ready, rows)
                    bias = a["b_mod"] if kind == "mod1" else a["b_ada_2"]
                    src = bias[l:l + 1, c * MODC:(c + 1) * MODC]
                    sp.dma_start(row[0:2, rows % 3, :], src.partition_broadcast(2)).then_inc(row_in[rows % 3], 16)
                    rows += 1
                if kind == "mod2" and c % 6 == 0:
                    sp.wait_ge(x_ready, 2 * L + 1 + 2 * l + c // 6)
                    gain = a["g_mix_post_2"] if c < 6 else a["g_ffn_post_2"]
                    sp.dma_start(post, gain[l:l + 1, :]).then_inc(post_in, 16)
                if i >= NSLOT:
                    sp.wait_ge(slot_read, i - NSLOT + 1)
                full = dst.rearrange("p (k n) -> p k n", n=MODC)
                if kind in ("mod1", "mod2"):
                    w = a["w_mod"] if kind == "mod1" else a["w_ada_2"]
                    src = w[l, :, c * MODC:(c + 1) * MODC].rearrange("(k p) n -> p k n", p=P)
                    sp.dma_start(full, src).then_inc(slot_in[i % NSLOT], 16)
                elif kind in ("in1", "in2"):
                    c0, c1 = CH1[c] if kind == "in1" else CH2[c]
                    w = a["w_in"] if kind == "in1" else a["w_in_2"]
                    src = w[l, :, c0:c1].rearrange("(k p) n -> p k n", p=P)
                    sp.dma_start(full[:, :, 0:c1 - c0], src).then_inc(slot_in[i % NSLOT], 16)
                elif kind in ("out1", "out2"):
                    w = a["w_out"] if kind == "out1" else a["w_out_2"]
                    src = w[l, :, c * MODC:(c + 1) * MODC].rearrange("(k p) n -> p k n", p=P)
                    sp.dma_start(full, src).then_inc(slot_in[i % NSLOT], 16)
                elif kind == "up1":
                    src = a["w_up"][l, :, c * MODC:(c + 1) * MODC].rearrange("(k p) n -> p k n", p=P)
                    sp.dma_start(full, src).then_inc(slot_in[i % NSLOT], 16)
                elif kind == "up2":
                    src = a["w_gate_up_2"][l].rearrange("(k p) (g n) -> p k g n", p=P, g=2)
                    for g in range(2):
                        sp.dma_start(full[:, :, g * 256:(g + 1) * 256],
                                     src[:, :, g, c * 256:(c + 1) * 256]).then_inc(slot_in[i % NSLOT], 16)
                elif kind == "down1":
                    half, kc_ = c // 4, c % 4
                    src = a["w_down"][l, kc_ * D:(kc_ + 1) * D, half * MODC:(half + 1) * MODC]
                    sp.dma_start(full, src.rearrange("(k p) n -> p k n", p=P)).then_inc(slot_in[i % NSLOT], 16)
                elif kind == "down2":
                    half, (k0, k1) = c // 3, HC2[c % 3]
                    src = a["w_down_2"][l, k0 * P:k1 * P, half * MODC:(half + 1) * MODC]
                    sp.dma_start(full[:, 0:k1 - k0, :], src.rearrange("(k p) n -> p k n", p=P))\
                      .then_inc(slot_in[i % NSLOT], 16)
                else:
                    w, n = (a["par1"], p1n) if kind == "par1" else (a["par2"], p2n)
                    sp.dma_start(dst[:, 0:n], w[l]).then_inc(slot_in[i % NSLOT], 16)
            sp.wait_ge(x_ready, 4 * L + 1)
            sp.dma_start(out[0].rearrange("(t p) d -> p t d", p=P), X[:, 0:2, :]).then_inc(out_stored, 16)
            sp.wait_ge(out_stored, 16)

        @block.gpsimd
        def _(pool):
            nc.gpsimd.memset(neghalf[:, :], -0.5).then_inc(pool_ready, 1)
            nc.gpsimd.memset(ms[:, :], 1.0).then_inc(pool_ready, 1)
            pool.wait_ge(v_emptied, 4)
            pool.dma_start(a["t5_rows"], t5rows).then_inc(t5_stored, 16)
            pool.wait_ge(t5_stored, 16)
            band_src = bass.AP(tensor=a["t5_rows"].tensor, offset=P - 1, ap=[[4 * 512 - 1, P], [512, 4], [1, S]])
            pool.dma_start(t5[:, :, :], band_src).then_inc(t5_in, 16)
            pool.wait_ge(pool_ready, 2)
            for i in range(RSTDS):
                pool.wait_ge(ms_ready, i + 1)
                nc.gpsimd.tensor_tensor(rs[:, :], ms[:, :], neghalf[:, :], ALU.pow).then_inc(rstd_ready, 1)

        @block.tensor
        def _(pe):
            nth = counter()
            k = {"v": 0, "a": 0, "s": 0, "unread": 0, "open": 0}
            rings = {"v": (VB, v_filled, v_emptied), "a": (AB, a_filled, a_emptied), "s": (SB, s_filled, s_emptied)}

            def take(r):
                banks, filled, emptied = rings[r]
                if k[r] >= len(banks):
                    pe.wait_ge(emptied, k[r] - len(banks) + 1)
                k[r] += 1
                return banks[(k[r] - 1) % len(banks)], filled

            def emptied(r):
                if k[r]:
                    pe.wait_ge(rings[r][2], k[r])

            def mm(out_, lhsT, rhs, start=True, stop=True, inc=None):
                ins = nc.tensor.matmul(out_, lhsT, rhs, start=start, stop=stop)
                if inc is not None:
                    ins.then_inc(inc, 1)
                elif k["unread"]:
                    ins.then_inc(slot_read, 1)
                    k["unread"] -= 1

            def tr(out_, in_, inc=None):
                n = in_.shape[0]
                ins = nc.tensor.transpose(out_, in_, ident[0:n, 0:n])
                if inc is not None:
                    ins.then_inc(inc, 1)
                elif k["unread"]:
                    ins.then_inc(slot_read, 1)
                    k["unread"] -= 1

            def through():
                k["unread"] += k["open"]
                k["open"] = 0

            def weights(key):
                through()
                slot_wait(pe, key)
                k["open"] = 1
                return slot(key).rearrange("p (k n) -> p k n", n=MODC)

            def contract(out_, lhs, rhs, inc, n=KT):
                for i in range(n):
                    mm(out_, lhs(i), rhs(i), i == 0, i == n - 1, inc if i == n - 1 else None)

            def modulation(kind, l, part):
                v0, m = (0, 2) if kind == "mod1" else (2, 1)
                for j in range(7):
                    if j < 6:
                        w = weights((kind, l, 6 * part + j))
                        b, filled = take("v")
                        contract(b[0:m, :], lambda i: cT[:, v0:v0 + m, i], lambda i: w[:, i, :], filled)
                    if j >= 1:
                        pe.wait_ge(row_ready, nth(row_ready))
                        r = row[0:m, (nth(row_ready, 0) - 1) % 3, :]
                        if j - 1 < 4:
                            b, filled = take("v")
                            for q in range(4):
                                tr(b[:, m * q:m * q + m], r[:, q * P:(q + 1) * P], filled if q == 3 else None)
                        else:
                            for s in range(m):
                                b, filled = take("v")
                                mm(b[:, :], sel[0:m, s, :], r, inc=filled)

            def turn(tiles, width, src):
                for ft in range(KT):
                    b, filled = take("va"[ft % 2])
                    for n, t in enumerate(tiles):
                        tr(b[:, n * P:(n + 1) * P], src(ft, t), filled if n == len(tiles) - 1 else None)

            def normed(tiles):
                pe.wait_ge(xn_ready, nth(xn_ready))
                turn(tiles, 512, lambda ft, t: xn[:, t, ft * P:(ft + 1) * P])
                emptied("v")
                emptied("a")

            def gla(l):
                par = ("par1", l, 0)
                slot_wait(pe, par)
                b, filled = take("v")
                for t in range(4):
                    tr(b[0:32, t * P:(t + 1) * P], u[:, t, RF:RF + 32], filled if t == 3 else None)
                emptied("v")
                for t in range(4):
                    b, filled = take("v")
                    mm(b[:, :], rT[:, t * P:(t + 1) * P], par1(l, "wg")[0:33, :], inc=filled)
                    mark["z", l, t] = k["v"]
                for col, tiles in ((GQ, tiles1(l)), (GK, tiles1(l))):
                    for hp in range(2):
                        b, filled = take("a")
                        for n, t in enumerate(tiles):
                            tr(b[:, t * P:(t + 1) * P], u[:, t, col + P * hp:col + P * (hp + 1)],
                               filled if n == len(tiles) - 1 else None)
                pe.wait_ge(la_ready, nth(la_ready))
                b, filled = take("a")
                for t in range(4):
                    for j in range(4):
                        mm(b[:, 4 * t + j:4 * t + j + 1], la[:, t, j * P:(j + 1) * P], const("up16")[:, P - 1:P],
                           inc=filled if t == 3 and j == 3 else None)
                for t in range(4):
                    b, filled = take("a")
                    mm(b[:, 0:256], const("after16"), la[:, t, 0:256])
                    mm(b[:, 256:512], const("before16"), la[:, t, 256:512], inc=filled)
                mark["dec", l] = k["a"] - 4
                pe.wait_ge(ke_ready, nth(ke_ready))
                for pair in STATES:
                    for d, (t, _) in enumerate(pair):
                        b, filled = take("v")
                        for h in range(4):
                            mm(b[64 * (h % 2):64 * (h % 2) + 64, 64 * (h // 2):64 * (h // 2) + 64],
                               ke4[:, t, 256 * d + 64 * h:256 * d + 64 * h + 64],
                               u[:, t, GV + 64 * h:GV + 64 * h + 64], inc=filled if h == 3 else None)
                emptied("v")
                for t in tiles1(l):
                    b, filled = take("a")
                    for d in range(2):
                        for hp in range(2):
                            j = 2 * d + hp
                            mm(b[:, j * P:(j + 1) * P], la[:, t, j * P:(j + 1) * P],
                               const("up16" if d == 0 else "lo16"), inc=filled if j == 3 else None)
                    mark["bT", l, t] = k["a"]
                    pe.wait_ge(qk_ready, nth(qk_ready))
                    for par_ in range(2):
                        b, filled = take("s")
                        po = 64 * par_
                        for hp in range(2):
                            o = P * hp

                            def block_(j0, i0, n, kk, qq, d, o_=None, inc=None):
                                at = o + i0 if o_ is None else o_
                                mm(b[j0:j0 + n, at:at + n], kk[po:po + 64, 2 * d + hp, j0:j0 + n],
                                   qq[po:po + 64, 2 * d + hp, i0:i0 + n], inc=inc)

                            block_(0, 64, 64, qk64, qk64, 0)
                            block_(64, 0, 64, qk64, qk64, 1)
                            for B in (0, 64):
                                block_(B, B + 32, 32, qk32, qk32, 0)
                                block_(B + 32, B, 32, qk32, qk32, 1)
                            for B in range(0, P, 32):
                                block_(B, B, 32, kd, qd, 0)
                                block_(B, B, 32, kd, qd, 1, 256 + 32 * hp, filled if hp == 1 and B == 96 else None)
                    pe.wait_ge(AT_ready, nth(AT_ready))
                    for par_ in range(2):
                        b, filled = take("v")
                        po = 64 * par_
                        for hp in range(2):
                            o_ = b[:, 64 * hp:64 * hp + 64]
                            h = 2 * hp + par_
                            dirs = [d for d in range(2) if not (d == 0 and t == 2) and not (d == 1 and t == 3)]
                            mm(o_, AT[:, 2 * par_ + hp, :], u[:, t, GV + 64 * h:GV + 64 * h + 64], True, False)
                            for d in dirs:
                                j = 2 * d + hp
                                last = d == dirs[-1]
                                mm(o_, qi[po:po + 64, j, :], St[po:po + 64, t, 64 * j:64 * j + 64], False, last,
                                   filled if last and hp == 1 else None)

            def pooling(l):
                n = S if l == L - 1 else 512
                band = par1(l, "band").rearrange("p (t g n) -> p t g n", t=2, g=4)
                for g in range(2):
                    b, filled = take("a")
                    for s in range(n // S):
                        for par_ in range(2):
                            for t in range(2):
                                end = s == n // S - 1 and par_ == 1 and t == 1
                                mm(b[64 * par_:64 * par_ + 64, S * s:S * s + S],
                                   u[:, 2 * s + t, P * g + 64 * par_:P * g + 64 * par_ + 64],
                                   band[:, t, 2 * g + par_, :], t == 0, t == 1, filled if end else None)
                emptied("a")
                for g in range(2):
                    b, filled = take("v")
                    mm(b[:, 0:n], par1(l, "wpool").rearrange("p (g n) -> p g n", g=2)[:, g, :], mT[:, g, 0:n],
                       inc=filled)

            def attention1(l):
                pe.wait_ge(aq_ready, nth(aq_ready))
                tiles = tiles1(l)
                for j in range(4):
                    b, filled = take("va"[j % 2])
                    for n, t in enumerate(tiles):
                        tr(b[:, t * P:(t + 1) * P], u[:, t, AQ + P * j:AQ + P * (j + 1)],
                           filled if n == len(tiles) - 1 else None)
                for g in range(2):
                    b, filled = take("v")
                    for t in range(4):
                        tr(b[:, t * P:(t + 1) * P], kdup[:, t, P * g:P * (g + 1)], filled if t == 3 else None)
                emptied("v")
                emptied("a")
                units = units1(l)
                s0, a0 = k["s"], k["a"]
                for i in range(len(units) + 2):
                    if i < len(units):
                        t, h, k0 = units[i]
                        b, filled = take("s")
                        po = 64 * (h % 2)
                        mm(b[:, 0:512 - k0], qT[po:po + 64, h // 2, t * P:(t + 1) * P],
                           kT[po:po + 64, h // 4, k0:512], inc=filled)
                    if 1 <= i <= len(units):
                        t, h, k0 = units[i - 1]
                        pe.wait_ge(s_emptied, s0 + i)
                        b, filled = take("a")
                        n = (512 - k0) // P
                        for c in range(n):
                            tr(b[:, c * P:(c + 1) * P], Pr[:, (i - 1) % 2, c * P:(c + 1) * P],
                               filled if c == n - 1 else None)
                    if i >= 2:
                        t, h, k0 = units[i - 2]
                        pe.wait_ge(a_emptied, a0 + i - 1)
                        b, filled = take("v")
                        n = (512 - k0) // P
                        contract(b[:, 0:64], lambda c: PT[:, i % 2, c * P:(c + 1) * P],
                                 lambda c: u[:, k0 // P + c, AV + 64 * (h // 4):AV + 64 * (h // 4) + 64], filled, n)

            def layer1(l):
                modulation("mod1", l, 0)
                normed([0, 1, 2, 3])
                last_c, w = -1, None
                for c, t, lo, hi, r in in1_jobs(l):
                    if c != last_c:
                        last_c, w = c, weights(("in1", l, c))
                    b, filled = take(r)
                    contract(b[:, 0:hi - lo], lambda i: actT[:, i, t * P:(t + 1) * P], lambda i: w[:, i, lo:hi], filled)
                through()
                mark["in1", l] = k["a"]
                emptied("v")
                emptied("a")
                gla(l)
                pooling(l)
                attention1(l)
                emptied("v")
                for j in range(6):
                    b, filled = take("va"[j % 2])
                    for n, t in enumerate(tiles1(l)):
                        tr(b[:, t * P:(t + 1) * P], mixt[:, t, j * P:(j + 1) * P],
                           filled if n == len(tiles1(l)) - 1 else None)
                emptied("v")
                emptied("a")
                k["open"] = 1
                for half in range(2):
                    w = weights(("out1", l, half))
                    for t in tiles1(l):
                        b, filled = take("v")
                        contract(b[:, :], lambda i: actT[:, i, t * P:(t + 1) * P], lambda i: w[:, i, :], filled)
                modulation("mod1", l, 1)
                normed(tiles1(l))
                n = P * len(tiles1(l))
                for c in range(F1 // MODC):
                    w = weights(("up1", l, c))
                    for m in range(4):
                        b, filled = take("a")
                        contract(b[:, 0:n], lambda i: w[:, i, m * P:(m + 1) * P], lambda i: actT[:, i, 0:n], filled)
                for half in range(2):
                    banks = [take("v") for t in tiles1(l)]
                    for c in range(4):
                        w = weights(("down1", l, 4 * half + c))
                        if half == 0:
                            pe.wait_ge(hid_ready, nth(hid_ready, 8))
                        for t, (b, filled) in zip(tiles1(l), banks):
                            for i in range(8):
                                mm(b[:, :], hid[:, 8 * c + i, t * P:(t + 1) * P], w[:, i, :], c == 0 and i == 0,
                                   c == 3 and i == 7, filled if c == 3 and i == 7 else None)

            def layer2(l):
                modulation("mod2", l, 0)
                normed([0, 1])
                for c, (c0, c1) in enumerate(CH2):
                    w = weights(("in2", l, c))
                    for t in range(TS):
                        b, filled = take("va"[t])
                        contract(b[:, 0:c1 - c0], lambda i: actT[:, i, t * P:(t + 1) * P],
                                 lambda i: w[:, i, 0:c1 - c0], filled)
                through()
                mark["in2", l] = k["a"]
                emptied("v")
                emptied("a")
                slot_wait(pe, ("par2", l, 0))
                for col in (QM, KM):
                    b, filled = take("a")
                    for hp in range(2):
                        for t in range(TS):
                            tr(b[:, S * hp + t * P:S * hp + (t + 1) * P], u2[:, t, col + P * hp:col + P * (hp + 1)],
                               filled if hp == 1 and t == 1 else None)
                pe.wait_ge(lf_ready, nth(lf_ready))
                b, filled = take("v")
                mm(b[:, 0:4], const("up"), lf[:, 0, :])
                mm(b[:, 4:8], ones, lf[:, 0, :], True, False)
                mm(b[:, 4:8], const("up"), lf[:, 1, :], False, True, filled)
                pe.wait_ge(lat_ready, nth(lat_ready))
                b, filled = take("v")
                for i in range(2):
                    for t in range(TS):
                        tr(b[:, S * i + t * P:S * i + (t + 1) * P], u2[:, t, CQ + i * P:CQ + (i + 1) * P],
                           filled if i == 1 and t == 1 else None)
                b, filled = take("v")
                for t in range(TS):
                    tr(b[:, t * P:(t + 1) * P], u2[:, t, CKV:KR], filled if t == 1 else None)
                emptied("v")
                wq = par2(l, "w_uq").rearrange("p (k n) -> p k n", k=2)
                wkv = par2(l, "w_ukv")
                for t in range(TS):
                    for n in range(2):
                        b, filled = take("v")
                        contract(b[:, 0:384], lambda i: cqT[:, i, t * P:(t + 1) * P],
                                 lambda i: wq[:, i, 384 * n:384 * (n + 1)], filled, 2)
                    for n in range(2):
                        b, filled = take("a")
                        mm(b[:, :], ckvT[:, t * P:(t + 1) * P], wkv[:, 512 * n:512 * (n + 1)], inc=filled)
                mark["kv", l] = k["a"]
                pe.wait_ge(qa_ready, nth(qa_ready))
                for src, n in ((qa, 0), (ka, 1)):
                    for hp in range(2):
                        b, filled = take("va"[n])
                        for e in range(2):
                            for t in range(TS):
                                tr(b[0:66, S * e + t * P:S * e + (t + 1) * P], src[:, 4 * t + 2 * hp + e, :],
                                   filled if e == 1 and t == 1 else None)
                pe.wait_ge(heads_ready, nth(heads_ready))
                emptied("a")
                for src, n in ((ql, 0), (kc, 1)):
                    for hp in range(4):
                        b, filled = take("va"[n])
                        for e in range(2):
                            for t in range(TS):
                                h = 2 * hp + e
                                tr(b[0:96, S * e + t * P:S * e + (t + 1) * P], src[:, t, 96 * h:96 * h + 96],
                                   filled if e == 1 and t == 1 else None)
                emptied("v")
                emptied("a")
                s0, a0 = k["s"], k["a"]
                for i in range(len(UNITS2) + 2):
                    if i < len(UNITS2):
                        kind, h, q = UNITS2[i]
                        n = P * (q + 1)
                        b, filled = take("s")
                        if kind == "fox":
                            lhs, rhs = qfT[0:66, h, q * P:(q + 1) * P], kfT[0:66, h, 0:n]
                        elif kind == "moba":
                            po = 64 * (h % 2)
                            lhs, rhs = qmT[po:po + 64, h // 2, q * P:(q + 1) * P], kmT[po:po + 64, h // 2, 0:n]
                        else:
                            lhs, rhs = qcT[0:96, h, q * P:(q + 1) * P], kcT[0:96, h, 0:n]
                        mm(b[:, 0:n], lhs, rhs, inc=filled)
                    if 1 <= i <= len(UNITS2):
                        kind, h, q = UNITS2[i - 1]
                        pe.wait_ge(p2_ready, nth(p2_ready))
                        b, filled = take("a")
                        for c in range(q + 1):
                            tr(b[:, c * P:(c + 1) * P], P2[:, (i - 1) % 2, c * P:(c + 1) * P],
                               filled if c == q else None)
                    if i >= 2:
                        kind, h, q = UNITS2[i - 2]
                        pe.wait_ge(a_emptied, a0 + i - 1)
                        b, filled = take("v")

                        def value(c):
                            if kind == "fox":
                                return u2[:, c, VF + 64 * h:VF + 64 * h + 64]
                            if kind == "moba":
                                return u2[:, c, VM + 64 * h:VM + 64 * h + 64]
                            return vv[:, c, 64 * h:64 * h + 64]
                        contract(b[:, 0:64], lambda c: PT2[:, i % 2, c * P:(c + 1) * P], value, filled, q + 1)
                pe.wait_ge(mixt_ready, nth(mixt_ready))
                turn([0, 1], S, lambda ft, t: mix2[:, t, ft * P:(ft + 1) * P])
                emptied("v")
                emptied("a")
                k["open"] = 1
                for half in range(2):
                    w = weights(("out2", l, half))
                    for t in range(TS):
                        b, filled = take("v")
                        contract(b[:, :], lambda i: actT[:, i, t * P:(t + 1) * P], lambda i: w[:, i, :], filled)
                modulation("mod2", l, 1)
                normed([0, 1])
                for c in range(F2 // 256):
                    w = weights(("up2", l, c))
                    for m in range(2):
                        b, filled = take("s")
                        for g in range(2):
                            contract(b[:, S * g:S * (g + 1)], lambda i: w[:, i, S * g + m * P:S * g + (m + 1) * P],
                                     lambda i: actT[:, i, 0:S], filled if g == 1 else None)
                for half in range(2):
                    banks = [take("v") for t in range(TS)]
                    for c, (k0, k1) in enumerate(HC2):
                        w = weights(("down2", l, 3 * half + c))
                        if c == 0 and half == 0:
                            emptied("s")
                        for t, (b, filled) in enumerate(banks):
                            for i in range(k1 - k0):
                                end = k0 + i == 21
                                mm(b[:, :], hid2[:, k0 + i, t * P:(t + 1) * P], w[:, i, :], k0 + i == 0, end,
                                   filled if end else None)

            pe.wait_ge(cons_in, 16 * NCONS)
            pe.wait_ge(cT_ready, 1)
            for h in range(4):
                b, filled = take("v")
                mm(b[:, :], t5col[:, h, :], t5hot, inc=filled)
            for l in range(L):
                layer1(l)
            for l in range(L):
                layer2(l)

        @block.vector
        def _(dve):
            nth = counter()
            v = nc.vector

            def step(ins, signal=v_step):
                ins.then_inc(signal, 1)
                dve.wait_ge(signal, nth(signal))

            def filled(r="v"):
                banks, s = (VB, v_filled) if r == "v" else (SB, s_filled)
                n = nth(s)
                dve.wait_ge(s, n)
                return banks[(n - 1) % len(banks)]

            def emptied(ins, r="v"):
                ins.then_inc(v_emptied if r == "v" else s_emptied, 1)

            def tt(o, x, y, op):
                return v.tensor_tensor(o, x, y, op)

            def minus_abs(x):
                return v.scalar_tensor_tensor(out=x, in0=x, scalar=-1.0, in1=x, op0=ALU.mult, op1=ALU.min)

            def rstd(parts):
                for i, (at, n, div) in enumerate(parts):
                    ins = v.tensor_scalar(ms[:, at:at + n], ss[:, at:at + n], 1.0 / div, EPS, ALU.mult, ALU.add)
                    if i < len(parts) - 1:
                        step(ins)
                ins.then_inc(ms_ready, 1)
                dve.wait_ge(rstd_ready, nth(rstd_ready))

            def modulation(kind, l, part):
                m = 2 if kind == "mod1" else 1
                gain = gcol[:, (0 if kind == "mod1" else 2) + part, l, :]
                for j in range(7):
                    if j < 6:
                        n = nth(row_ready, 0)
                        r = row[0:m, n % 3, :]
                        dve.wait_ge(row_in[n % 3], 16 * (n // 3 + 1))
                        b = filled()
                        gate = kind == "mod2" and j >= 4
                        step(tt(r, b[0:m, :], r, ALU.add), v_emptied)
                        if gate:
                            if j == 4:
                                dve.wait_ge(post_in, nth(post_in, 16))
                            tt(r, r, post[:, (j - 4) * MODC:(j - 3) * MODC], ALU.mult).then_inc(row_ready, 1)
                        else:
                            v.tensor_copy(nm[0:1, 0:1], r[0:1, 0:1]).then_inc(row_ready, 1)
                        dve.wait_ge(row_ready, nth(row_ready))
                    if j >= 1:
                        i = j - 1
                        if i < 4:
                            b = filled()
                            src = b[:, 0:4 * m].rearrange("p (q m) -> p q m", m=m)
                            dst = modT[:, i // 2, 4 * (i % 2):4 * (i % 2) + 4, 0:m]
                            if i < 2:
                                step(v.tensor_copy(dst, src), v_emptied)
                            else:
                                g4 = bc(gain[:, 4 * (i % 2):4 * (i % 2) + 4], 2, m)
                                step(v.scalar_tensor_tensor(out=dst, in0=src, scalar=1.0, in1=g4, op0=ALU.add,
                                                            op1=ALU.mult), v_emptied)
                        else:
                            for s in range(m):
                                b = filled()
                                step(v.tensor_copy(GA[:, s, (i - 4) * MODC:(i - 3) * MODC], b[:, :]), v_emptied)

            def normed(tiles):
                dve.wait_ge(sq_ready, nth(sq_ready))
                rstd([(0, len(tiles), D)])
                for t in tiles:
                    ins = v.tensor_scalar(xn[:, t, :], X[:, t, :], rs[:, t:t + 1], None, ALU.mult)
                    if t < tiles[-1]:
                        step(ins)
                step(ins, xn_ready)
                for ft in range(0, KT, 2):
                    b = filled()
                    for s in range(len(tiles) // 2):
                        ins = v.tensor_scalar(actT[:, ft, S * s:S * s + S], b[:, S * s:S * s + S],
                                              modT[:, 1, ft, s:s + 1], modT[:, 0, ft, s:s + 1], ALU.mult, ALU.add)
                        if s < len(tiles) // 2 - 1:
                            step(ins)
                    step(ins, v_emptied)

            def gla(l):
                slot_wait(dve, ("par1", l, 0))
                step(v.memset(rT[32:33, :], 1.0))
                b = filled()
                step(v.tensor_copy(rT[0:32, :], b[0:32, :]), v_emptied)
                for t in range(4):
                    b = filled()
                    step(v.tensor_scalar(la[:, t, :], b[:, :], 0.0, None, ALU.min))
                    step(v.scalar_tensor_tensor(out=zt[:, t, :], in0=la[:, t, :], scalar=2.0, in1=b[:, :],
                                                op0=ALU.mult, op1=ALU.subtract), v_emptied)
                for t in range(4):
                    dve.wait_ge(zlog_ready, nth(zlog_ready))
                    step(tt(la[:, t, :], la[:, t, :], zt[:, t, :], ALU.subtract), la_ready if t == 3 else v_step)
                for t in range(4):
                    dve.wait_ge(a_emptied, mark["dec", l] + 1 + t)
                    for d in range(2):
                        o = ke4[:, t, 256 * d:256 * (d + 1)]
                        step(tt(o, o, u[:, t, GK:GV], ALU.mult), ke_ready if t == 3 and d == 1 else v_step)
                for n, pair in enumerate(STATES):
                    for d, (t, to) in enumerate(pair):
                        b = filled()
                        for hp in range(2):
                            j = 2 * d + hp
                            o = St[:, to, 64 * j:64 * j + 64]
                            part = b[:, 64 * hp:64 * hp + 64]
                            if n == 0:
                                ins = v.tensor_copy(o, part)
                            else:
                                ins = v.scalar_tensor_tensor(out=o, in0=St[:, t, 64 * j:64 * j + 64],
                                                             scalar=dec[:, 4 * t + j:4 * t + j + 1], in1=part,
                                                             op0=ALU.mult, op1=ALU.add)
                            step(ins, v_emptied if hp == 1 else v_step)
                for t in tiles1(l):
                    dve.wait_ge(a_emptied, mark["bT", l, t])
                    for d in range(2):
                        j = slice(2 * d, 2 * d + 2)
                        src = bT[:, j, :]
                        step(tt(qk64[:, j, :], src, bT[:, j, 63 + d:64 + d].broadcast_to([P, 2, P]), ALU.subtract))
                        for dst, n in ((qk32, 64), (qd, 32)):
                            s4 = src.rearrange("p h (b i) -> p h b i", i=n)
                            ref = s4[:, :, :, n // 2 - 1 + d:n // 2 + d].broadcast_to([P, 2, P // n, n])
                            step(tt(dst[:, j, :].rearrange("p h (b i) -> p h b i", i=n), s4, ref, ALU.subtract))
                    step(minus_abs(qk96))
                    step(v.tensor_scalar(qd[:, :, :], qd[:, :, :], 80.0, -80.0, ALU.min, ALU.max), exps_in)
                    dve.wait_ge(exps_out, nth(exps_out))
                    q, kk = qgT[:, :, t * P:(t + 1) * P], kgT[:, :, t * P:(t + 1) * P]
                    for d in range(2):
                        j = slice(2 * d, 2 * d + 2)
                        for dst, src in ((qd, q), (kd, kk), (qi, q)):
                            step(tt(dst[:, j, :], dst[:, j, :], src, ALU.mult))
                        for half in range(2):
                            src = q if half != d else kk
                            o = qk64[:, j, 64 * half:64 * half + 64]
                            step(tt(o, o, src[:, :, 64 * half:64 * half + 64], ALU.mult))
                            o = qk32[:, j, :].rearrange("p h (b g i) -> p h b g i", b=2, g=2)[:, :, :, half, :]
                            sv = src.rearrange("p h (b g i) -> p h b g i", b=2, g=2)[:, :, :, half, :]
                            step(tt(o, o, sv, ALU.mult), qk_ready if d == 1 and half == 1 else v_step)
                    for pr in range(2):
                        b = filled("s")
                        main = b[:, 0:256].rearrange("p (h i) -> p h i", h=2)
                        step(tt(AT[:, 2 * pr:2 * pr + 2, :], main, bc(const("mask_f"), 1, 2), ALU.mult))
                        diag = b[:, 256:320].rearrange("p (h i) -> p h i", h=2)
                        step(tt(atb[:, 2 * pr:2 * pr + 2, :], diag, bc(const("mask_b"), 1, 2), ALU.mult), s_emptied)
                    for B in range(0, P, 32):
                        o = AT[B:B + 32, :, B:B + 32]
                        step(tt(o, o, atb[B:B + 32, :, :], ALU.add), AT_ready if B == 96 else v_step)
                    for pr in range(2):
                        b = filled()
                        o = mixt[:, t, 0:256].rearrange("p (h e c) -> p h e c", h=2, e=2)[:, :, pr, :]
                        step(v.tensor_copy(o, b[:, 0:128].rearrange("p (h c) -> p h c", h=2)), v_emptied)
                n = len(tiles1(l))
                o = mixt[:, 0:n, 0:256]
                o4 = o.rearrange("p t (h c) -> p t h c", h=4)
                step(tt(gsq[:, 0:n, :], o, o, ALU.mult))
                step(v.tensor_reduce(ss[:, 0:4 * n].rearrange("p (t h) -> p t h", h=4),
                                     gsq[:, 0:n, :].rearrange("p t (h c) -> p t h c", h=4), X_AXIS, ALU.add))
                rstd([(0, 4 * n, 64)])
                for t in range(n):
                    step(tt(o4[:, t], o4[:, t], bc(rs[:, 4 * t:4 * t + 4], 2, 64), ALU.mult))
                    step(tt(o4[:, t], o4[:, t], bc(par1(l, "g_gla"), 1, 4), ALU.mult))
                g = gexp[:, 0:n, :]
                dve.wait_ge(gexp_ready, nth(gexp_ready))
                step(v.tensor_scalar(g, g, 1.0, None, ALU.add))
                step(v.reciprocal(g, g))
                step(tt(g, g, u[:, 0:n, GG:RF], ALU.mult))
                step(tt(o, o, g, ALU.mult))

            def rope(x1, x2, cos, sin, t1, t2):
                step(tt(t1, x1, sin, ALU.mult))
                step(tt(t2, x2, sin, ALU.mult))
                step(tt(x1, x1, cos, ALU.mult))
                step(tt(x2, x2, cos, ALU.mult))
                step(tt(x1, x1, t2, ALU.subtract))
                step(tt(x2, x2, t1, ALU.add))

            def attention1(l):
                def span(t):
                    return 0 if t in tiles1(l) else 8

                for t in range(4):
                    h0 = span(t)
                    x = u[:, t, AQ + 64 * h0:AV]
                    sq = tmp[:, 0:64 * (10 - h0)]
                    step(tt(sq, x, x, ALU.mult))
                    step(v.tensor_reduce(ss[:, 10 * t + h0:10 * t + 10], sq.rearrange("p (h c) -> p h c", c=64),
                                         X_AXIS, ALU.add))
                rstd([(0, 40, 64)])
                for t in range(4):
                    h0 = span(t)
                    x = u[:, t, AQ + 64 * h0:AV].rearrange("p (h c) -> p h c", c=64)
                    step(tt(x, x, bc(rs[:, 10 * t + h0:10 * t + 10], 2, 64), ALU.mult))
                    if h0 == 0:
                        step(tt(x[:, 0:8, :], x[:, 0:8, :], bc(par1(l, "g_q"), 1, 8), ALU.mult))
                    xk = x[:, 8 - h0:10 - h0, :]
                    step(tt(xk, xk, bc(par1(l, "g_k"), 1, 2), ALU.mult))
                table = const("rope1").rearrange("p (t c a f) -> p t c a f", t=2, c=2, a=2)
                for t in range(TS):
                    x = u[:, t, AQ:AV].rearrange("p (h a b f) -> p h a b f", a=2, b=2, f=16)
                    for axis in range(2):
                        t1 = tmp[:, 0:160].rearrange("p (h f) -> p h f", f=16)
                        t2 = tmp[:, 160:320].rearrange("p (h f) -> p h f", f=16)
                        rope(x[:, :, axis, 0, :], x[:, :, axis, 1, :], bc(table[:, t, 0, axis, :], 1, 10),
                             bc(table[:, t, 1, axis, :], 1, 10), t1, t2)
                for t in range(4):
                    o = kdup[:, t, :].rearrange("p (g e c) -> p g e c", g=2, e=2)
                    k2 = u[:, t, AK:AV].rearrange("p (g c) -> p g c", g=2)
                    step(v.tensor_copy(o, bc(k2, 2, 2)), aq_ready if t == 3 else v_step)
                n = P * len(tiles1(l))
                for g in range(2):
                    b = filled()
                    step(v.tensor_scalar(actT[:, g, 0:n], b[:, 0:n], spool[:, l, g:g + 1], None, ALU.mult), v_emptied)
                for j in (0, 2):
                    b = filled()
                    step(v.tensor_copy(qT[:, j, 0:n], b[:, 0:n]), v_emptied)
                for g in range(2):
                    b = filled()
                    step(v.tensor_copy(kT[:, g, :], b[:, :]), v_emptied)
                units = units1(l)
                for i in range(len(units) + 2):
                    if i < len(units):
                        t, h, k0 = units[i]
                        b = filled("s")
                        step(v.tensor_reduce(mx[:, i % 2:i % 2 + 1], b[:, 0:512 - k0], X_AXIS, ALU.max))
                        step(v.tensor_scalar(nm[:, i % 2:i % 2 + 1], mx[:, i % 2:i % 2 + 1], -0.125, None, ALU.mult),
                             nm_ready)
                    if i >= 2:
                        t, h, k0 = units[i - 2]
                        b = filled()
                        r = rinv[:, i % 2:i % 2 + 1]
                        step(v.reciprocal(r, rsum[:, (i - 2) % 4:(i - 2) % 4 + 1]))
                        step(v.tensor_scalar(mixt[:, t, 256 + 64 * h:320 + 64 * h], b[:, 0:64], r, None, ALU.mult),
                             v_emptied)
                nth(s_emptied, len(units))

            def residual1(tiles):
                for half in range(2):
                    c = slice(half * MODC, (half + 1) * MODC)
                    for t in tiles:
                        b = filled()
                        step(tt(tmpx[:, t % 2, :], b[:, :], GA[:, t // 2, c], ALU.mult), v_emptied)
                        last = half == 1 and t == tiles[-1]
                        step(tt(X[:, t, c], X[:, t, c], tmpx[:, t % 2, :], ALU.add), x_ready if last else v_step)

            def layer1(l):
                modulation("mod1", l, 0)
                if l == 0:
                    dve.wait_ge(t5_in, 16)
                    step(tt(t5[:, :, :], t5[:, :, :], bc(const("causal"), 1, 4), ALU.add))
                normed([0, 1, 2, 3])
                for c, t, lo, hi, r in in1_jobs(l):
                    if r == "v":
                        b = filled()
                        c0 = CH1[c][0]
                        step(v.tensor_copy(u[:, t, c0 + lo:c0 + hi], b[:, 0:hi - lo]), v_emptied)
                dve.wait_ge(a_emptied, mark["in1", l])
                gla(l)
                attention1(l)
                n = P * len(tiles1(l))
                for j in (0, 2, 4):
                    b = filled()
                    step(v.tensor_copy(actT[:, 2 + j, 0:n], b[:, 0:n]), v_emptied)
                residual1(tiles1(l))
                modulation("mod1", l, 1)
                normed(tiles1(l))
                residual1(tiles1(l))

            def squares(o, src, at):
                step(v.tensor_tensor_reduce(out=o, in0=src, in1=src, scale=1.0, scalar=0.0, op0=ALU.mult,
                                            op1=ALU.add, accum_out=ss[:, at:at + 1]))

            def residual2():
                for half in range(2):
                    for t in range(TS):
                        b = filled()
                        step(v.tensor_copy(y2[:, t, half * MODC:(half + 1) * MODC], b[:, :]), v_emptied)
                for t in range(TS):
                    squares(tmp2[:, 0:D], y2[:, t, :], t)
                rstd([(0, 2, D)])
                for t in range(TS):
                    step(v.scalar_tensor_tensor(out=y2[:, t, :], in0=y2[:, t, :], scalar=rs[:, t:t + 1],
                                                in1=GA[:, 0, :], op0=ALU.mult, op1=ALU.mult))
                    step(tt(X[:, t, :], X[:, t, :], y2[:, t, :], ALU.add), x_ready if t == 1 else v_step)

            def layer2(l):
                modulation("mod2", l, 0)
                normed([0, 1])
                for c, (c0, c1) in enumerate(CH2):
                    b = filled()
                    step(v.tensor_copy(u2[:, 0, c0:c1], b[:, 0:c1 - c0]), v_emptied)
                dve.wait_ge(a_emptied, mark["in2", l])
                slot_wait(dve, ("par2", l, 0))
                for t in range(TS):
                    step(tt(lft[:, t, :], u2[:, t, FL:QM], par2(l, "b_forget"), ALU.add))
                step(v.tensor_scalar(lf[:, :, :], lft[:, :, :], 0.0, None, ALU.min))
                step(minus_abs(lft[:, :, :]), fneg_ready)
                for t in range(TS):
                    squares(tmp2[:, 0:256], u2[:, t, CQ:CKV], t)
                    squares(tmp2[:, 0:128], u2[:, t, CKV:KR], 2 + t)
                dve.wait_ge(flog_ready, nth(flog_ready))
                step(tt(lf[:, :, :], lf[:, :, :], lft[:, :, :], ALU.subtract), lf_ready)
                rstd([(0, 2, 256), (2, 2, 128)])
                for t in range(TS):
                    for i, (c0, c1, g) in enumerate(((CQ, CKV, "g_q_lat"), (CKV, KR, "g_kv_lat"))):
                        x = u2[:, t, c0:c1]
                        step(v.scalar_tensor_tensor(out=x, in0=x, scalar=rs[:, 2 * i + t:2 * i + t + 1],
                                                    in1=par2(l, g), op0=ALU.mult, op1=ALU.mult),
                             lat_ready if t == 1 and i == 1 else v_step)
                b = filled()
                step(v.tensor_copy(Fc[:, :, :], b[:, 0:8].rearrange("p (t h) -> p t h", h=4)), v_emptied)
                b = filled()
                step(v.tensor_copy(cqT[:, :, :], b[:, :].rearrange("p (k n) -> p k n", k=2)), v_emptied)
                b = filled()
                step(v.tensor_copy(ckvT, b[:, 0:S]), v_emptied)
                for t in range(TS):
                    h4 = slice(4 * t, 4 * t + 4)
                    step(v.tensor_scalar(qa[:, h4, 0:64], u2[:, t, QF:KF].rearrange("p (h c) -> p h c", h=4), 0.125,
                                         None, ALU.mult))
                    step(v.tensor_copy(ka[:, h4, 0:64], u2[:, t, KF:VF].rearrange("p (h c) -> p h c", h=4)))
                    step(v.tensor_copy(qa[:, h4, 65:66], bc(Fc[:, t, :], 2, 1)))
                    step(v.tensor_scalar(ka[:, h4, 64:65], bc(Fc[:, t, :], 2, 1), -1.0, None, ALU.mult))
                step(v.memset(qa[:, :, 64:65], 1.0))
                step(v.memset(ka[:, :, 65:66], 1.0), qa_ready)
                for t in range(TS):
                    for n in range(2):
                        b = filled()
                        step(v.tensor_copy(ql[:, t, 384 * n:384 * n + 384], b[:, 0:384]), v_emptied)
                table = const("rope2").rearrange("p (t c f) -> p t c f", t=2, c=2)
                for t in range(TS):
                    q8 = ql[:, t, :].rearrange("p (h c) -> p h c", h=8)
                    t1 = tmp2[:, 0:128].rearrange("p (h f) -> p h f", f=16)
                    t2 = tmp2[:, 128:256].rearrange("p (h f) -> p h f", f=16)
                    rope(q8[:, :, 64:80], q8[:, :, 80:96], bc(table[:, t, 0, :], 1, 8), bc(table[:, t, 1, :], 1, 8),
                         t1, t2)
                    kr = u2[:, t, KR:IN2]
                    rope(kr[:, 0:16], kr[:, 16:32], table[:, t, 0, :], table[:, t, 1, :], tmp2[:, 0:16],
                         tmp2[:, 16:32])
                    k8 = kc[:, t, :].rearrange("p (h c) -> p h c", h=8)
                    step(v.tensor_copy(k8[:, :, 64:96], bc(kr, 1, 8)), heads_ready if t == 1 else v_step)
                for hp in range(2):
                    b = filled()
                    step(v.tensor_copy(qfT[0:66, 2 * hp:2 * hp + 2, :], b[0:66, :].rearrange("p (h n) -> p h n", h=2)),
                         v_emptied)
                for hp in range(4):
                    b = filled()
                    step(v.tensor_copy(qcT[0:96, 2 * hp:2 * hp + 2, :], b[0:96, :].rearrange("p (h n) -> p h n", h=2)),
                         v_emptied)
                for i in range(len(UNITS2) + 2):
                    if i < len(UNITS2):
                        kind, h, q = UNITS2[i]
                        n = P * (q + 1)
                        mask = (t5[:, h, :] if kind == "moba" else const("causal"))[:, S - n:S]
                        b = filled("s")
                        step(v.tensor_tensor_reduce(out=S2[:, i % 2, 0:n], in0=b[:, 0:n], in1=mask, scale=1.0,
                                                    scalar=-3.0e38, op0=ALU.add, op1=ALU.max,
                                                    accum_out=mx[:, i % 2:i % 2 + 1]), s_emptied)
                        step(v.tensor_scalar(nm[:, i % 2:i % 2 + 1], mx[:, i % 2:i % 2 + 1], -SCALE2[kind], None,
                                             ALU.mult), nm_ready)
                    if i >= 2:
                        kind, h, q = UNITS2[i - 2]
                        c0 = {"fox": 0, "moba": 256, "mla": 512}[kind] + 64 * h
                        b = filled()
                        r = rinv[:, i % 2:i % 2 + 1]
                        step(v.reciprocal(r, rsum[:, (i - 2) % 4:(i - 2) % 4 + 1]))
                        step(v.tensor_scalar(mix2[:, q, c0:c0 + 64], b[:, 0:64], r, None, ALU.mult), v_emptied)
                groups = ((0, 256), (256, 512), (512, 1024))
                for g, (c0, c1) in enumerate(groups):
                    for t in range(TS):
                        squares(tmp2[:, 0:c1 - c0], mix2[:, t, c0:c1], 2 * g + t)
                rstd([(0, 4, 256), (4, 2, 512)])
                for g, (c0, c1) in enumerate(groups):
                    for t in range(TS):
                        x = mix2[:, t, c0:c1]
                        step(v.scalar_tensor_tensor(out=x, in0=x, scalar=rs[:, 2 * g + t:2 * g + t + 1],
                                                    in1=par2(l, "g_group")[:, c0:c1], op0=ALU.mult, op1=ALU.mult),
                             mixt_ready if g == 2 and t == 1 else v_step)
                for ft in range(0, KT, 2):
                    b = filled()
                    step(v.tensor_copy(actT[:, ft, 0:S], b[:, 0:S]), v_emptied)
                residual2()
                modulation("mod2", l, 1)
                normed([0, 1])
                for m in range(F2 // P):
                    dve.wait_ge(sg_ready, nth(sg_ready))
                    b = filled("s")
                    g = sg2[:, m % 2, :]
                    step(v.tensor_scalar(g, g, 1.0, None, ALU.add))
                    step(v.reciprocal(g, g))
                    step(tt(g, g, b[:, 0:S], ALU.mult))
                    step(tt(hid2[:, m, :], g, b[:, S:512], ALU.mult), s_emptied)
                residual2()

            dve.wait_ge(pool_ready, 2)
            step(v.memset(ss[:, :], 0.0))
            dve.wait_ge(cons_in, 16 * NCONS)
            step(v.tensor_copy(t5col, bc(t5tab, 2, P)))
            dve.wait_ge(cexp_ready, 1)
            step(v.tensor_scalar(csig[:, :], csig[:, :], 1.0, None, ALU.add))
            step(v.reciprocal(csig[:, :], csig[:, :]))
            step(tt(cT[:, :, :].rearrange("p a k -> p (a k)"), cols[:, 0:24], csig[:, :], ALU.mult), cT_ready)
            for h in range(4):
                b = filled()
                step(v.tensor_scalar(t5rows[:, h, :], b[:, :], 8.0, None, ALU.mult), v_emptied)
            for l in range(L):
                layer1(l)
            dve.wait_ge(sq_ready, nth(sq_ready))
            rstd([(0, 2, D)])
            dve.wait_ge(gf_in, 16)
            for t in range(TS):
                step(v.scalar_tensor_tensor(out=X[:, t, :], in0=X[:, t, :], scalar=rs[:, t:t + 1], in1=gf,
                                            op0=ALU.mult, op1=ALU.mult), x_ready if t == 1 else v_step)
            for l in range(L):
                layer2(l)

        @block.scalar
        def _(act):
            nth = counter()
            norms = [0]

            def step(ins, signal=a_step):
                ins.then_inc(signal, 1)
                act.wait_ge(signal, nth(signal))

            def filled(r="a"):
                banks, s = (AB, a_filled) if r == "a" else (SB, s_filled)
                n = nth(s)
                act.wait_ge(s, n)
                return banks[(n - 1) % len(banks)]

            def f(o, x, func, **kw):
                return nc.scalar.activation(o, x, func, **kw)

            def squares(tiles):
                if norms[0]:
                    act.wait_ge(x_ready, norms[0])
                norms[0] += 1
                for t in tiles:
                    step(f(xn[:, t, :], X[:, t, :], ACT.Square, accum_out=ss[:, t:t + 1]),
                         sq_ready if t == tiles[-1] else a_step)

            def normed(tiles):
                squares(tiles)
                for ft in range(1, KT, 2):
                    b = filled()
                    for s in range(len(tiles) // 2):
                        last = s == len(tiles) // 2 - 1
                        step(f(actT[:, ft, S * s:S * s + S], b[:, S * s:S * s + S], ACT.Identity,
                               scale=modT[:, 1, ft, s:s + 1], bias=modT[:, 0, ft, s:s + 1]),
                             a_emptied if last else a_step)

            def softplus(x, out_):
                step(f(x, x, ACT.Exp))
                step(f(x, x, ACT.Ln, bias=1.0), out_)

            def layer1(l):
                n = P * len(tiles1(l))
                normed([0, 1, 2, 3])
                for c, t, lo, hi, r in in1_jobs(l):
                    if r == "a":
                        b = filled()
                        c0 = CH1[c][0]
                        step(f(u[:, t, c0 + lo:c0 + hi], b[:, 0:hi - lo], ACT.Copy), a_emptied)
                for t in range(4):
                    act.wait_ge(v_emptied, mark["z", l, t])
                    softplus(zt[:, t, :], zlog_ready)
                for dst, scale in ((qgT, 0.125), (kgT, 1.0)):
                    for hp in range(2):
                        b = filled()
                        step(f(dst[:, hp, 0:n], b[:, 0:n], ACT.Copy, scale=scale), a_emptied)
                b = filled()
                step(f(dec, b[:, 0:16], ACT.Exp), a_emptied)
                for t in range(4):
                    b = filled()
                    step(f(ke4[:, t, :], b[:, :], ACT.Exp), a_emptied)
                for t in tiles1(l):
                    b = filled()
                    step(f(bT[:, :, :], b[:, :].rearrange("p (j n) -> p j n", j=4), ACT.Copy), a_emptied)
                    act.wait_ge(exps_in, nth(exps_in))
                    step(f(qk96, qk96, ACT.Exp))
                    step(f(kd[:, :, :], qd[:, :, :], ACT.Exp, scale=-1.0))
                    step(f(qd[:, :, :], qd[:, :, :], ACT.Exp))
                    step(f(qi[:, :, :], bT[:, :, :], ACT.Exp), exps_out)
                    act.wait_ge(qk_ready, nth(qk_ready))
                step(f(gexp[:, 0:len(tiles1(l)), :], u[:, 0:len(tiles1(l)), GG:RF], ACT.Exp, scale=-1.0), gexp_ready)
                for g in range(2):
                    b = filled()
                    step(f(mT[:, g, 0:n], b[:, 0:n], ACT.Copy), a_emptied)
                for sem_ in (s_filled, s_emptied):
                    nth(sem_, 2 * len(tiles1(l)))
                for j in (1, 3):
                    b = filled()
                    step(f(qT[:, j, 0:n], b[:, 0:n], ACT.Copy), a_emptied)
                units = units1(l)
                for i in range(len(units) + 1):
                    if i < len(units):
                        k0 = units[i][2]
                        act.wait_ge(nm_ready, nth(nm_ready))
                        b = filled("s")
                        step(f(Pr[:, i % 2, 0:512 - k0], b[:, 0:512 - k0], ACT.Exp, bias=nm[:, i % 2:i % 2 + 1],
                               scale=0.125, accum_out=rsum[:, i % 4:i % 4 + 1]), s_emptied)
                    if i >= 1:
                        k0 = units[i - 1][2]
                        b = filled()
                        step(f(PT[:, (i - 1) % 2, 0:512 - k0], b[:, 0:512 - k0], ACT.Copy), a_emptied)
                for j in (1, 3, 5):
                    b = filled()
                    step(f(actT[:, 2 + j, 0:n], b[:, 0:n], ACT.Copy), a_emptied)
                normed(tiles1(l))
                for m in range(F1 // P):
                    b = filled()
                    step(f(hid[:, m, 0:n], b[:, 0:n], ACT.Relu), a_emptied)
                    step(f(hid[:, m, 0:n], hid[:, m, 0:n], ACT.Square), hid_ready)

            def layer2(l):
                normed([0, 1])
                for c, (c0, c1) in enumerate(CH2):
                    b = filled()
                    step(f(u2[:, 1, c0:c1], b[:, 0:c1 - c0], ACT.Copy), a_emptied)
                for dst in (qmT, kmT):
                    b = filled()
                    step(f(dst[:, :, :], b[:, :].rearrange("p (h n) -> p h n", h=2), ACT.Copy), a_emptied)
                act.wait_ge(fneg_ready, nth(fneg_ready))
                softplus(lft[:, :, :], flog_ready)
                for t in range(TS):
                    for n in range(2):
                        b = filled()
                        kv = b[:, :].rearrange("p (h e c) -> p h e c", h=4, e=2)
                        k8 = kc[:, t, :].rearrange("p (h c) -> p h c", h=8)
                        step(f(k8[:, 4 * n:4 * n + 4, 0:64], kv[:, :, 0, :], ACT.Copy))
                        step(f(vv[:, t, 256 * n:256 * n + 256].rearrange("p (h c) -> p h c", h=4), kv[:, :, 1, :],
                               ACT.Copy), a_emptied)
                for hp in range(2):
                    b = filled()
                    step(f(kfT[0:66, 2 * hp:2 * hp + 2, :], b[0:66, :].rearrange("p (h n) -> p h n", h=2), ACT.Copy),
                         a_emptied)
                for hp in range(4):
                    b = filled()
                    step(f(kcT[0:96, 2 * hp:2 * hp + 2, :], b[0:96, :].rearrange("p (h n) -> p h n", h=2), ACT.Copy),
                         a_emptied)
                for i in range(len(UNITS2) + 1):
                    if i < len(UNITS2):
                        kind, h, q = UNITS2[i]
                        n = P * (q + 1)
                        act.wait_ge(nm_ready, nth(nm_ready))
                        step(f(P2[:, i % 2, 0:n], S2[:, i % 2, 0:n], ACT.Exp, bias=nm[:, i % 2:i % 2 + 1],
                               scale=SCALE2[kind], accum_out=rsum[:, i % 4:i % 4 + 1]), p2_ready)
                    if i >= 1:
                        n = P * (UNITS2[i - 1][2] + 1)
                        b = filled()
                        step(f(PT2[:, (i - 1) % 2, 0:n], b[:, 0:n], ACT.Copy), a_emptied)
                for ft in range(1, KT, 2):
                    b = filled()
                    step(f(actT[:, ft, 0:S], b[:, 0:S], ACT.Copy), a_emptied)
                nth(s_filled, len(UNITS2))
                normed([0, 1])
                for m in range(F2 // P):
                    b = filled("s")
                    step(f(sg2[:, m % 2, :], b[:, 0:S], ACT.Exp, scale=-1.0), sg_ready)

            act.dma_start(cons[:, :], a["cons"]).then_inc(cons_in, 16)
            act.dma_start(cols[:, :], a["cols"]).then_inc(cons_in, 16)
            act.dma_start(t5tab, a["t5_table_2"]).then_inc(cons_in, 16)
            act.dma_start(t5hot, a["t5hot"]).then_inc(cons_in, 16)
            act.dma_start(X[:, 0:2, :], a["x"][0].rearrange("(t p) d -> p t d", p=P)).then_inc(x_in, 16)
            act.dma_start(X[:, 2:4, :], a["ctx"][0].rearrange("(t p) d -> p t d", p=P)).then_inc(x_in, 16)
            act.wait_ge(cons_in, 16 * NCONS)
            step(f(csig[:, :], cols[:, 0:24], ACT.Exp, scale=-1.0), cexp_ready)
            act.wait_ge(x_in, 32)
            act.wait_ge(cT_ready, 1)
            for l in range(L):
                layer1(l)
            act.wait_ge(x_ready, 2 * L)
            act.dma_start(gf, a["g_final"].partition_broadcast(P)).then_inc(gf_in, 16)
            squares([0, 1])
            for l in range(L):
                layer2(l)


def bucket(dist):
    n = np.maximum(dist, 0)
    nf = np.maximum(n, 16).astype(np.float32)
    large = 16 + (np.log(nf / np.float32(16)) / np.float32(math.log(8)) * np.float32(16)).astype(np.int32)
    return np.where(n < 16, n, np.minimum(large, 31))


def constants():
    i = np.arange(P)
    t, j = i[:, None], i[None, :]
    out = {}
    out["ident"] = t == j
    out["up16"] = (t <= j) / 16.0
    out["lo16"] = (t >= j) / 16.0
    out["after16"] = (t > j) / 16.0
    out["before16"] = (t < j) / 16.0
    out["up"] = t <= j
    out["ones"] = np.ones((P, P))
    out["mask_f"] = (t // 32 != j // 32) | (t <= j)
    out["mask_b"] = (t % 32) > np.arange(32)[None, :]
    out["causal"] = np.concatenate([np.zeros((P, P)), np.where(j <= t, 0.0, NEG)], 1)
    inv1 = np.float32(10000.0) ** (-np.arange(0, 32, 2, dtype=np.float32) / np.float32(32))
    tok = np.arange(S)
    axes = np.stack([tok // 64, tok % 64], 1).astype(np.float32)
    ang = axes[:, :, None] * inv1
    r1 = np.stack([np.cos(ang), np.sin(ang)], 1)
    out["rope1"] = r1.reshape(TS, P, 64).transpose(1, 0, 2).reshape(P, 128)
    inv2 = np.float32(1.0) / (np.float32(10000.0) ** (np.arange(16, dtype=np.float32) / np.float32(16)))
    ang = tok.astype(np.float32)[:, None] * inv2
    r2 = np.stack([np.cos(ang), np.sin(ang)], 1)
    out["rope2"] = r2.reshape(TS, P, 32).transpose(1, 0, 2).reshape(P, 64)
    sel = np.zeros((P, 2, P))
    sel[0, 0] = 1
    sel[1, 1] = 1
    out["sel"] = sel.reshape(P, 256)
    cons = np.concatenate([out[n].astype(np.float32) for n, _ in CONST], 1)
    hot = np.zeros((32, 512), np.float32)
    e = np.arange(256)
    hot[bucket(255 - e), e] = 1
    band = np.zeros((4, S, S), np.float32)
    for g, w in enumerate((2, 4, 8, 16)):
        lo, hi = np.clip(tok - w // 2, 0, S - 1), np.clip(tok + w // 2 - 1, 0, S - 1)
        inside = (tok[:, None] >= lo[None, :]) & (tok[:, None] <= hi[None, :])
        band[g] = inside / (hi - lo + 1)[None, :].astype(np.float32) - np.eye(S)
    band = band.reshape(4, TS, P, S).transpose(2, 1, 0, 3).reshape(P, 2048)
    return cons, hot, band


def kernel(**inputs):
    import concourse.bacc as _bacc
    from concourse import mybir as _mybir
    from concourse.bass_utils import run_bass_kernel_spmd as _run

    x = {k: np.ascontiguousarray(v) for k, v in inputs.items()}
    cons, hot, band = constants()

    def columns(w):
        return w.reshape(-1, P).T

    cols = np.concatenate([columns(x[n]) for n in ("c", "c_ctx", "c_2", "g_mix", "g_mlp", "g_mix_pre_2",
                                                   "g_ffn_pre_2", "s_pool")], 1)
    par1 = np.zeros((L, P, sum(n for _, n in PAR1)), np.float32)
    par2 = np.zeros((L, P, sum(n for _, n in PAR2)), np.float32)
    at1, at2 = offsets(PAR1)[0], offsets(PAR2)[0]

    def put(dst, at, name, value):
        s, n = at[name]
        dst[:, s:s + n] = value

    for l in range(L):
        put(par1[l], at1, "band", band)
        wg = np.zeros((P, 512), np.float32)
        wg[0:16, 0:256], wg[16:32, 256:512] = x["w_gate"][l, 0], x["w_gate"][l, 1]
        wg[32, 0:256], wg[32, 256:512] = x["b_gate"][l, 0], x["b_gate"][l, 1]
        put(par1[l], at1, "wg", wg)
        wp = np.zeros((P, 2, P), np.float32)
        for g in range(4):
            o = 64 * (g % 2)
            wp[o:o + 64, g // 2, o:o + 64] = x["w_pool"][l, g]
        put(par1[l], at1, "wpool", wp.reshape(P, 256))
        for n in ("g_q", "g_k", "g_gla"):
            put(par1[l], at1, n, x[n][l][None, :])
        put(par2[l], at2, "w_uq", x["w_uq_2"][l].reshape(2, P, 768).transpose(1, 0, 2).reshape(P, 1536))
        put(par2[l], at2, "w_ukv", x["w_ukv_2"][l])
        for n in ("g_q_lat", "g_kv_lat", "g_group", "b_forget"):
            put(par2[l], at2, n, x[n + "_2"][l][None, :])
    arrays = {"cons": cons, "cols": cols, "t5hot": hot, "par1": par1, "par2": par2}
    for n in ("x", "ctx", "w_mod", "b_mod", "w_in", "w_out", "w_up", "w_down", "g_final", "t5_table_2", "w_ada_2",
              "b_ada_2", "g_mix_post_2", "w_in_2", "w_out_2", "g_ffn_post_2", "w_gate_up_2", "w_down_2"):
        arrays[n] = x[n]
    arrays["g_final"] = x["g_final"].reshape(1, D)

    nc = _bacc.Bacc("TRN2", target_bir_lowering=False, num_devices=1)
    feed, aps = {}, {}
    for n, v in arrays.items():
        v = np.ascontiguousarray(v)
        feed[f"in_{n}"] = v
        aps[n] = nc.dram_tensor(f"in_{n}", v.shape, _mybir.dt.from_np(v.dtype), kind="ExternalInput").ap()
    aps["t5_rows"] = nc.dram_tensor("t5_rows", [P, 4, 512], _mybir.dt.float32, kind="Internal").ap()
    out = nc.dram_tensor("out", (1, S, D), _mybir.dt.float32, kind="ExternalOutput").ap()
    trunks(nc, aps, out)
    r = _run(nc, [feed], core_ids=[0])
    return r.results[0]["out"]
```

```python
import math
import numpy as np
import concourse.bass as bass
from concourse import mybir
from contextlib import ExitStack

D = 1024
P = 128
KT = D // P
L = 2
S = 256
TS = S // P
MODC = 512
F1 = 4096
F2 = 2816
IN1 = 2080
IN2 = 1956
EPS = 1e-6
NEG = -1.0e30
GQ, GK, GV, GG, RF, AQ, AK, AV = 256, 512, 768, 1024, 1280, 1312, 1824, 1952
CH1 = [(0, 512), (512, 1024), (1024, 1312), (1312, 1824), (1824, 2080)]
QF, KF, VF, FL, QM, KM, VM, CQ, CKV, KR = 0, 256, 512, 768, 772, 1028, 1284, 1540, 1796, 1924
CH2 = [(489 * i, 489 * (i + 1)) for i in range(4)]
PAR1 = [("band", 2048), ("wg", 512), ("wpool", 256), ("g_q", 64), ("g_k", 64), ("g_gla", 64)]
PAR2 = [("w_uq", 1536), ("w_ukv", 1024), ("g_q_lat", 256), ("g_kv_lat", 128), ("g_group", 1024), ("b_forget", 4)]
CONST = [("ident", 128), ("up16", 128), ("lo16", 128), ("after16", 128), ("before16", 128), ("up", 128),
         ("ones", 128), ("mask_f", 128), ("mask_b", 32), ("causal", 256), ("rope1", 128), ("rope2", 64),
         ("sel", 256)]
NCONS = 4
NSLOT = 3
SLOT = 4096
HC2 = [(0, 8), (8, 15), (15, 22)]


def offsets(table):
    at, out = 0, {}
    for name, n in table:
        out[name] = (at, n)
        at += n
    return out, at


MODS = [("mod1", l, k) for l in range(L) for k in range(12)] + [("mod2", l, k) for l in range(L) for k in range(12)]
NFIRST = 6


def loads():
    out, mods = MODS[:NFIRST], MODS[NFIRST:]
    for n in (1, 2):
        for l in range(L):
            out += [(f"in{n}", l, c) for c in range(len((CH1, CH2)[n - 1]))]
            out += [(f"par{n}", l, 0)]
            out += mods[:12]
            mods = mods[12:]
            out += [(f"out{n}", l, h) for h in range(2)]
            out += [(f"up{n}", l, c) for c in range((F1 // MODC, F2 // 256)[n - 1])]
            out += [(f"down{n}", l, c) for c in range((8, 2 * len(HC2))[n - 1])]
    return out


LOADS = loads()
PLACE = {key: i for i, key in enumerate(key for key in LOADS if key[0][:3] != "par")}


def landed():
    at, out = [0] * NSLOT, {}
    for key, i in PLACE.items():
        at[i % NSLOT] += 32 if key[0] == "up2" else 16
        out[key] = at[i % NSLOT]
    return out


LANDED = landed()


def in1_jobs(l):
    out = []
    for c, (c0, c1) in enumerate(CH1):
        for t in range(4):
            lo, hi = 0, c1 - c0
            if l == L - 1 and t >= 2:
                if c in (0, 3):
                    continue
                if c == 2:
                    lo = RF - c0
            out.append((c, t, lo, hi, "va"[len(out) % 2]))
    return out


def units1(l):
    return [(2 * s + q, h, 256 * s) for s in range(2 if l < L - 1 else 1) for q in range(TS) for h in range(8)]


UNITS2 = [(kind, h, q) for q in range(TS) for kind, n in (("fox", 4), ("moba", 4), ("mla", 8)) for h in range(n)]
STATES = [((2, 3), (3, 2)), ((3, 0), (2, 1)), ((0, 1), (1, 0))]


SCALE2 = {"fox": 1.0, "moba": 0.125, "mla": 96.0 ** -0.5}


def counter():
    seen = {}

    def nth(sem, k=1):
        seen[sem.name] = seen.get(sem.name, 0) + k
        return seen[sem.name]
    return nth


def trunks(nc, a, out):
    f32 = mybir.dt.float32
    ALU = mybir.AluOpType
    ACT = mybir.ActivationFunctionType
    X_AXIS = mybir.AxisListType.X
    ctx = ExitStack()
    with ctx:
        def sb(name, shape):
            return ctx.enter_context(nc.sbuf_tensor(name, shape, f32))

        def sem(name):
            return ctx.enter_context(nc.semaphore(name))

        X = sb("X", [P, 4, D])
        actT = sb("actT", [P, KT, 512])
        ring = sb("ring", [P, NSLOT, SLOT])
        arena = sb("arena", [P, 20480])
        params = sb("params", [P, 3972])
        GA = sb("GA", [P, 2, D])
        cons_at, cons_n = offsets(CONST)
        cons = sb("cons", [P, cons_n])
        cols = sb("cols", [P, 92])
        csig = sb("csig", [P, 24])
        cT = sb("cT", [P, 3, KT])
        row = sb("row", [2, 3, MODC])
        modrow = sb("modrow", [32, P])
        modT = sb("modT", [P, 2, KT, 2])
        t5 = sb("t5", [P, 4, S])
        post = GA[:, 1, :]
        ms = sb("ms", [P, 64])
        rs = sb("rs", [P, 64])
        neghalf = sb("neghalf", [P, 64])
        ss = sb("ss", [P, 48])
        rsum = sb("rsum", [P, 4])
        mx = sb("mx", [P, 2])
        nm = sb("nm", [P, 2])
        rinv = sb("rinv", [P, 2])

        def const(name):
            at, n = cons_at[name]
            return cons[:, at:at + n]

        ident = const("ident")
        ones = const("ones")
        sel = const("sel").rearrange("p (s q) -> p s q", s=2)
        gcol = cols[:, 24:88].rearrange("p (w l k) -> p w l k", w=4, l=2)
        spool = cols[:, 88:92].rearrange("p (l g) -> p l g", l=2)

        def carve(start, *shape):
            n = int(np.prod(shape))
            v = arena[:, start:start + n]
            assert start + n <= 20480, (start, shape)
            if len(shape) == 2:
                v = v.rearrange("p (a b) -> p a b", a=shape[0])
            elif len(shape) == 3:
                v = v.rearrange("p (a b c) -> p a b c", a=shape[0], b=shape[1])
            return v

        xn = carve(0, 4, D)
        u = carve(0, 4, IN1)
        mixt = carve(8320, 4, 768)
        la = carve(11392, 4, 512)
        qgT = carve(13440, 2, 512)
        kgT = carve(14464, 2, 512)
        zt = carve(15488, 4, 512)
        ke4 = carve(15488, 4, 512)
        bT = carve(15488, 4, P)
        qk64 = carve(16000, 4, P)
        qk32 = carve(16512, 4, P)
        qk96 = carve(16000, 1024)
        qd = carve(17024, 4, P)
        kd = carve(17536, 4, P)
        qi = carve(18048, 4, P)
        AT = carve(18560, 4, P)
        rT = arena[0:33, 18560:19072]
        St = carve(19072, 4, 256)
        atb = carve(20096, 4, 32)
        dec = carve(20224, 16)
        gsq = carve(13440, 4, 256)
        gexp = carve(14464, 4, 256)
        qT = carve(11392, 4, 512)
        kT = carve(13440, 2, 512)
        Pr = carve(14464, 2, 512)
        PT = carve(15488, 2, 512)
        mT = carve(16512, 2, 512)
        kdup = mixt[:, :, 512:768]
        sqq = mixt[:, 0:2, 256:512]
        sqk = mixt[:, 2, 256:384]
        hid = carve(0, 32, 512)
        tmpx = params[:, 0:1024].rearrange("p (a n) -> p a n", a=2)
        u2 = carve(0, 2, IN2)
        y2 = carve(0, 2, D)
        qa = carve(3912, 8, 66)
        ka = carve(4440, 8, 66)
        qfT = carve(4968, 4, S)
        kfT = carve(5992, 4, S)
        qmT = carve(7016, 2, S)
        kmT = carve(7528, 2, S)
        cqT = carve(8040, 2, S)
        ckvT = carve(8552, S)
        ql = carve(8808, 2, 768)
        kc = carve(10344, 2, 768)
        vv = carve(11880, 2, 512)
        qcT = carve(12904, 8, S)
        kcT = carve(14952, 8, S)
        S2 = carve(17000, 2, S)
        P2 = carve(17512, 2, S)
        PT2 = carve(18024, 2, S)
        mix2 = carve(8808, 2, D)
        Fc = carve(18536, 2, 4)
        lf = carve(18544, 2, 4)
        lft = carve(18552, 2, 4)
        tmp2 = carve(18560, 1920)
        hid2 = carve(4096, 22, S)
        sg2 = carve(10240, 2, S)

        bank = [ctx.enter_context(nc.psum_tensor(f"bank{i}", [P, 512], f32)) for i in range(8)]
        VB, AB, SB, MB = bank[0:4], bank[4:5], bank[5:7], bank[7]

        names = """cons_in slot_read par_in ga_in modrow_in m_filled t5_stored t5_in out_stored
            v_filled v_emptied a_filled a_emptied s_filled s_emptied v_step a_step
            ms_ready rstd_ready pool_ready cexp_ready cT_ready row_ready
            x_in gf_in x_ready sq_ready xn_ready zlog_ready la_ready exps_in exps_out qk_ready
            ke_ready AT_ready gexp_ready aq_ready nm_ready mixt_ready hid_ready hidv_ready
            fneg_ready flog_ready lf_ready qa_ready lat_ready heads_ready p2_ready sg_ready""".split()
        (cons_in, slot_read, par_in, ga_in, modrow_in, m_filled, t5_stored, t5_in, out_stored,
         v_filled, v_emptied, a_filled, a_emptied, s_filled, s_emptied, v_step, a_step,
         ms_ready, rstd_ready, pool_ready, cexp_ready, cT_ready, row_ready,
         x_in, gf_in, x_ready, sq_ready, xn_ready, zlog_ready, la_ready, exps_in, exps_out, qk_ready,
         ke_ready, AT_ready, gexp_ready, aq_ready, nm_ready, mixt_ready, hid_ready, hidv_ready,
         fneg_ready, flog_ready, lf_ready, qa_ready, lat_ready, heads_ready,
         p2_ready, sg_ready) = [sem(n) for n in names]
        slot_in = [sem(f"slot_in{i}") for i in range(NSLOT)]
        row_in = [sem(f"row_in{i}") for i in range(3)]
        row_out = [sem(f"row_out{i}") for i in range(3)]
        p1at, p1n = offsets(PAR1)
        p2at, p2n = offsets(PAR2)

        def slot(key):
            return ring[:, PLACE[key] % NSLOT, :]

        def slot_wait(eng, key):
            eng.wait_ge(slot_in[PLACE[key] % NSLOT], LANDED[key])

        def par(at, name):
            s, n = at[name]
            return params[:, s:s + n]

        def par1(name):
            return par(p1at, name)

        def par2(name):
            return par(p2at, name)

        def bc(ap, at, n):
            ap = ap.unsqueeze(at)
            shape = list(ap.shape)
            shape[at] = n
            return ap.broadcast_to(shape)

        t5hot = arena[0:32, 18560:19072]
        t5tab = arena[0:32, 19072:19076]
        t5col = arena[0:32, 11264:11776].rearrange("p (h n) -> p h n", h=4)
        t5rows = carve(9216, 4, 512)
        gf = params[:, 1024:2048]
        mark = {}
        powers = []

        def tiles1(l):
            return [0, 1, 2, 3] if l < L - 1 else [0, 1]

        def updates(kind, l):
            if kind == "par1":
                return sum(2 * len(tiles1(i)) for i in range(l))
            return updates("par1", L) + TS + 2 * TS * l

        block = ctx.enter_context(nc.Block())

        @block.sync
        def _(sp):
            def bias_row(m):
                if m < len(MODS):
                    if m >= 3:
                        sp.wait_ge(row_out[m % 3], 16 * (m // 3))
                    kind, l, c = MODS[m]
                    bias = a["b_mod"] if kind == "mod1" else a["b_ada_2"]
                    src = bias[l:l + 1, c * MODC:(c + 1) * MODC]
                    sp.dma_start(row[0:2, m % 3, :], src.partition_broadcast(2)).then_inc(row_in[m % 3], 16)

            def store_row(m):
                sp.wait_ge(row_ready, m + 1)
                kind, l, c = MODS[m]
                dst = a["mods"][2 * (kind == "mod2") + l, :, c * MODC:(c + 1) * MODC]
                sp.dma_start(dst, row[0:2, m % 3, :]).then_inc(row_out[m % 3], 16)

            for m in range(3):
                bias_row(m)
            stored = 0
            order = list(PLACE)
            for key in LOADS:
                kind, l, c = key
                if kind[:3] == "par":
                    if kind == "par2" or l > 0:
                        sp.wait_ge(x_ready, updates(kind, l))
                    w, n = (a["par1"], p1n) if kind == "par1" else (a["par2"], p2n)
                    sp.dma_start(params[:, 0:n], w[l]).then_inc(par_in, 16)
                    continue
                i = PLACE[key]
                dst = ring[:, i % NSLOT, :]
                if i >= NSLOT:
                    before = order[i - NSLOT]
                    if before in MODS:
                        sp.wait_ge(m_filled, MODS.index(before) + 1)
                    else:
                        sp.wait_ge(slot_read, sum(x not in MODS for x in order[:i - NSLOT + 1]))
                full = dst.rearrange("p (k n) -> p k n", n=MODC)
                if kind in ("mod1", "mod2"):
                    w = a["w_mod"] if kind == "mod1" else a["w_ada_2"]
                    src = w[l, :, c * MODC:(c + 1) * MODC].rearrange("(k p) n -> p k n", p=P)
                    sp.dma_start(full, src).then_inc(slot_in[i % NSLOT], 16)
                elif kind in ("in1", "in2"):
                    c0, c1 = CH1[c] if kind == "in1" else CH2[c]
                    w = a["w_in"] if kind == "in1" else a["w_in_2"]
                    src = w[l, :, c0:c1].rearrange("(k p) n -> p k n", p=P)
                    sp.dma_start(full[:, :, 0:c1 - c0], src).then_inc(slot_in[i % NSLOT], 16)
                elif kind in ("out1", "out2"):
                    w = a["w_out"] if kind == "out1" else a["w_out_2"]
                    src = w[l, :, c * MODC:(c + 1) * MODC].rearrange("(k p) n -> p k n", p=P)
                    sp.dma_start(full, src).then_inc(slot_in[i % NSLOT], 16)
                elif kind == "up1":
                    src = a["w_up"][l, :, c * MODC:(c + 1) * MODC].rearrange("(k p) n -> p k n", p=P)
                    sp.dma_start(full, src).then_inc(slot_in[i % NSLOT], 16)
                elif kind == "up2":
                    src = a["w_gate_up_2"][l].rearrange("(k p) (g n) -> p k g n", p=P, g=2)
                    for g in range(2):
                        sp.dma_start(full[:, :, g * 256:(g + 1) * 256],
                                     src[:, :, g, c * 256:(c + 1) * 256]).then_inc(slot_in[i % NSLOT], 16)
                elif kind == "down1":
                    half, kc_ = c // 4, c % 4
                    src = a["w_down"][l, kc_ * D:(kc_ + 1) * D, half * MODC:(half + 1) * MODC]
                    sp.dma_start(full, src.rearrange("(k p) n -> p k n", p=P)).then_inc(slot_in[i % NSLOT], 16)
                elif kind == "down2":
                    half, (k0, k1) = c // 3, HC2[c % 3]
                    src = a["w_down_2"][l, k0 * P:k1 * P, half * MODC:(half + 1) * MODC]
                    sp.dma_start(full[:, 0:k1 - k0, :], src.rearrange("(k p) n -> p k n", p=P))\
                      .then_inc(slot_in[i % NSLOT], 16)
                while stored < len(MODS) and PLACE[MODS[stored]] <= i - NSLOT:
                    if stored >= 1:
                        bias_row(stored + 2)
                    store_row(stored)
                    stored += 1
            sp.wait_ge(x_ready, updates("par2", L))
            sp.dma_start(out[0].rearrange("(t p) d -> p t d", p=P), X[:, 0:2, :]).then_inc(out_stored, 16)
            sp.wait_ge(out_stored, 16)

        @block.tensor
        def _(pe):
            nth = counter()
            k = {"v": 0, "a": 0, "s": 0, "unread": 0, "open": 0}
            rings = {"v": (VB, v_filled, v_emptied), "a": (AB, a_filled, a_emptied), "s": (SB, s_filled, s_emptied)}

            def take(r):
                banks, filled, emptied = rings[r]
                if k[r] >= len(banks):
                    pe.wait_ge(emptied, k[r] - len(banks) + 1)
                k[r] += 1
                return banks[(k[r] - 1) % len(banks)], filled

            def emptied(r):
                if k[r]:
                    pe.wait_ge(rings[r][2], k[r])

            def mm(out_, lhsT, rhs, start=True, stop=True, inc=None):
                ins = nc.tensor.matmul(out_, lhsT, rhs, start=start, stop=stop)
                if inc is not None:
                    ins.then_inc(inc, 1)
                elif k["unread"]:
                    ins.then_inc(slot_read, 1)
                    k["unread"] -= 1

            def tr(out_, in_, inc=None):
                n = in_.shape[0]
                ins = nc.tensor.transpose(out_, in_, ident[0:n, 0:n])
                if inc is not None:
                    ins.then_inc(inc, 1)
                elif k["unread"]:
                    ins.then_inc(slot_read, 1)
                    k["unread"] -= 1

            def through():
                k["unread"] += k["open"]
                k["open"] = 0

            def weights(key):
                through()
                slot_wait(pe, key)
                k["open"] = 1
                return slot(key).rearrange("p (k n) -> p k n", n=MODC)

            def contract(out_, lhs, rhs, inc, n=KT):
                for i in range(n):
                    mm(out_, lhs(i), rhs(i), i == 0, i == n - 1, inc if i == n - 1 else None)

            def fill():
                if not due:
                    return
                key = due.pop(0)
                n = MODS.index(key)
                v0, m = (0, 2) if key[0] == "mod1" else (2, 1)
                w = weights(key)
                if n:
                    pe.wait_ge(row_ready, n)
                contract(MB[0:m, :], lambda i: cT[:, v0:v0 + m, i], lambda i: w[:, i, :], m_filled)
                k["open"] = 0

            def mod_columns():
                pe.wait_ge(modrow_in, nth(modrow_in, 32))
                b, filled = take("v")
                tr(b[:, 0:32], modrow[:, :], filled)

            def turn(tiles, width, src):
                for ft in range(KT):
                    b, filled = take("va"[ft % 2])
                    for n, t in enumerate(tiles):
                        tr(b[:, n * P:(n + 1) * P], src(ft, t), filled if n == len(tiles) - 1 else None)

            def normed(tiles):
                pe.wait_ge(xn_ready, nth(xn_ready, len(tiles)))
                turn(tiles, 512, lambda ft, t: xn[:, t, ft * P:(ft + 1) * P])
                emptied("v")
                emptied("a")

            def gla(l):
                pe.wait_ge(par_in, nth(par_in, 16))
                b, filled = take("v")
                for t in range(4):
                    tr(b[0:32, t * P:(t + 1) * P], u[:, t, RF:RF + 32], filled if t == 3 else None)
                emptied("v")
                for t in range(4):
                    b, filled = take("v")
                    mm(b[:, :], rT[:, t * P:(t + 1) * P], par1("wg")[0:33, :], inc=filled)
                    mark["z", l, t] = k["v"]
                for col, tiles in ((GQ, tiles1(l)), (GK, tiles1(l))):
                    for hp in range(2):
                        b, filled = take("a")
                        for n, t in enumerate(tiles):
                            tr(b[:, t * P:(t + 1) * P], u[:, t, col + P * hp:col + P * (hp + 1)],
                               filled if n == len(tiles) - 1 else None)
                fill()
                pe.wait_ge(la_ready, nth(la_ready))
                b, filled = take("a")
                for t in range(4):
                    for j in range(4):
                        mm(b[:, 4 * t + j:4 * t + j + 1], la[:, t, j * P:(j + 1) * P], const("up16")[:, P - 1:P],
                           inc=filled if t == 3 and j == 3 else None)
                for t in range(4):
                    b, filled = take("a")
                    mm(b[:, 0:256], const("after16"), la[:, t, 0:256])
                    mm(b[:, 256:512], const("before16"), la[:, t, 256:512], inc=filled)
                mark["dec", l] = k["a"] - 4
                fill()
                pe.wait_ge(ke_ready, nth(ke_ready))
                for pair in STATES:
                    for d, (t, _) in enumerate(pair):
                        b, filled = take("v")
                        for h in range(4):
                            mm(b[64 * (h % 2):64 * (h % 2) + 64, 64 * (h // 2):64 * (h // 2) + 64],
                               ke4[:, t, 256 * d + 64 * h:256 * d + 64 * h + 64],
                               u[:, t, GV + 64 * h:GV + 64 * h + 64], inc=filled if h == 3 else None)
                emptied("v")
                for t in tiles1(l):
                    b, filled = take("a")
                    for d in range(2):
                        for hp in range(2):
                            j = 2 * d + hp
                            mm(b[:, j * P:(j + 1) * P], la[:, t, j * P:(j + 1) * P],
                               const("up16" if d == 0 else "lo16"), inc=filled if j == 3 else None)
                    mark["bT", l, t] = k["a"]
                    fill()
                    fill()
                    pe.wait_ge(qk_ready, nth(qk_ready))
                    for par_ in range(2):
                        b, filled = take("s")
                        po = 64 * par_
                        for hp in range(2):
                            o = P * hp

                            def block_(j0, i0, n, kk, qq, d, o_=None, inc=None):
                                at = o + i0 if o_ is None else o_
                                mm(b[j0:j0 + n, at:at + n], kk[po:po + 64, 2 * d + hp, j0:j0 + n],
                                   qq[po:po + 64, 2 * d + hp, i0:i0 + n], inc=inc)

                            block_(0, 64, 64, qk64, qk64, 0)
                            block_(64, 0, 64, qk64, qk64, 1)
                            for B in (0, 64):
                                block_(B, B + 32, 32, qk32, qk32, 0)
                                block_(B + 32, B, 32, qk32, qk32, 1)
                            for B in range(0, P, 32):
                                block_(B, B, 32, kd, qd, 0)
                                block_(B, B, 32, kd, qd, 1, 256 + 32 * hp, filled if hp == 1 and B == 96 else None)
                    pe.wait_ge(AT_ready, nth(AT_ready))
                    for par_ in range(2):
                        b, filled = take("v")
                        po = 64 * par_
                        for hp in range(2):
                            o_ = b[:, 64 * hp:64 * hp + 64]
                            h = 2 * hp + par_
                            dirs = [d for d in range(2) if not (d == 0 and t == 2) and not (d == 1 and t == 3)]
                            mm(o_, AT[:, 2 * par_ + hp, :], u[:, t, GV + 64 * h:GV + 64 * h + 64], True, False)
                            for d in dirs:
                                j = 2 * d + hp
                                last = d == dirs[-1]
                                mm(o_, qi[po:po + 64, j, :], St[po:po + 64, t, 64 * j:64 * j + 64], False, last,
                                   filled if last and hp == 1 else None)

            def pooling(l):
                n = S if l == L - 1 else 512
                band = par1("band").rearrange("p (t g n) -> p t g n", t=2, g=4)
                for g in range(2):
                    b, filled = take("a")
                    for s in range(n // S):
                        for par_ in range(2):
                            for t in range(2):
                                end = s == n // S - 1 and par_ == 1 and t == 1
                                mm(b[64 * par_:64 * par_ + 64, S * s:S * s + S],
                                   u[:, 2 * s + t, P * g + 64 * par_:P * g + 64 * par_ + 64],
                                   band[:, t, 2 * g + par_, :], t == 0, t == 1, filled if end else None)
                emptied("a")
                for g in range(2):
                    b, filled = take("v")
                    mm(b[:, 0:n], par1("wpool").rearrange("p (g n) -> p g n", g=2)[:, g, :], mT[:, g, 0:n],
                       inc=filled)

            def attention1(l):
                for _ in range(2):
                    fill()
                pe.wait_ge(aq_ready, nth(aq_ready))
                tiles = tiles1(l)
                for j in range(4):
                    b, filled = take("va"[j % 2])
                    for n, t in enumerate(tiles):
                        tr(b[:, t * P:(t + 1) * P], u[:, t, AQ + P * j:AQ + P * (j + 1)],
                           filled if n == len(tiles) - 1 else None)
                for g in range(2):
                    b, filled = take("v")
                    for t in range(4):
                        tr(b[:, t * P:(t + 1) * P], kdup[:, t, P * g:P * (g + 1)], filled if t == 3 else None)
                emptied("v")
                emptied("a")
                units = units1(l)
                s0, a0 = k["s"], k["a"]
                for i in range(len(units) + 2):
                    if i < len(units):
                        t, h, k0 = units[i]
                        b, filled = take("s")
                        po = 64 * (h % 2)
                        mm(b[:, 0:512 - k0], qT[po:po + 64, h // 2, t * P:(t + 1) * P],
                           kT[po:po + 64, h // 4, k0:512], inc=filled)
                    if 1 <= i <= len(units):
                        t, h, k0 = units[i - 1]
                        pe.wait_ge(s_emptied, s0 + i)
                        b, filled = take("a")
                        n = (512 - k0) // P
                        for c in range(n):
                            tr(b[:, c * P:(c + 1) * P], Pr[:, (i - 1) % 2, c * P:(c + 1) * P],
                               filled if c == n - 1 else None)
                    if i >= 2:
                        t, h, k0 = units[i - 2]
                        pe.wait_ge(a_emptied, a0 + i - 1)
                        b, filled = take("v")
                        n = (512 - k0) // P
                        contract(b[:, 0:64], lambda c: PT[:, i % 2, c * P:(c + 1) * P],
                                 lambda c: u[:, k0 // P + c, AV + 64 * (h // 4):AV + 64 * (h // 4) + 64], filled, n)
                    if i < len(units) and i % 4 == 3:
                        fill()

            def layer1(l):
                due.extend(MODS[12 * l + NFIRST:12 * l + NFIRST + 12])
                normed([0, 1, 2, 3])
                last_c, w = -1, None
                for c, t, lo, hi, r in in1_jobs(l):
                    if c != last_c:
                        last_c, w = c, weights(("in1", l, c))
                    b, filled = take(r)
                    contract(b[:, 0:hi - lo], lambda i: actT[:, i, t * P:(t + 1) * P], lambda i: w[:, i, lo:hi], filled)
                through()
                mark["in1", l] = k["a"]
                emptied("v")
                emptied("a")
                gla(l)
                pooling(l)
                attention1(l)
                emptied("v")
                for j in range(6):
                    b, filled = take("va"[j % 2])
                    for n, t in enumerate(tiles1(l)):
                        tr(b[:, t * P:(t + 1) * P], mixt[:, t, j * P:(j + 1) * P],
                           filled if n == len(tiles1(l)) - 1 else None)
                emptied("v")
                emptied("a")
                mod_columns()
                for half in range(2):
                    w = weights(("out1", l, half))
                    for t in tiles1(l):
                        b, filled = take("v")
                        contract(b[:, :], lambda i: actT[:, i, t * P:(t + 1) * P], lambda i: w[:, i, :], filled)
                normed(tiles1(l))
                mod_columns()
                n = P * len(tiles1(l))
                for c in range(F1 // MODC):
                    w = weights(("up1", l, c))
                    for m in range(4):
                        b, filled = take("va"[m % 2])
                        contract(b[:, 0:n], lambda i: w[:, i, m * P:(m + 1) * P], lambda i: actT[:, i, 0:n], filled)
                for half in range(2):
                    banks = [take("v") for t in tiles1(l)]
                    for c in range(4):
                        w = weights(("down1", l, 4 * half + c))
                        if half == 0:
                            pe.wait_ge(hid_ready, nth(hid_ready, 4))
                            pe.wait_ge(hidv_ready, nth(hidv_ready, 4))
                        for t, (b, filled) in zip(tiles1(l), banks):
                            for i in range(8):
                                mm(b[:, :], hid[:, 8 * c + i, t * P:(t + 1) * P], w[:, i, :], c == 0 and i == 0,
                                   c == 3 and i == 7, filled if c == 3 and i == 7 else None)

            def layer2(l):
                due.extend(MODS[12 * (L + l) + NFIRST:12 * (L + l) + NFIRST + 12])
                normed([0, 1])
                for c, (c0, c1) in enumerate(CH2):
                    w = weights(("in2", l, c))
                    for t in range(TS):
                        b, filled = take("va"[t])
                        contract(b[:, 0:c1 - c0], lambda i: actT[:, i, t * P:(t + 1) * P],
                                 lambda i: w[:, i, 0:c1 - c0], filled)
                through()
                mark["in2", l] = k["a"]
                emptied("v")
                emptied("a")
                pe.wait_ge(par_in, nth(par_in, 16))
                for col in (QM, KM):
                    b, filled = take("a")
                    for hp in range(2):
                        for t in range(TS):
                            tr(b[:, S * hp + t * P:S * hp + (t + 1) * P], u2[:, t, col + P * hp:col + P * (hp + 1)],
                               filled if hp == 1 and t == 1 else None)
                fill()
                pe.wait_ge(lf_ready, nth(lf_ready))
                b, filled = take("v")
                mm(b[:, 0:4], const("up"), lf[:, 0, :])
                mm(b[:, 4:8], ones, lf[:, 0, :], True, False)
                mm(b[:, 4:8], const("up"), lf[:, 1, :], False, True, filled)
                fill()
                pe.wait_ge(lat_ready, nth(lat_ready))
                b, filled = take("v")
                for i in range(2):
                    for t in range(TS):
                        tr(b[:, S * i + t * P:S * i + (t + 1) * P], u2[:, t, CQ + i * P:CQ + (i + 1) * P],
                           filled if i == 1 and t == 1 else None)
                b, filled = take("v")
                for t in range(TS):
                    tr(b[:, t * P:(t + 1) * P], u2[:, t, CKV:KR], filled if t == 1 else None)
                emptied("v")
                wq = par2("w_uq").rearrange("p (k n) -> p k n", k=2)
                wkv = par2("w_ukv")
                for t in range(TS):
                    for n in range(2):
                        b, filled = take("v")
                        contract(b[:, 0:384], lambda i: cqT[:, i, t * P:(t + 1) * P],
                                 lambda i: wq[:, i, 384 * n:384 * (n + 1)], filled, 2)
                    for n in range(2):
                        b, filled = take("a")
                        mm(b[:, :], ckvT[:, t * P:(t + 1) * P], wkv[:, 512 * n:512 * (n + 1)], inc=filled)
                mark["kv", l] = k["a"]
                fill()
                pe.wait_ge(qa_ready, nth(qa_ready))
                for src, n in ((qa, 0), (ka, 1)):
                    for hp in range(2):
                        b, filled = take("va"[n])
                        for e in range(2):
                            for t in range(TS):
                                tr(b[0:66, S * e + t * P:S * e + (t + 1) * P], src[:, 4 * t + 2 * hp + e, :],
                                   filled if e == 1 and t == 1 else None)
                fill()
                pe.wait_ge(heads_ready, nth(heads_ready))
                emptied("a")
                for src, n in ((ql, 0), (kc, 1)):
                    for hp in range(4):
                        b, filled = take("va"[n])
                        for e in range(2):
                            for t in range(TS):
                                h = 2 * hp + e
                                tr(b[0:96, S * e + t * P:S * e + (t + 1) * P], src[:, t, 96 * h:96 * h + 96],
                                   filled if e == 1 and t == 1 else None)
                emptied("v")
                emptied("a")
                s0, a0 = k["s"], k["a"]
                for i in range(len(UNITS2) + 2):
                    if i < len(UNITS2):
                        kind, h, q = UNITS2[i]
                        n = P * (q + 1)
                        b, filled = take("s")
                        if kind == "fox":
                            lhs, rhs = qfT[0:66, h, q * P:(q + 1) * P], kfT[0:66, h, 0:n]
                        elif kind == "moba":
                            po = 64 * (h % 2)
                            lhs, rhs = qmT[po:po + 64, h // 2, q * P:(q + 1) * P], kmT[po:po + 64, h // 2, 0:n]
                        else:
                            lhs, rhs = qcT[0:96, h, q * P:(q + 1) * P], kcT[0:96, h, 0:n]
                        mm(b[:, 0:n], lhs, rhs, inc=filled)
                    if 1 <= i <= len(UNITS2):
                        kind, h, q = UNITS2[i - 1]
                        pe.wait_ge(p2_ready, nth(p2_ready))
                        b, filled = take("a")
                        for c in range(q + 1):
                            tr(b[:, c * P:(c + 1) * P], P2[:, (i - 1) % 2, c * P:(c + 1) * P],
                               filled if c == q else None)
                    if i >= 2:
                        kind, h, q = UNITS2[i - 2]
                        pe.wait_ge(a_emptied, a0 + i - 1)
                        b, filled = take("v")

                        def value(c):
                            if kind == "fox":
                                return u2[:, c, VF + 64 * h:VF + 64 * h + 64]
                            if kind == "moba":
                                return u2[:, c, VM + 64 * h:VM + 64 * h + 64]
                            return vv[:, c, 64 * h:64 * h + 64]
                        contract(b[:, 0:64], lambda c: PT2[:, i % 2, c * P:(c + 1) * P], value, filled, q + 1)
                    if i < len(UNITS2) and i % 4 == 3:
                        fill()
                pe.wait_ge(mixt_ready, nth(mixt_ready))
                turn([0, 1], S, lambda ft, t: mix2[:, t, ft * P:(ft + 1) * P])
                emptied("v")
                emptied("a")
                mod_columns()
                for half in range(2):
                    w = weights(("out2", l, half))
                    for t in range(TS):
                        b, filled = take("v")
                        contract(b[:, :], lambda i: actT[:, i, t * P:(t + 1) * P], lambda i: w[:, i, :], filled)
                normed([0, 1])
                if l < L - 1:
                    mod_columns()
                for c in range(F2 // 256):
                    w = weights(("up2", l, c))
                    for m in range(2):
                        b, filled = take("s")
                        for g in range(2):
                            contract(b[:, S * g:S * (g + 1)], lambda i: w[:, i, S * g + m * P:S * g + (m + 1) * P],
                                     lambda i: actT[:, i, 0:S], filled if g == 1 else None)
                for half in range(2):
                    banks = [take("v") for t in range(TS)]
                    for c, (k0, k1) in enumerate(HC2):
                        w = weights(("down2", l, 3 * half + c))
                        if c == 0 and half == 0:
                            emptied("s")
                        for t, (b, filled) in enumerate(banks):
                            for i in range(k1 - k0):
                                end = k0 + i == 21
                                mm(b[:, :], hid2[:, k0 + i, t * P:(t + 1) * P], w[:, i, :], k0 + i == 0, end,
                                   filled if end else None)

            pe.wait_ge(cons_in, 16 * NCONS)
            pe.wait_ge(cT_ready, 1)
            for h in range(4):
                b, filled = take("v")
                mm(b[:, :], t5col[:, h, :], t5hot, inc=filled)
            due = MODS[:NFIRST]
            for _ in range(NFIRST):
                fill()
            mod_columns()
            for l in range(L):
                layer1(l)
            for l in range(L):
                layer2(l)

        @block.vector
        def _(dve):
            nth = counter()
            v = nc.vector

            def step(ins, signal=v_step):
                ins.then_inc(signal, 1)
                dve.wait_ge(signal, nth(signal))

            def filled(r="v"):
                banks, s = (VB, v_filled) if r == "v" else (SB, s_filled)
                n = nth(s)
                dve.wait_ge(s, n)
                return banks[(n - 1) % len(banks)]

            def emptied(ins, r="v"):
                ins.then_inc(v_emptied if r == "v" else s_emptied, 1)

            def tt(o, x, y, op):
                return v.tensor_tensor(o, x, y, op)

            def minus_abs(x):
                return v.scalar_tensor_tensor(out=x, in0=x, scalar=-1.0, in1=x, op0=ALU.mult, op1=ALU.min)

            def power(ins, at, n):
                ins.then_inc(ms_ready, 1)
                powers.append((at, n))
                dve.wait_ge(rstd_ready, nth(rstd_ready))

            def rstd(parts):
                for i, (at, n, div) in enumerate(parts):
                    ins = v.tensor_scalar(ms[:, at:at + n], ss[:, at:at + n], 1.0 / div, EPS, ALU.mult, ALU.add)
                    if i < len(parts) - 1:
                        step(ins)
                power(ins, parts[0][0], parts[-1][0] + parts[-1][1] - parts[0][0])

            def mod_row():
                if not due:
                    return
                n = MODS.index(due.pop(0))
                m = 2 if n < 12 * L else 1
                dve.wait_ge(row_in[n % 3], 16 * (n // 3 + 1))
                dve.wait_ge(m_filled, n + 1)
                r = row[0:m, n % 3, :]
                step(tt(r, MB[0:m, :], r, ALU.add), row_ready)

            def mod_columns(kind, l, part):
                m = 2 if kind == "mod1" else 1
                gain = gcol[:, (0 if kind == "mod1" else 2) + part, l, :]
                b = filled()
                src = b[:, 0:32].rearrange("p (v w k) -> p w k v", v=2, w=2)
                step(v.tensor_copy(modT[:, 0, :, 0:m], src[:, 0, :, 0:m]))
                step(v.scalar_tensor_tensor(out=modT[:, 1, :, 0:m], in0=src[:, 1, :, 0:m], scalar=1.0,
                                            in1=bc(gain, 2, m), op0=ALU.add, op1=ALU.mult), v_emptied)

            def norm_tile(t):
                dve.wait_ge(sq_ready, nth(sq_ready))
                rstd([(t, 1, D)])
                step(v.tensor_scalar(xn[:, t, :], X[:, t, :], rs[:, t:t + 1], None, ALU.mult), xn_ready)

            def turned(tiles):
                for ft in range(0, KT, 2):
                    b = filled()
                    for s in range(len(tiles) // 2):
                        ins = v.tensor_scalar(actT[:, ft, S * s:S * s + S], b[:, S * s:S * s + S],
                                              modT[:, 1, ft, s:s + 1], modT[:, 0, ft, s:s + 1], ALU.mult, ALU.add)
                        if s < len(tiles) // 2 - 1:
                            step(ins)
                    step(ins, v_emptied)

            def gla(l):
                dve.wait_ge(par_in, nth(par_in, 16))
                step(v.memset(rT[32:33, :], 1.0))
                b = filled()
                step(v.tensor_copy(rT[0:32, :], b[0:32, :]), v_emptied)
                for t in range(4):
                    b = filled()
                    step(v.tensor_scalar(la[:, t, :], b[:, :], 0.0, None, ALU.min))
                    step(v.scalar_tensor_tensor(out=zt[:, t, :], in0=la[:, t, :], scalar=2.0, in1=b[:, :],
                                                op0=ALU.mult, op1=ALU.subtract), v_emptied)
                aq_sums(l)
                for t in range(4):
                    dve.wait_ge(zlog_ready, nth(zlog_ready))
                    step(tt(la[:, t, :], la[:, t, :], zt[:, t, :], ALU.subtract), la_ready if t == 3 else v_step)
                mod_row()
                for t in range(4):
                    dve.wait_ge(a_emptied, mark["dec", l] + 1 + t)
                    for d in range(2):
                        o = ke4[:, t, 256 * d:256 * (d + 1)]
                        step(tt(o, o, u[:, t, GK:GV], ALU.mult), ke_ready if t == 3 and d == 1 else v_step)
                for n, pair in enumerate(STATES):
                    for d, (t, to) in enumerate(pair):
                        b = filled()
                        for hp in range(2):
                            j = 2 * d + hp
                            o = St[:, to, 64 * j:64 * j + 64]
                            part = b[:, 64 * hp:64 * hp + 64]
                            if n == 0:
                                ins = v.tensor_copy(o, part)
                            else:
                                ins = v.scalar_tensor_tensor(out=o, in0=St[:, t, 64 * j:64 * j + 64],
                                                             scalar=dec[:, 4 * t + j:4 * t + j + 1], in1=part,
                                                             op0=ALU.mult, op1=ALU.add)
                            step(ins, v_emptied if hp == 1 else v_step)
                mod_row()
                dve.wait_ge(rstd_ready, nth(rstd_ready))
                for t in tiles1(l):
                    dve.wait_ge(a_emptied, mark["bT", l, t])
                    for d in range(2):
                        j = slice(2 * d, 2 * d + 2)
                        src = bT[:, j, :]
                        step(tt(qk64[:, j, :], src, bT[:, j, 63 + d:64 + d].broadcast_to([P, 2, P]), ALU.subtract))
                        for dst, n in ((qk32, 64), (qd, 32)):
                            s4 = src.rearrange("p h (b i) -> p h b i", i=n)
                            ref = s4[:, :, :, n // 2 - 1 + d:n // 2 + d].broadcast_to([P, 2, P // n, n])
                            step(tt(dst[:, j, :].rearrange("p h (b i) -> p h b i", i=n), s4, ref, ALU.subtract))
                    step(minus_abs(qk96))
                    step(v.tensor_scalar(qd[:, :, :], qd[:, :, :], 80.0, -80.0, ALU.min, ALU.max), exps_in)
                    aq_norm(l, t)
                    mod_row()
                    aq_rope(t)
                    if l == L - 1:
                        aq_norm(l, t + 2)
                    dve.wait_ge(exps_out, nth(exps_out))
                    q, kk = qgT[:, :, t * P:(t + 1) * P], kgT[:, :, t * P:(t + 1) * P]
                    for d in range(2):
                        j = slice(2 * d, 2 * d + 2)
                        for dst, src in ((qd, q), (kd, kk), (qi, q)):
                            step(tt(dst[:, j, :], dst[:, j, :], src, ALU.mult))
                        for half in range(2):
                            src = q if half != d else kk
                            o = qk64[:, j, 64 * half:64 * half + 64]
                            step(tt(o, o, src[:, :, 64 * half:64 * half + 64], ALU.mult))
                            o = qk32[:, j, :].rearrange("p h (b g i) -> p h b g i", b=2, g=2)[:, :, :, half, :]
                            sv = src.rearrange("p h (b g i) -> p h b g i", b=2, g=2)[:, :, :, half, :]
                            step(tt(o, o, sv, ALU.mult), qk_ready if d == 1 and half == 1 else v_step)
                    for pr in range(2):
                        b = filled("s")
                        main = b[:, 0:256].rearrange("p (h i) -> p h i", h=2)
                        step(tt(AT[:, 2 * pr:2 * pr + 2, :], main, bc(const("mask_f"), 1, 2), ALU.mult))
                        diag = b[:, 256:320].rearrange("p (h i) -> p h i", h=2)
                        step(tt(atb[:, 2 * pr:2 * pr + 2, :], diag, bc(const("mask_b"), 1, 2), ALU.mult), s_emptied)
                    for B in range(0, P, 32):
                        o = AT[B:B + 32, :, B:B + 32]
                        step(tt(o, o, atb[B:B + 32, :, :], ALU.add), AT_ready if B == 96 else v_step)
                    mod_row()
                    for pr in range(2):
                        b = filled()
                        o = mixt[:, t, 0:256].rearrange("p (h e c) -> p h e c", h=2, e=2)[:, :, pr, :]
                        step(v.tensor_copy(o, b[:, 0:128].rearrange("p (h c) -> p h c", h=2)), v_emptied)
                n = len(tiles1(l))
                o = mixt[:, 0:n, 0:256]
                o4 = o.rearrange("p t (h c) -> p t h c", h=4)
                step(tt(gsq[:, 0:n, :], o, o, ALU.mult))
                step(v.tensor_reduce(ss[:, 0:4 * n].rearrange("p (t h) -> p t h", h=4),
                                     gsq[:, 0:n, :].rearrange("p t (h c) -> p t h c", h=4), X_AXIS, ALU.add))
                rstd([(0, 4 * n, 64)])
                mod_row()
                for t in range(n):
                    step(tt(o4[:, t], o4[:, t], bc(rs[:, 4 * t:4 * t + 4], 2, 64), ALU.mult))
                    step(tt(o4[:, t], o4[:, t], bc(par1("g_gla"), 1, 4), ALU.mult))
                g = gexp[:, 0:n, :]
                dve.wait_ge(gexp_ready, nth(gexp_ready))
                step(v.tensor_scalar(g, g, 1.0, None, ALU.add))
                step(v.reciprocal(g, g))
                step(tt(g, g, u[:, 0:n, GG:RF], ALU.mult))
                step(tt(o, o, g, ALU.mult))

            def rope(x1, x2, cos, sin, t1, t2):
                step(tt(t1, x1, sin, ALU.mult))
                step(tt(t2, x2, sin, ALU.mult))
                step(tt(x1, x1, cos, ALU.mult))
                step(tt(x2, x2, cos, ALU.mult))
                step(tt(x1, x1, t2, ALU.subtract))
                step(tt(x2, x2, t1, ALU.add))

            def span(l, t):
                return 0 if t in tiles1(l) else 8

            def aq_sums(l):
                for t in range(4):
                    if span(l, t) == 0:
                        x = u[:, t, AQ:AK].rearrange("p (a n) -> p a n", a=2)
                        step(tt(sqq, x, x, ALU.mult))
                        step(v.tensor_reduce(ss[:, 10 * t:10 * t + 8].rearrange("p (a h) -> p a h", a=2),
                                             sqq.rearrange("p a (h c) -> p a h c", c=64), X_AXIS, ALU.add))
                    x = u[:, t, AK:AV]
                    step(tt(sqk, x, x, ALU.mult))
                    step(v.tensor_reduce(ss[:, 10 * t + 8:10 * t + 10], sqk.rearrange("p (h c) -> p h c", c=64),
                                         X_AXIS, ALU.add))
                step(v.tensor_scalar(ms[:, 0:40], ss[:, 0:40], 1.0 / 64, EPS, ALU.mult, ALU.add), ms_ready)
                powers.append((0, 40))

            def aq_norm(l, t):
                h0 = span(l, t)
                x = u[:, t, AQ + 64 * h0:AV].rearrange("p (h c) -> p h c", c=64)
                step(tt(x, x, bc(rs[:, 10 * t + h0:10 * t + 10], 2, 64), ALU.mult))
                if h0 == 0:
                    step(tt(x[:, 0:8, :], x[:, 0:8, :], bc(par1("g_q"), 1, 8), ALU.mult))
                xk = x[:, 8 - h0:10 - h0, :]
                step(tt(xk, xk, bc(par1("g_k"), 1, 2), ALU.mult))

            def aq_rope(t):
                if t < TS:
                    table = const("rope1").rearrange("p (t c a f) -> p t c a f", t=2, c=2, a=2)
                    x = u[:, t, AQ:AV].rearrange("p (h a b f) -> p h a b f", a=2, b=2, f=16)
                    for axis in range(2):
                        t1 = mixt[:, 2, 256:416].rearrange("p (h f) -> p h f", f=16)
                        t2 = mixt[:, 3, 256:416].rearrange("p (h f) -> p h f", f=16)
                        rope(x[:, :, axis, 0, :], x[:, :, axis, 1, :], bc(table[:, t, 0, axis, :], 1, 10),
                             bc(table[:, t, 1, axis, :], 1, 10), t1, t2)

            def attention1(l):
                for t in range(4):
                    o = kdup[:, t, :].rearrange("p (g e c) -> p g e c", g=2, e=2)
                    k2 = u[:, t, AK:AV].rearrange("p (g c) -> p g c", g=2)
                    step(v.tensor_copy(o, bc(k2, 2, 2)), aq_ready if t == 3 else v_step)
                mod_row()
                n = P * len(tiles1(l))
                for g in range(2):
                    b = filled()
                    step(v.tensor_scalar(actT[:, g, 0:n], b[:, 0:n], spool[:, l, g:g + 1], None, ALU.mult), v_emptied)
                for j in (0, 2):
                    b = filled()
                    step(v.tensor_copy(qT[:, j, 0:n], b[:, 0:n]), v_emptied)
                for g in range(2):
                    b = filled()
                    step(v.tensor_copy(kT[:, g, :], b[:, :]), v_emptied)
                units = units1(l)
                for i in range(len(units) + 2):
                    if i < len(units):
                        t, h, k0 = units[i]
                        if i % 4 == 2 and i > 2:
                            mod_row()
                        b = filled("s")
                        step(v.tensor_reduce(mx[:, i % 2:i % 2 + 1], b[:, 0:512 - k0], X_AXIS, ALU.max))
                        step(v.tensor_scalar(nm[:, i % 2:i % 2 + 1], mx[:, i % 2:i % 2 + 1], -0.125, None, ALU.mult),
                             nm_ready)
                    if i >= 2:
                        t, h, k0 = units[i - 2]
                        b = filled()
                        r = rinv[:, i % 2:i % 2 + 1]
                        step(v.reciprocal(r, rsum[:, (i - 2) % 4:(i - 2) % 4 + 1]))
                        step(v.tensor_scalar(mixt[:, t, 256 + 64 * h:320 + 64 * h], b[:, 0:64], r, None, ALU.mult),
                             v_emptied)
                nth(s_emptied, len(units))
                mod_row()

            def residual1(tiles, behind):
                dve.wait_ge(ga_in, nth(ga_in, 32))
                for half in range(2):
                    c = slice(half * MODC, (half + 1) * MODC)
                    for t in tiles:
                        b = filled()
                        step(tt(tmpx[:, t % 2, :], b[:, :], GA[:, t // 2, c], ALU.mult), v_emptied)
                        step(tt(X[:, t, c], X[:, t, c], tmpx[:, t % 2, :], ALU.add), x_ready if half else v_step)
                        if half:
                            behind(t)

            def layer1(l):
                due.extend(MODS[12 * l + NFIRST:12 * l + NFIRST + 12])
                if l == 0:
                    dve.wait_ge(t5_in, 16)
                    step(tt(t5[:, :, :], t5[:, :, :], bc(const("causal"), 1, 4), ALU.add))
                turned([0, 1, 2, 3])
                for c, t, lo, hi, r in in1_jobs(l):
                    if r == "v":
                        b = filled()
                        c0 = CH1[c][0]
                        step(v.tensor_copy(u[:, t, c0 + lo:c0 + hi], b[:, 0:hi - lo]), v_emptied)
                dve.wait_ge(a_emptied, mark["in1", l])
                gla(l)
                attention1(l)
                n = P * len(tiles1(l))
                for j in (0, 2, 4):
                    b = filled()
                    step(v.tensor_copy(actT[:, 2 + j, 0:n], b[:, 0:n]), v_emptied)
                mod_columns("mod1", l, 1)
                residual1(tiles1(l), norm_tile)
                turned(tiles1(l))
                mod_columns("mod1" if l < L - 1 else "mod2", (l + 1) % L, 0)
                n = P * len(tiles1(l))
                for m in range(0, F1 // P, 2):
                    b = filled()
                    step(v.tensor_scalar(hid[:, m, 0:n], b[:, 0:n], 0.0, None, ALU.max), v_emptied)
                    step(tt(hid[:, m, 0:n], hid[:, m, 0:n], hid[:, m, 0:n], ALU.mult), hidv_ready)
                residual1(tiles1(l), norm_tile if l < L - 1 else last_norm)

            def last_norm(t):
                dve.wait_ge(sq_ready, nth(sq_ready))
                rstd([(t, 1, D)])
                dve.wait_ge(gf_in, 16)
                step(v.scalar_tensor_tensor(out=X[:, t, :], in0=X[:, t, :], scalar=rs[:, t:t + 1], in1=gf,
                                            op0=ALU.mult, op1=ALU.mult), x_ready)
                norm_tile(t)

            def squares(o, src, at):
                step(v.tensor_tensor_reduce(out=o, in0=src, in1=src, scale=1.0, scalar=0.0, op0=ALU.mult,
                                            op1=ALU.add, accum_out=ss[:, at:at + 1]))

            def residual2(behind):
                dve.wait_ge(ga_in, nth(ga_in, 32))
                step(tt(GA[:, 0, :], GA[:, 0, :], post, ALU.mult))
                for half in range(2):
                    c = slice(half * MODC, (half + 1) * MODC)
                    for t in range(TS):
                        b = filled()
                        y = y2[:, t, c]
                        step(v.tensor_copy(y, b[:, :]), v_emptied)
                        squares(tmp2[:, 0:MODC], y, t)
                        mean = ms[:, t:t + 1]
                        if half == 0:
                            step(v.tensor_scalar(mean, ss[:, t:t + 1], 1.0 / D, EPS, ALU.mult, ALU.add))
                            step(tt(y, y, GA[:, 0, c], ALU.mult))
                        else:
                            v.scalar_tensor_tensor(out=mean, in0=ss[:, t:t + 1], scalar=1.0 / D, in1=mean,
                                                   op0=ALU.mult, op1=ALU.add).then_inc(ms_ready, 1)
                            powers.append((t, 1))
                            step(tt(y, y, GA[:, 0, c], ALU.mult))
                            dve.wait_ge(rstd_ready, nth(rstd_ready))
                            step(v.scalar_tensor_tensor(out=X[:, t, :], in0=y2[:, t, :], scalar=rs[:, t:t + 1],
                                                        in1=X[:, t, :], op0=ALU.mult, op1=ALU.add), x_ready)
                            behind(t)

            def layer2(l):
                due.extend(MODS[12 * (L + l) + NFIRST:12 * (L + l) + NFIRST + 12])
                turned([0, 1])
                for c, (c0, c1) in enumerate(CH2):
                    b = filled()
                    step(v.tensor_copy(u2[:, 0, c0:c1], b[:, 0:c1 - c0]), v_emptied)
                dve.wait_ge(a_emptied, mark["in2", l])
                dve.wait_ge(par_in, nth(par_in, 16))
                for t in range(TS):
                    step(tt(lft[:, t, :], u2[:, t, FL:QM], par2("b_forget"), ALU.add))
                step(v.tensor_scalar(lf[:, :, :], lft[:, :, :], 0.0, None, ALU.min))
                step(minus_abs(lft[:, :, :]), fneg_ready)
                for t in range(TS):
                    squares(tmp2[:, 0:256], u2[:, t, CQ:CKV], t)
                    squares(tmp2[:, 0:128], u2[:, t, CKV:KR], 2 + t)
                dve.wait_ge(flog_ready, nth(flog_ready))
                step(tt(lf[:, :, :], lf[:, :, :], lft[:, :, :], ALU.subtract), lf_ready)
                mod_row()
                rstd([(0, 2, 256), (2, 2, 128)])
                for t in range(TS):
                    for i, (c0, c1, g) in enumerate(((CQ, CKV, "g_q_lat"), (CKV, KR, "g_kv_lat"))):
                        x = u2[:, t, c0:c1]
                        step(v.scalar_tensor_tensor(out=x, in0=x, scalar=rs[:, 2 * i + t:2 * i + t + 1],
                                                    in1=par2(g), op0=ALU.mult, op1=ALU.mult),
                             lat_ready if t == 1 and i == 1 else v_step)
                b = filled()
                step(v.tensor_copy(Fc[:, :, :], b[:, 0:8].rearrange("p (t h) -> p t h", h=4)), v_emptied)
                mod_row()
                b = filled()
                step(v.tensor_copy(cqT[:, :, :], b[:, :].rearrange("p (k n) -> p k n", k=2)), v_emptied)
                b = filled()
                step(v.tensor_copy(ckvT, b[:, 0:S]), v_emptied)
                for t in range(TS):
                    h4 = slice(4 * t, 4 * t + 4)
                    step(v.tensor_scalar(qa[:, h4, 0:64], u2[:, t, QF:KF].rearrange("p (h c) -> p h c", h=4), 0.125,
                                         None, ALU.mult))
                    step(v.tensor_copy(ka[:, h4, 0:64], u2[:, t, KF:VF].rearrange("p (h c) -> p h c", h=4)))
                    step(v.tensor_copy(qa[:, h4, 65:66], bc(Fc[:, t, :], 2, 1)))
                    step(v.tensor_scalar(ka[:, h4, 64:65], bc(Fc[:, t, :], 2, 1), -1.0, None, ALU.mult))
                step(v.memset(qa[:, :, 64:65], 1.0))
                step(v.memset(ka[:, :, 65:66], 1.0), qa_ready)
                for t in range(TS):
                    for n in range(2):
                        b = filled()
                        step(v.tensor_copy(ql[:, t, 384 * n:384 * n + 384], b[:, 0:384]), v_emptied)
                mod_row()
                table = const("rope2").rearrange("p (t c f) -> p t c f", t=2, c=2)
                for t in range(TS):
                    q8 = ql[:, t, :].rearrange("p (h c) -> p h c", h=8)
                    t1 = tmp2[:, 0:128].rearrange("p (h f) -> p h f", f=16)
                    t2 = tmp2[:, 128:256].rearrange("p (h f) -> p h f", f=16)
                    rope(q8[:, :, 64:80], q8[:, :, 80:96], bc(table[:, t, 0, :], 1, 8), bc(table[:, t, 1, :], 1, 8),
                         t1, t2)
                    kr = u2[:, t, KR:IN2]
                    rope(kr[:, 0:16], kr[:, 16:32], table[:, t, 0, :], table[:, t, 1, :], tmp2[:, 0:16],
                         tmp2[:, 16:32])
                    k8 = kc[:, t, :].rearrange("p (h c) -> p h c", h=8)
                    step(v.tensor_copy(k8[:, :, 64:96], bc(kr, 1, 8)), heads_ready if t == 1 else v_step)
                for hp in range(2):
                    b = filled()
                    step(v.tensor_copy(qfT[0:66, 2 * hp:2 * hp + 2, :], b[0:66, :].rearrange("p (h n) -> p h n", h=2)),
                         v_emptied)
                for hp in range(4):
                    b = filled()
                    step(v.tensor_copy(qcT[0:96, 2 * hp:2 * hp + 2, :], b[0:96, :].rearrange("p (h n) -> p h n", h=2)),
                         v_emptied)
                mod_row()
                for i in range(len(UNITS2) + 2):
                    if i < len(UNITS2):
                        kind, h, q = UNITS2[i]
                        if i % 4 == 2 and i > 2:
                            mod_row()
                        n = P * (q + 1)
                        mask = (t5[:, h, :] if kind == "moba" else const("causal"))[:, S - n:S]
                        b = filled("s")
                        step(v.tensor_tensor_reduce(out=S2[:, i % 2, 0:n], in0=b[:, 0:n], in1=mask, scale=1.0,
                                                    scalar=-3.0e38, op0=ALU.add, op1=ALU.max,
                                                    accum_out=mx[:, i % 2:i % 2 + 1]), s_emptied)
                        step(v.tensor_scalar(nm[:, i % 2:i % 2 + 1], mx[:, i % 2:i % 2 + 1], -SCALE2[kind], None,
                                             ALU.mult), nm_ready)
                    if i >= 2:
                        kind, h, q = UNITS2[i - 2]
                        c0 = {"fox": 0, "moba": 256, "mla": 512}[kind] + 64 * h
                        b = filled()
                        r = rinv[:, i % 2:i % 2 + 1]
                        step(v.reciprocal(r, rsum[:, (i - 2) % 4:(i - 2) % 4 + 1]))
                        step(v.tensor_scalar(mix2[:, q, c0:c0 + 64], b[:, 0:64], r, None, ALU.mult), v_emptied)
                mod_row()
                groups = ((0, 256), (256, 512), (512, 1024))
                for g, (c0, c1) in enumerate(groups):
                    for t in range(TS):
                        squares(tmp2[:, 0:c1 - c0], mix2[:, t, c0:c1], 2 * g + t)
                rstd([(0, 4, 256), (4, 2, 512)])
                for g, (c0, c1) in enumerate(groups):
                    for t in range(TS):
                        x = mix2[:, t, c0:c1]
                        step(v.scalar_tensor_tensor(out=x, in0=x, scalar=rs[:, 2 * g + t:2 * g + t + 1],
                                                    in1=par2("g_group")[:, c0:c1], op0=ALU.mult, op1=ALU.mult),
                             mixt_ready if g == 2 and t == 1 else v_step)
                for ft in range(0, KT, 2):
                    b = filled()
                    step(v.tensor_copy(actT[:, ft, 0:S], b[:, 0:S]), v_emptied)
                mod_columns("mod2", l, 1)
                residual2(norm_tile)
                turned([0, 1])
                if l < L - 1:
                    mod_columns("mod2", l + 1, 0)
                for m in range(F2 // P):
                    dve.wait_ge(sg_ready, nth(sg_ready))
                    b = filled("s")
                    g = sg2[:, m % 2, :]
                    step(v.tensor_scalar(g, g, 1.0, None, ALU.add))
                    step(v.reciprocal(g, g))
                    step(tt(g, g, b[:, 0:S], ALU.mult))
                    step(tt(hid2[:, m, :], g, b[:, S:512], ALU.mult), s_emptied)
                residual2(norm_tile if l < L - 1 else lambda t: None)

            step(v.memset(ss[:, :], 0.0))
            dve.wait_ge(cons_in, 16 * NCONS)
            step(v.tensor_copy(t5col, bc(t5tab, 2, P)))
            dve.wait_ge(cexp_ready, 1)
            step(v.tensor_scalar(csig[:, :], csig[:, :], 1.0, None, ALU.add))
            step(v.reciprocal(csig[:, :], csig[:, :]))
            step(tt(cT[:, :, :].rearrange("p a k -> p (a k)"), cols[:, 0:24], csig[:, :], ALU.mult), cT_ready)
            for h in range(4):
                b = filled()
                step(v.tensor_scalar(t5rows[:, h, :], b[:, :], 8.0, None, ALU.mult), v_emptied)
            due = MODS[:NFIRST]
            for _ in range(NFIRST):
                mod_row()
            mod_columns("mod1", 0, 0)
            for t in range(4):
                norm_tile(t)
            for l in range(L):
                layer1(l)
            for l in range(L):
                layer2(l)

        @block.scalar
        def _(act):
            nth = counter()

            def step(ins, signal=a_step):
                ins.then_inc(signal, 1)
                act.wait_ge(signal, nth(signal))

            def filled(r="a"):
                banks, s = (AB, a_filled) if r == "a" else (SB, s_filled)
                n = nth(s)
                act.wait_ge(s, n)
                return banks[(n - 1) % len(banks)]

            def f(o, x, func, **kw):
                return nc.scalar.activation(o, x, func, **kw)

            def stored(m0, m1):
                for m in range(m0, m1):
                    act.wait_ge(row_out[m % 3], 16 * (m // 3 + 1))

            def mod_loads(n):
                stored(6 * n + 1, 6 * n + 4)
                i, part = n // 2, n % 2
                for vec in range(2):
                    src = a["mods"][i, vec, 3 * D * part:3 * D * part + 2 * D].rearrange("(k p) -> k p", p=P)
                    act.dma_start(modrow[16 * vec:16 * vec + 16, :], src).then_inc(modrow_in, 16)

            def gate_loads(n):
                stored(6 * n + 3, 6 * n + 6)
                i, part = n // 2, n % 2
                gates = a["mods"][i:i + 1, :, 3 * D * part + 2 * D:3 * D * part + 3 * D]
                act.dma_start(GA[:, 0, :], gates[:, 0, :].partition_broadcast(P)).then_inc(ga_in, 16)
                if i < L:
                    src = gates[:, 1, :]
                else:
                    src = a["g_mix_post_2" if part == 0 else "g_ffn_post_2"][i - L:i - L + 1, :]
                act.dma_start(GA[:, 1, :], src.partition_broadcast(P)).then_inc(ga_in, 16)

            def normed(tiles, n):
                for t in tiles:
                    for _ in range(2 if n == 2 * L else 1):
                        if n:
                            act.wait_ge(x_ready, nth(x_ready))
                        step(f(xn[:, t, :], X[:, t, :], ACT.Square, accum_out=ss[:, t:t + 1]), sq_ready)
                gate_loads(n)
                for ft in range(1, KT, 2):
                    b = filled()
                    for s in range(len(tiles) // 2):
                        last = s == len(tiles) // 2 - 1
                        step(f(actT[:, ft, S * s:S * s + S], b[:, S * s:S * s + S], ACT.Identity,
                               scale=modT[:, 1, ft, s:s + 1], bias=modT[:, 0, ft, s:s + 1]),
                             a_emptied if last else a_step)

            def softplus(x, out_):
                step(f(x, x, ACT.Exp))
                step(f(x, x, ACT.Ln, bias=1.0), out_)

            def layer1(l):
                n = P * len(tiles1(l))
                normed([0, 1, 2, 3], 2 * l)
                for c, t, lo, hi, r in in1_jobs(l):
                    if r == "a":
                        b = filled()
                        c0 = CH1[c][0]
                        step(f(u[:, t, c0 + lo:c0 + hi], b[:, 0:hi - lo], ACT.Copy), a_emptied)
                for t in range(4):
                    act.wait_ge(v_emptied, mark["z", l, t])
                    softplus(zt[:, t, :], zlog_ready)
                for dst, scale in ((qgT, 0.125), (kgT, 1.0)):
                    for hp in range(2):
                        b = filled()
                        step(f(dst[:, hp, 0:n], b[:, 0:n], ACT.Copy, scale=scale), a_emptied)
                b = filled()
                step(f(dec, b[:, 0:16], ACT.Exp), a_emptied)
                for t in range(4):
                    b = filled()
                    step(f(ke4[:, t, :], b[:, :], ACT.Exp), a_emptied)
                for t in tiles1(l):
                    b = filled()
                    step(f(bT[:, :, :], b[:, :].rearrange("p (j n) -> p j n", j=4), ACT.Copy), a_emptied)
                    act.wait_ge(exps_in, nth(exps_in))
                    step(f(qk96, qk96, ACT.Exp))
                    step(f(kd[:, :, :], qd[:, :, :], ACT.Exp, scale=-1.0))
                    step(f(qd[:, :, :], qd[:, :, :], ACT.Exp))
                    step(f(qi[:, :, :], bT[:, :, :], ACT.Exp), exps_out)
                    act.wait_ge(qk_ready, nth(qk_ready))
                step(f(gexp[:, 0:len(tiles1(l)), :], u[:, 0:len(tiles1(l)), GG:RF], ACT.Exp, scale=-1.0), gexp_ready)
                for g in range(2):
                    b = filled()
                    step(f(mT[:, g, 0:n], b[:, 0:n], ACT.Copy), a_emptied)
                for sem_ in (s_filled, s_emptied):
                    nth(sem_, 2 * len(tiles1(l)))
                for j in (1, 3):
                    b = filled()
                    step(f(qT[:, j, 0:n], b[:, 0:n], ACT.Copy), a_emptied)
                units = units1(l)
                for i in range(len(units) + 1):
                    if i < len(units):
                        k0 = units[i][2]
                        act.wait_ge(nm_ready, nth(nm_ready))
                        b = filled("s")
                        step(f(Pr[:, i % 2, 0:512 - k0], b[:, 0:512 - k0], ACT.Exp, bias=nm[:, i % 2:i % 2 + 1],
                               scale=0.125, accum_out=rsum[:, i % 4:i % 4 + 1]), s_emptied)
                    if i >= 1:
                        k0 = units[i - 1][2]
                        b = filled()
                        step(f(PT[:, (i - 1) % 2, 0:512 - k0], b[:, 0:512 - k0], ACT.Copy), a_emptied)
                for j in (1, 3, 5):
                    b = filled()
                    step(f(actT[:, 2 + j, 0:n], b[:, 0:n], ACT.Copy), a_emptied)
                mod_loads(2 * l + 1)
                if l == L - 1:
                    act.dma_start(gf, a["g_final"].partition_broadcast(P)).then_inc(gf_in, 16)
                normed(tiles1(l), 2 * l + 1)
                mod_loads(2 * l + 2)
                for m in range(1, F1 // P, 2):
                    b = filled()
                    step(f(hid[:, m, 0:n], b[:, 0:n], ACT.Relu), a_emptied)
                    step(f(hid[:, m, 0:n], hid[:, m, 0:n], ACT.Square), hid_ready)

            def layer2(l):
                normed([0, 1], 2 * (L + l))
                for c, (c0, c1) in enumerate(CH2):
                    b = filled()
                    step(f(u2[:, 1, c0:c1], b[:, 0:c1 - c0], ACT.Copy), a_emptied)
                for dst in (qmT, kmT):
                    b = filled()
                    step(f(dst[:, :, :], b[:, :].rearrange("p (h n) -> p h n", h=2), ACT.Copy), a_emptied)
                act.wait_ge(fneg_ready, nth(fneg_ready))
                softplus(lft[:, :, :], flog_ready)
                for t in range(TS):
                    for n in range(2):
                        b = filled()
                        kv = b[:, :].rearrange("p (h e c) -> p h e c", h=4, e=2)
                        k8 = kc[:, t, :].rearrange("p (h c) -> p h c", h=8)
                        step(f(k8[:, 4 * n:4 * n + 4, 0:64], kv[:, :, 0, :], ACT.Copy))
                        step(f(vv[:, t, 256 * n:256 * n + 256].rearrange("p (h c) -> p h c", h=4), kv[:, :, 1, :],
                               ACT.Copy), a_emptied)
                for hp in range(2):
                    b = filled()
                    step(f(kfT[0:66, 2 * hp:2 * hp + 2, :], b[0:66, :].rearrange("p (h n) -> p h n", h=2), ACT.Copy),
                         a_emptied)
                for hp in range(4):
                    b = filled()
                    step(f(kcT[0:96, 2 * hp:2 * hp + 2, :], b[0:96, :].rearrange("p (h n) -> p h n", h=2), ACT.Copy),
                         a_emptied)
                for i in range(len(UNITS2) + 1):
                    if i < len(UNITS2):
                        kind, h, q = UNITS2[i]
                        n = P * (q + 1)
                        act.wait_ge(nm_ready, nth(nm_ready))
                        step(f(P2[:, i % 2, 0:n], S2[:, i % 2, 0:n], ACT.Exp, bias=nm[:, i % 2:i % 2 + 1],
                               scale=SCALE2[kind], accum_out=rsum[:, i % 4:i % 4 + 1]), p2_ready)
                    if i >= 1:
                        n = P * (UNITS2[i - 1][2] + 1)
                        b = filled()
                        step(f(PT2[:, (i - 1) % 2, 0:n], b[:, 0:n], ACT.Copy), a_emptied)
                for ft in range(1, KT, 2):
                    b = filled()
                    step(f(actT[:, ft, 0:S], b[:, 0:S], ACT.Copy), a_emptied)
                nth(s_filled, len(UNITS2))
                mod_loads(2 * (L + l) + 1)
                normed([0, 1], 2 * (L + l) + 1)
                if l < L - 1:
                    mod_loads(2 * (L + l) + 2)
                for m in range(F2 // P):
                    b = filled("s")
                    step(f(sg2[:, m % 2, :], b[:, 0:S], ACT.Exp, scale=-1.0), sg_ready)

            act.dma_start(cons[:, :], a["cons"]).then_inc(cons_in, 16)
            act.dma_start(cols[:, :], a["cols"]).then_inc(cons_in, 16)
            act.dma_start(t5tab, a["t5_table_2"]).then_inc(cons_in, 16)
            act.dma_start(t5hot, a["t5hot"]).then_inc(cons_in, 16)
            act.dma_start(X[:, 0:2, :], a["x"][0].rearrange("(t p) d -> p t d", p=P)).then_inc(x_in, 16)
            act.dma_start(X[:, 2:4, :], a["ctx"][0].rearrange("(t p) d -> p t d", p=P)).then_inc(x_in, 16)
            act.wait_ge(cons_in, 16 * NCONS)
            step(f(csig[:, :], cols[:, 0:24], ACT.Exp, scale=-1.0), cexp_ready)
            act.wait_ge(x_in, 32)
            act.wait_ge(cT_ready, 1)
            mod_loads(0)
            for l in range(L):
                layer1(l)
            for l in range(L):
                layer2(l)

        @block.gpsimd
        def _(pool):
            nc.gpsimd.memset(neghalf[:, :], -0.5).then_inc(pool_ready, 1)
            pool.wait_ge(v_emptied, 4)
            pool.dma_start(a["t5_rows"], t5rows).then_inc(t5_stored, 16)
            pool.wait_ge(t5_stored, 16)
            band_src = bass.AP(tensor=a["t5_rows"].tensor, offset=P - 1, ap=[[4 * 512 - 1, P], [512, 4], [1, S]])
            pool.dma_start(t5[:, :, :], band_src).then_inc(t5_in, 16)
            pool.wait_ge(pool_ready, 1)
            for i, (at, n) in enumerate(powers):
                pool.wait_ge(ms_ready, i + 1)
                nc.gpsimd.tensor_tensor(rs[:, at:at + n], ms[:, at:at + n], neghalf[:, at:at + n], ALU.pow)\
                  .then_inc(rstd_ready, 1)


def bucket(dist):
    n = np.maximum(dist, 0)
    nf = np.maximum(n, 16).astype(np.float32)
    large = 16 + (np.log(nf / np.float32(16)) / np.float32(math.log(8)) * np.float32(16)).astype(np.int32)
    return np.where(n < 16, n, np.minimum(large, 31))


def constants():
    i = np.arange(P)
    t, j = i[:, None], i[None, :]
    out = {}
    out["ident"] = t == j
    out["up16"] = (t <= j) / 16.0
    out["lo16"] = (t >= j) / 16.0
    out["after16"] = (t > j) / 16.0
    out["before16"] = (t < j) / 16.0
    out["up"] = t <= j
    out["ones"] = np.ones((P, P))
    out["mask_f"] = (t // 32 != j // 32) | (t <= j)
    out["mask_b"] = (t % 32) > np.arange(32)[None, :]
    out["causal"] = np.concatenate([np.zeros((P, P)), np.where(j <= t, 0.0, NEG)], 1)
    inv1 = np.float32(10000.0) ** (-np.arange(0, 32, 2, dtype=np.float32) / np.float32(32))
    tok = np.arange(S)
    axes = np.stack([tok // 64, tok % 64], 1).astype(np.float32)
    ang = axes[:, :, None] * inv1
    r1 = np.stack([np.cos(ang), np.sin(ang)], 1)
    out["rope1"] = r1.reshape(TS, P, 64).transpose(1, 0, 2).reshape(P, 128)
    inv2 = np.float32(1.0) / (np.float32(10000.0) ** (np.arange(16, dtype=np.float32) / np.float32(16)))
    ang = tok.astype(np.float32)[:, None] * inv2
    r2 = np.stack([np.cos(ang), np.sin(ang)], 1)
    out["rope2"] = r2.reshape(TS, P, 32).transpose(1, 0, 2).reshape(P, 64)
    sel = np.zeros((P, 2, P))
    sel[0, 0] = 1
    sel[1, 1] = 1
    out["sel"] = sel.reshape(P, 256)
    cons = np.concatenate([out[n].astype(np.float32) for n, _ in CONST], 1)
    hot = np.zeros((32, 512), np.float32)
    e = np.arange(256)
    hot[bucket(255 - e), e] = 1
    band = np.zeros((4, S, S), np.float32)
    for g, w in enumerate((2, 4, 8, 16)):
        lo, hi = np.clip(tok - w // 2, 0, S - 1), np.clip(tok + w // 2 - 1, 0, S - 1)
        inside = (tok[:, None] >= lo[None, :]) & (tok[:, None] <= hi[None, :])
        band[g] = inside / (hi - lo + 1)[None, :].astype(np.float32) - np.eye(S)
    band = band.reshape(4, TS, P, S).transpose(2, 1, 0, 3).reshape(P, 2048)
    return cons, hot, band


def kernel(**inputs):
    import concourse.bacc as _bacc
    from concourse import mybir as _mybir
    from concourse.bass_utils import run_bass_kernel_spmd as _run

    x = {k: np.ascontiguousarray(v) for k, v in inputs.items()}
    cons, hot, band = constants()

    def columns(w):
        return w.reshape(-1, P).T

    cols = np.concatenate([columns(x[n]) for n in ("c", "c_ctx", "c_2", "g_mix", "g_mlp", "g_mix_pre_2",
                                                   "g_ffn_pre_2", "s_pool")], 1)
    par1 = np.zeros((L, P, sum(n for _, n in PAR1)), np.float32)
    par2 = np.zeros((L, P, sum(n for _, n in PAR2)), np.float32)
    at1, at2 = offsets(PAR1)[0], offsets(PAR2)[0]

    def put(dst, at, name, value):
        s, n = at[name]
        dst[:, s:s + n] = value

    for l in range(L):
        put(par1[l], at1, "band", band)
        wg = np.zeros((P, 512), np.float32)
        wg[0:16, 0:256], wg[16:32, 256:512] = x["w_gate"][l, 0], x["w_gate"][l, 1]
        wg[32, 0:256], wg[32, 256:512] = x["b_gate"][l, 0], x["b_gate"][l, 1]
        put(par1[l], at1, "wg", wg)
        wp = np.zeros((P, 2, P), np.float32)
        for g in range(4):
            o = 64 * (g % 2)
            wp[o:o + 64, g // 2, o:o + 64] = x["w_pool"][l, g]
        put(par1[l], at1, "wpool", wp.reshape(P, 256))
        for n in ("g_q", "g_k", "g_gla"):
            put(par1[l], at1, n, x[n][l][None, :])
        put(par2[l], at2, "w_uq", x["w_uq_2"][l].reshape(2, P, 768).transpose(1, 0, 2).reshape(P, 1536))
        put(par2[l], at2, "w_ukv", x["w_ukv_2"][l])
        for n in ("g_q_lat", "g_kv_lat", "g_group", "b_forget"):
            put(par2[l], at2, n, x[n + "_2"][l][None, :])
    arrays = {"cons": cons, "cols": cols, "t5hot": hot, "par1": par1, "par2": par2}
    for n in ("x", "ctx", "w_mod", "b_mod", "w_in", "w_out", "w_up", "w_down", "g_final", "t5_table_2", "w_ada_2",
              "b_ada_2", "g_mix_post_2", "w_in_2", "w_out_2", "g_ffn_post_2", "w_gate_up_2", "w_down_2"):
        arrays[n] = x[n]
    arrays["g_final"] = x["g_final"].reshape(1, D)

    nc = _bacc.Bacc("TRN2", target_bir_lowering=False, num_devices=1)
    feed, aps = {}, {}
    for n, v in arrays.items():
        v = np.ascontiguousarray(v)
        feed[f"in_{n}"] = v
        aps[n] = nc.dram_tensor(f"in_{n}", v.shape, _mybir.dt.from_np(v.dtype), kind="ExternalInput").ap()
    aps["mods"] = nc.dram_tensor("mods", [2 * L, 2, 6 * D], _mybir.dt.float32, kind="Internal").ap()
    aps["t5_rows"] = nc.dram_tensor("t5_rows", [P, 4, 512], _mybir.dt.float32, kind="Internal").ap()
    out = nc.dram_tensor("out", (1, S, D), _mybir.dt.float32, kind="ExternalOutput").ap()
    trunks(nc, aps, out)
    r = _run(nc, [feed], core_ids=[0])
    return r.results[0]["out"]
```

```python
import math
import numpy as np
import concourse.bass as bass
from concourse import mybir
from contextlib import ExitStack

D = 1024
P = 128
KT = D // P
L = 2
S = 256
TS = S // P
MODC = 512
F1 = 4096
F2 = 2816
IN1 = 2080
IN2 = 1956
EPS = 1e-6
NEG = -1.0e30
GQ, GK, GV, GG, RF, AQ, AK, AV = 256, 512, 768, 1024, 1280, 1312, 1824, 1952
CH1 = [(0, 512), (512, 1024), (1024, 1312), (1312, 1824), (1824, 2080)]
QF, KF, VF, FL, QM, KM, VM, CQ, CKV, KR = 0, 256, 512, 768, 772, 1028, 1284, 1540, 1796, 1924
CH2 = [(0, 490), (490, 980), (980, 1468), (1468, 1956)]
PAR1 = [("band", 2048), ("wg", 512), ("wpool", 256), ("g_q", 64), ("g_k", 64), ("g_gla", 64)]
PAR2 = [("w_uq", 1536), ("w_ukv", 1024), ("g_q_lat", 256), ("g_kv_lat", 128), ("g_group", 1024), ("b_forget", 4)]
CONST = [("ident", 128), ("up16", 128), ("lo16", 128), ("after16", 128), ("before16", 128), ("up", 128),
         ("ones", 128), ("mask_f", 128), ("mask_b", 32), ("causal", 256), ("rope1", 128), ("rope2", 64)]
NCONS = 4
NSLOT = 3
SLOT = 4096
ARENA = 20608
WHI = ARENA - 2 * SLOT
HC2 = [(0, 8), (8, 15), (15, 22)]


def offsets(table):
    at, out = 0, {}
    for name, n in table:
        out[name] = (at, n)
        at += n
    return out, at


MODS = [("mod1", l, k) for l in range(L) for k in range(12)] + [("mod2", l, k) for l in range(L) for k in range(12)]
NFIRST = 6


def loads():
    out, mods = MODS[:NFIRST], MODS[NFIRST:]
    for n in (1, 2):
        for l in range(L):
            out += [(f"in{n}", l, c) for c in range(len((CH1, CH2)[n - 1]))]
            out += [(f"par{n}", l, 0)]
            out += mods[:12]
            mods = mods[12:]
            out += [(f"out{n}", l, h) for h in range(2)]
            if n == 1:
                for q in range(4):
                    out += [("up1", l, 2 * q + i) for i in range(2)] + [("down1", l, 2 * q + i) for i in range(2)]
            else:
                out += [("up2", l, c) for c in range(F2 // 256)]
                out += [("down2", l, c) for c in range(2 * len(HC2))]
    return out


LOADS = loads()
PLACE = {key: i for i, key in enumerate(key for key in LOADS if key[0][:3] != "par")}


def landed():
    at, out = [0] * NSLOT, {}
    for key, i in PLACE.items():
        at[i % NSLOT] += 32 if key[0] == "up2" else 16
        out[key] = at[i % NSLOT]
    return out


LANDED = landed()
SPLITS = [key for key in PLACE if key not in MODS]




def share(key):
    if key[0] == "out2" and key[2] == 0:
        return 0
    return 4 if key[0] == "up2" or key[0] == "out1" and key[2] == 0 else 8


V_SPLITS = [key for key in SPLITS if share(key) > 0]
P_SPLITS = [key for key in SPLITS if share(key) < 8]


def in1_jobs(l):
    out = []
    for c, (c0, c1) in enumerate(CH1):
        for t in range(4):
            lo, hi = 0, c1 - c0
            if l == L - 1 and t >= 2:
                if c in (0, 3):
                    continue
                if c == 2:
                    lo = RF - c0
            out.append((c, t, lo, hi, "va"[len(out) % 2]))
    return out


def units1(l):
    return [(2 * s + q, h, 256 * s) for s in range(2 if l < L - 1 else 1) for q in range(TS) for h in range(8)]


UNITS2 = [(kind, h, q) for q in range(TS) for kind, n in (("fox", 4), ("moba", 4), ("mla", 8)) for h in range(n)]
STATES = [((2, 3), (3, 2)), ((3, 0), (2, 1)), ((0, 1), (1, 0))]


SCALE2 = {"fox": 1.0, "moba": 0.125, "mla": 96.0 ** -0.5}


def counter():
    seen = {}

    def nth(sem, k=1):
        seen[sem.name] = seen.get(sem.name, 0) + k
        return seen[sem.name]
    return nth


def trunks(nc, a, out):
    f32 = mybir.dt.float32
    f32r = mybir.dt.float32r
    ALU = mybir.AluOpType
    ACT = mybir.ActivationFunctionType
    X_AXIS = mybir.AxisListType.X
    ctx = ExitStack()
    with ctx:
        def sb(name, shape):
            return ctx.enter_context(nc.sbuf_tensor(name, shape, f32))

        def sem(name):
            return ctx.enter_context(nc.semaphore(name))

        base = -(-nc.sbuf_base // 32) * 32
        actT = sb("actT", [P, KT, 512])
        ring = sb("ring", [P, NSLOT, SLOT])
        arena = sb("arena", [P, ARENA])
        actT_r = nc.alloc_sbuf_tensor_at("actT_r", [P, KT, 512], f32r, offset=base)
        ring_r = nc.alloc_sbuf_tensor_at("ring_r", [P, NSLOT, SLOT], f32r, offset=base + 4 * KT * 512)
        arena_r = nc.alloc_sbuf_tensor_at("arena_r", [P, ARENA], f32r, offset=base + 4 * (KT * 512 + NSLOT * SLOT))
        X = sb("X", [P, 4, D])
        params = sb("params", [P, 3972])
        GA = sb("GA", [P, 2, D])
        cons_at, cons_n = offsets(CONST)
        cons = sb("cons", [P, cons_n])
        cols = sb("cols", [P, 92])
        csig = sb("csig", [P, 24])
        cT = sb("cT", [P, 3, KT])
        row = sb("row", [2, 3, MODC])
        modrow = sb("modrow", [32, P])
        modT = sb("modT", [P, 2, KT, 2])
        t5 = sb("t5", [P, 4, S])
        post = GA[:, 1, :]
        ms = sb("ms", [P, 64])
        rs = sb("rs", [P, 64])
        neghalf = sb("neghalf", [P, 64])
        ss = sb("ss", [P, 48])
        rsum = sb("rsum", [P, 4])
        mx = sb("mx", [P, 2])
        nm = sb("nm", [P, 2])
        rinv = sb("rinv", [P, 2])

        def const(name):
            at, n = cons_at[name]
            return cons[:, at:at + n]

        ident = const("ident")
        ones = const("ones")
        gcol = cols[:, 24:88].rearrange("p (w l k) -> p w l k", w=4, l=2)
        spool = cols[:, 88:92].rearrange("p (l g) -> p l g", l=2)

        def carve(start, *shape, buf=arena):
            n = int(np.prod(shape))
            v = buf[:, start:start + n]
            assert start + n <= ARENA, (start, shape)
            if len(shape) == 2:
                v = v.rearrange("p (a b) -> p a b", a=shape[0])
            elif len(shape) == 3:
                v = v.rearrange("p (a b c) -> p a b c", a=shape[0], b=shape[1])
            return v

        xn = carve(0, 4, D)
        u = carve(0, 4, IN1)
        mixt = carve(8320, 4, 768)
        la = carve(11392, 4, 512)
        qgT = carve(13440, 2, 512)
        kgT = carve(14464, 2, 512)
        zt = carve(15488, 4, 512)
        ke4 = carve(15488, 4, 512)
        bT = carve(15488, 4, P)
        qk64 = carve(16000, 4, P)
        qk32 = carve(16512, 4, P)
        qk96 = carve(16000, 1024)
        qd = carve(17024, 4, P)
        kd = carve(17536, 4, P)
        qi = carve(18048, 4, P)
        AT = carve(18560, 4, P)
        rT = arena[0:33, 18560:19072]
        St = carve(19072, 4, 256)
        atb = carve(20096, 4, 32)
        dec = carve(20224, 16)
        gsq = carve(13440, 4, 256)
        gexp = carve(14464, 4, 256)
        qT = carve(11392, 4, 512)
        kT = carve(13440, 2, 512)
        Pr = carve(14464, 2, 512)
        PT = carve(15488, 2, 512)
        mT = carve(16512, 2, 512)
        kdup = mixt[:, :, 512:768]
        sqq = mixt[:, 0:2, 256:512]
        sqk = mixt[:, 2, 256:384]
        plo = carve(17536, 2, 512)
        hid_hi = carve(0, 4, KT, P, buf=arena_r)
        hid_lo, hid_lo_r = carve(4096, 4, KT, P), carve(4096, 4, KT, P, buf=arena_r)
        act_lo, act_lo_r = carve(8320, KT, 512), carve(8320, KT, 512, buf=arena_r)
        mix_lo, mix_lo_r = carve(4096, KT, 512), carve(4096, KT, 512, buf=arena_r)
        act2_lo, act2_lo_r = actT[:, :, S:2 * S], actT_r[:, :, S:2 * S]
        tmpx = params[:, 0:1024].rearrange("p (a n) -> p a n", a=2)
        u2 = carve(0, 2, IN2)
        y2 = params[:, 0:2048].rearrange("p (t n) -> p t n", t=2)
        qa = carve(3912, 8, 66)
        ka = carve(4440, 8, 66)
        qfT = carve(4968, 4, S)
        kfT = carve(5992, 4, S)
        qmT = carve(7016, 2, S)
        kmT = carve(7528, 2, S)
        cqT = carve(8040, 2, S)
        ckvT = carve(8552, S)
        ql = carve(8808, 2, 768)
        kc = carve(10344, 2, 768)
        vv = carve(11880, 2, 512)
        qcT = carve(12904, 8, S)
        kcT = carve(14952, 8, S)
        S2 = carve(17000, 2, S)
        P2 = carve(17512, 2, S)
        PT2 = carve(18024, 2, S)
        mix2 = carve(8808, 2, D)
        Fc = carve(18536, 2, 4)
        lf = carve(18544, 2, 4)
        lft = carve(18552, 2, 4)
        tmp2 = carve(18560, 1920)
        hid2_hi = carve(0, 22, S, buf=arena_r)
        hid2_lo, hid2_lo_r = carve(5632, 22, S), carve(5632, 22, S, buf=arena_r)
        sg2 = params[:, 2048:2560].rearrange("p (a n) -> p a n", a=2)
        junk2 = params[:, 2560:3072]

        bank = [ctx.enter_context(nc.psum_tensor(f"bank{i}", [P, 512], f32)) for i in range(8)]
        VB, AB, SB, MB = bank[0:2], (bank[2], bank[4]), bank[5:7], (bank[3], bank[7])

        names = """cons_in slot_read par_in ga_in modrow_in m_filled t5_stored t5_in out_stored
            v_filled v_emptied a_filled a_emptied s_filled s_emptied v_step a_step
            ms_ready rstd_ready pool_ready cexp_ready cT_ready row_ready
            x_in gf_in x_ready sq_ready xn_ready zlog_ready la_ready exps_in exps_out qk_ready
            ke_ready AT_ready gexp_ready aq_ready nm_ready mixt_ready hid_ready hsq_ready whi_ready w_ready wp_ready acth_ready act_ready actp_ready
            fneg_ready flog_ready lf_ready qa_ready lat_ready heads_ready p2_ready sg_ready""".split()
        (cons_in, slot_read, par_in, ga_in, modrow_in, m_filled, t5_stored, t5_in, out_stored,
         v_filled, v_emptied, a_filled, a_emptied, s_filled, s_emptied, v_step, a_step,
         ms_ready, rstd_ready, pool_ready, cexp_ready, cT_ready, row_ready,
         x_in, gf_in, x_ready, sq_ready, xn_ready, zlog_ready, la_ready, exps_in, exps_out, qk_ready,
         ke_ready, AT_ready, gexp_ready, aq_ready, nm_ready, mixt_ready, hid_ready, hsq_ready,
         whi_ready, w_ready, wp_ready, acth_ready, act_ready, actp_ready,
         fneg_ready, flog_ready, lf_ready, qa_ready, lat_ready, heads_ready,
         p2_ready, sg_ready) = [sem(n) for n in names]
        slot_in = [sem(f"slot_in{i}") for i in range(NSLOT)]
        row_in = [sem(f"row_in{i}") for i in range(3)]
        row_out = [sem(f"row_out{i}") for i in range(3)]
        p1at, p1n = offsets(PAR1)
        p2at, p2n = offsets(PAR2)

        def slot(key):
            return ring[:, PLACE[key] % NSLOT, :]

        def normal(n):
            return xn if n <= 2 * L else y2

        def extent(buf, key):
            kind, l, c = key
            k_, n = KT, MODC
            if kind in ("in1", "in2"):
                c0, c1 = (CH1, CH2)[kind == "in2"][c]
                n = c1 - c0
            elif kind == "down2":
                k_ = HC2[c % 3][1] - HC2[c % 3][0]
            return buf.rearrange("p (k n) -> p k n", n=MODC)[:, 0:k_, 0:n]

        def upper(key):
            if key[0] == "out1" and key[2] == 0:
                at = 0
            else:
                at = WHI + SLOT * (SPLITS.index(key) % 2)
            return extent(arena_r[:, at:at + SLOT], key)

        def lower(key):
            return extent(ring_r[:, PLACE[key] % NSLOT, :], key)

        def after(key):
            i = SPLITS.index(key) + 1
            return [] if i == len(SPLITS) or key[0][:2] == "in" and SPLITS[i][0][:3] == "out" else [SPLITS[i]]

        def slot_wait(eng, key):
            eng.wait_ge(slot_in[PLACE[key] % NSLOT], LANDED[key])

        def par(at, name):
            s, n = at[name]
            return params[:, s:s + n]

        def par1(name):
            return par(p1at, name)

        def par2(name):
            return par(p2at, name)

        def bc(ap, at, n):
            ap = ap.unsqueeze(at)
            shape = list(ap.shape)
            shape[at] = n
            return ap.broadcast_to(shape)

        t5hot = arena[0:32, 18560:19072]
        t5tab = arena[0:32, 19072:19076]
        t5col = arena[0:32, 11264:11776].rearrange("p (h n) -> p h n", h=4)
        t5rows = carve(9216, 4, 512)
        gf = params[:, 1024:2048]
        mark = {}
        handed = []

        def tiles1(l):
            return [0, 1, 2, 3] if l < L - 1 else [0, 1]

        def updates(kind, l):
            if kind == "par1":
                return sum(2 * len(tiles1(i)) for i in range(l))
            return updates("par1", L) + TS + 2 * TS * l

        block = ctx.enter_context(nc.Block())

        @block.sync
        def _(sp):
            def bias_row(m):
                if m < len(MODS):
                    if m >= 3:
                        sp.wait_ge(row_out[m % 3], 16 * (m // 3))
                    kind, l, c = MODS[m]
                    bias = a["b_mod"] if kind == "mod1" else a["b_ada_2"]
                    src = bias[l:l + 1, c * MODC:(c + 1) * MODC]
                    sp.dma_start(row[0:2, m % 3, :], src.partition_broadcast(2)).then_inc(row_in[m % 3], 16)

            def store_row(m):
                sp.wait_ge(row_ready, m + 1)
                kind, l, c = MODS[m]
                dst = a["mods"][2 * (kind == "mod2") + l, :, c * MODC:(c + 1) * MODC]
                sp.dma_start(dst, row[0:2, m % 3, :]).then_inc(row_out[m % 3], 16)

            for m in range(3):
                bias_row(m)
            stored = 0
            order = list(PLACE)
            for key in LOADS:
                kind, l, c = key
                if kind[:3] == "par":
                    if kind == "par2" or l > 0:
                        sp.wait_ge(x_ready, updates(kind, l))
                    w, n = (a["par1"], p1n) if kind == "par1" else (a["par2"], p2n)
                    sp.dma_start(params[:, 0:n], w[l]).then_inc(par_in, 16)
                    continue
                i = PLACE[key]
                dst = ring[:, i % NSLOT, :]
                if i >= NSLOT:
                    before = order[i - NSLOT]
                    if before in MODS:
                        sp.wait_ge(m_filled, MODS.index(before) + 1)
                    else:
                        sp.wait_ge(slot_read, sum(x not in MODS for x in order[:i - NSLOT + 1]))
                full = dst.rearrange("p (k n) -> p k n", n=MODC)
                if kind in ("mod1", "mod2"):
                    w = a["w_mod"] if kind == "mod1" else a["w_ada_2"]
                    src = w[l, :, c * MODC:(c + 1) * MODC].rearrange("(k p) n -> p k n", p=P)
                    sp.dma_start(full, src).then_inc(slot_in[i % NSLOT], 16)
                elif kind in ("in1", "in2"):
                    c0, c1 = CH1[c] if kind == "in1" else CH2[c]
                    w = a["w_in"] if kind == "in1" else a["w_in_2"]
                    src = w[l, :, c0:c1].rearrange("(k p) n -> p k n", p=P)
                    sp.dma_start(full[:, :, 0:c1 - c0], src).then_inc(slot_in[i % NSLOT], 16)
                elif kind in ("out1", "out2"):
                    w = a["w_out"] if kind == "out1" else a["w_out_2"]
                    src = w[l, :, c * MODC:(c + 1) * MODC].rearrange("(k p) n -> p k n", p=P)
                    sp.dma_start(full, src).then_inc(slot_in[i % NSLOT], 16)
                elif kind == "up1":
                    src = a["w_up"][l, :, c * MODC:(c + 1) * MODC].rearrange("(k p) n -> p k n", p=P)
                    sp.dma_start(full, src).then_inc(slot_in[i % NSLOT], 16)
                elif kind == "up2":
                    src = a["w_gate_up_2"][l].rearrange("(k p) (g n) -> p k g n", p=P, g=2)
                    for g in range(2):
                        sp.dma_start(full[:, :, g * 256:(g + 1) * 256],
                                     src[:, :, g, c * 256:(c + 1) * 256]).then_inc(slot_in[i % NSLOT], 16)
                elif kind == "down1":
                    kc_, half = c // 2, c % 2
                    src = a["w_down"][l, kc_ * D:(kc_ + 1) * D, half * MODC:(half + 1) * MODC]
                    sp.dma_start(full, src.rearrange("(k p) n -> p k n", p=P)).then_inc(slot_in[i % NSLOT], 16)
                elif kind == "down2":
                    half, (k0, k1) = c // 3, HC2[c % 3]
                    src = a["w_down_2"][l, k0 * P:k1 * P, half * MODC:(half + 1) * MODC]
                    sp.dma_start(full[:, 0:k1 - k0, :], src.rearrange("(k p) n -> p k n", p=P))\
                      .then_inc(slot_in[i % NSLOT], 16)
                while stored < len(MODS) and PLACE[MODS[stored]] <= i - NSLOT:
                    if stored >= 1:
                        bias_row(stored + 2)
                    store_row(stored)
                    stored += 1
            sp.wait_ge(x_ready, updates("par2", L))
            sp.dma_start(out[0].rearrange("(t p) d -> p t d", p=P), X[:, 0:2, :]).then_inc(out_stored, 16)
            sp.wait_ge(out_stored, 16)

        @block.tensor
        def _(pe):
            nth = counter()
            k = {"v": 0, "a": 0, "s": 0, "unread": 0, "open": 0, "turned": 0}
            rings = {"v": (VB, v_filled, v_emptied), "a": (AB, a_filled, a_emptied), "s": (SB, s_filled, s_emptied)}

            def take(r):
                banks, filled, emptied = rings[r]
                if k[r] >= len(banks):
                    pe.wait_ge(emptied, k[r] - len(banks) + 1)
                k[r] += 1
                return banks[(k[r] - 1) % len(banks)], filled

            def emptied(r):
                if k[r]:
                    pe.wait_ge(rings[r][2], k[r])

            def mm(out_, lhsT, rhs, start=True, stop=True, inc=None):
                ins = nc.tensor.matmul(out_, lhsT, rhs, start=start, stop=stop)
                if inc is not None:
                    ins.then_inc(inc, 1)
                elif k["unread"]:
                    ins.then_inc(slot_read, 1)
                    k["unread"] -= 1

            def tr(out_, in_, inc=None):
                n = in_.shape[0]
                ins = nc.tensor.transpose(out_, in_, ident[0:n, 0:n])
                if inc is not None:
                    ins.then_inc(inc, 1)
                elif k["unread"]:
                    ins.then_inc(slot_read, 1)
                    k["unread"] -= 1

            def through():
                k["unread"] += k["open"]
                k["open"] = 0

            def weights(key):
                through()
                if key in V_SPLITS:
                    pe.wait_ge(w_ready, V_SPLITS.index(key) + 1)
                if key in P_SPLITS:
                    pe.wait_ge(wp_ready, P_SPLITS.index(key) + 1)
                k["open"] = 1
                return upper(key), lower(key)

            def three(out_, lhs, rhs, first, last, inc=None):
                mm(out_, lhs[0], rhs[0], first, False)
                mm(out_, lhs[0], rhs[1], False, False)
                mm(out_, lhs[1], rhs[0], False, last, inc)

            def linear(out_, lhs, rhs, inc, order=range(KT)):
                for i in order:
                    if k["turned"]:
                        who = actp_ready if i % 2 else act_ready
                        pe.wait_ge(who, nth(who))
                        k["turned"] -= 1
                    three(out_, lhs(i), rhs(i), i == order[0], i == order[-1], inc if i == order[-1] else None)

            def contract(out_, lhs, rhs, inc, n=KT):
                for i in range(n):
                    mm(out_, lhs(i), rhs(i), i == 0, i == n - 1, inc if i == n - 1 else None)

            def fill():
                if not due:
                    return
                key = due.pop(0)
                n = MODS.index(key)
                v0, m = (0, 2) if key[0] == "mod1" else (2, 1)
                through()
                slot_wait(pe, key)
                w = slot(key).rearrange("p (k n) -> p k n", n=MODC)
                if n >= 2:
                    pe.wait_ge(row_ready, n - 1)
                contract(MB[n % 2][0:m, :], lambda i: cT[:, v0:v0 + m, i], lambda i: w[:, i, :], m_filled)

            def mod_columns():
                pe.wait_ge(modrow_in, nth(modrow_in, 32))
                b, filled = take("v")
                tr(b[:, 0:32], modrow[:, :], filled)

            def turn(tiles, width, src):
                for ft in range(KT):
                    b, filled = take("va"[ft % 2])
                    for n, t in enumerate(tiles):
                        tr(b[:, n * P:(n + 1) * P], src(ft, t), filled if n == len(tiles) - 1 else None)

            def normed(tiles, n):
                pe.wait_ge(xn_ready, nth(xn_ready, len(tiles)))
                turn(tiles, 512, lambda ft, t: normal(n)[:, t, ft * P:(ft + 1) * P])
                k["turned"] = KT

            def gla(l):
                pe.wait_ge(par_in, nth(par_in, 16))
                b, filled = take("v")
                for t in range(4):
                    tr(b[0:32, t * P:(t + 1) * P], u[:, t, RF:RF + 32], filled if t == 3 else None)
                emptied("v")
                for t in range(4):
                    b, filled = take("v")
                    mm(b[:, :], rT[:, t * P:(t + 1) * P], par1("wg")[0:33, :], inc=filled)
                    mark["z", l, t] = k["v"]
                for col, tiles in ((GQ, tiles1(l)), (GK, tiles1(l))):
                    for hp in range(2):
                        b, filled = take("a")
                        for n, t in enumerate(tiles):
                            tr(b[:, t * P:(t + 1) * P], u[:, t, col + P * hp:col + P * (hp + 1)],
                               filled if n == len(tiles) - 1 else None)
                fill()
                pe.wait_ge(la_ready, nth(la_ready))
                b, filled = take("a")
                for t in range(4):
                    for j in range(4):
                        mm(b[:, 4 * t + j:4 * t + j + 1], la[:, t, j * P:(j + 1) * P], const("up16")[:, P - 1:P],
                           inc=filled if t == 3 and j == 3 else None)
                for t in range(4):
                    b, filled = take("a")
                    mm(b[:, 0:256], const("after16"), la[:, t, 0:256])
                    mm(b[:, 256:512], const("before16"), la[:, t, 256:512], inc=filled)
                mark["dec", l] = k["a"] - 4
                fill()
                pe.wait_ge(ke_ready, nth(ke_ready))
                for pair in STATES:
                    for d, (t, _) in enumerate(pair):
                        b, filled = take("v")
                        for h in range(4):
                            mm(b[64 * (h % 2):64 * (h % 2) + 64, 64 * (h // 2):64 * (h // 2) + 64],
                               ke4[:, t, 256 * d + 64 * h:256 * d + 64 * h + 64],
                               u[:, t, GV + 64 * h:GV + 64 * h + 64], inc=filled if h == 3 else None)
                emptied("v")
                for t in tiles1(l):
                    b, filled = take("a")
                    for d in range(2):
                        for hp in range(2):
                            j = 2 * d + hp
                            mm(b[:, j * P:(j + 1) * P], la[:, t, j * P:(j + 1) * P],
                               const("up16" if d == 0 else "lo16"), inc=filled if j == 3 else None)
                    mark["bT", l, t] = k["a"]
                    fill()
                    fill()
                    pe.wait_ge(qk_ready, nth(qk_ready))
                    for par_ in range(2):
                        b, filled = take("s")
                        po = 64 * par_
                        for hp in range(2):
                            o = P * hp

                            def block_(j0, i0, n, kk, qq, d, o_=None, inc=None):
                                at = o + i0 if o_ is None else o_
                                mm(b[j0:j0 + n, at:at + n], kk[po:po + 64, 2 * d + hp, j0:j0 + n],
                                   qq[po:po + 64, 2 * d + hp, i0:i0 + n], inc=inc)

                            block_(0, 64, 64, qk64, qk64, 0)
                            block_(64, 0, 64, qk64, qk64, 1)
                            for B in (0, 64):
                                block_(B, B + 32, 32, qk32, qk32, 0)
                                block_(B + 32, B, 32, qk32, qk32, 1)
                            for B in range(0, P, 32):
                                block_(B, B, 32, kd, qd, 0)
                                block_(B, B, 32, kd, qd, 1, 256 + 32 * hp, filled if hp == 1 and B == 96 else None)
                    pe.wait_ge(AT_ready, nth(AT_ready))
                    for par_ in range(2):
                        b, filled = take("v")
                        po = 64 * par_
                        for hp in range(2):
                            o_ = b[:, 64 * hp:64 * hp + 64]
                            h = 2 * hp + par_
                            dirs = [d for d in range(2) if not (d == 0 and t == 2) and not (d == 1 and t == 3)]
                            mm(o_, AT[:, 2 * par_ + hp, :], u[:, t, GV + 64 * h:GV + 64 * h + 64], True, False)
                            for d in dirs:
                                j = 2 * d + hp
                                last = d == dirs[-1]
                                mm(o_, qi[po:po + 64, j, :], St[po:po + 64, t, 64 * j:64 * j + 64], False, last,
                                   filled if last and hp == 1 else None)

            def pooling(l):
                n = S if l == L - 1 else 512
                band = par1("band").rearrange("p (t g n) -> p t g n", t=2, g=4)
                for g in range(2):
                    b, filled = take("a")
                    for s in range(n // S):
                        for par_ in range(2):
                            for t in range(2):
                                end = s == n // S - 1 and par_ == 1 and t == 1
                                mm(b[64 * par_:64 * par_ + 64, S * s:S * s + S],
                                   u[:, 2 * s + t, P * g + 64 * par_:P * g + 64 * par_ + 64],
                                   band[:, t, 2 * g + par_, :], t == 0, t == 1, filled if end else None)
                emptied("a")
                for g in range(2):
                    b, filled = take("v")
                    mm(b[:, 0:n], par1("wpool").rearrange("p (g n) -> p g n", g=2)[:, g, :], mT[:, g, 0:n],
                       inc=filled)

            def attention1(l):
                for _ in range(2):
                    fill()
                pe.wait_ge(aq_ready, nth(aq_ready))
                tiles = tiles1(l)
                for j in range(4):
                    b, filled = take("va"[j % 2])
                    for n, t in enumerate(tiles):
                        tr(b[:, t * P:(t + 1) * P], u[:, t, AQ + P * j:AQ + P * (j + 1)],
                           filled if n == len(tiles) - 1 else None)
                for g in range(2):
                    b, filled = take("v")
                    for t in range(4):
                        tr(b[:, t * P:(t + 1) * P], kdup[:, t, P * g:P * (g + 1)], filled if t == 3 else None)
                emptied("v")
                emptied("a")
                units = units1(l)
                s0, a0 = k["s"], k["a"]
                for i in range(len(units) + 2):
                    if i < len(units):
                        t, h, k0 = units[i]
                        b, filled = take("s")
                        po = 64 * (h % 2)
                        mm(b[:, 0:512 - k0], qT[po:po + 64, h // 2, t * P:(t + 1) * P],
                           kT[po:po + 64, h // 4, k0:512], inc=filled)
                    if 1 <= i <= len(units):
                        t, h, k0 = units[i - 1]
                        pe.wait_ge(s_emptied, s0 + i)
                        b, filled = take("a")
                        n = (512 - k0) // P
                        for c in range(n):
                            tr(b[:, c * P:(c + 1) * P], Pr[:, (i - 1) % 2, c * P:(c + 1) * P],
                               filled if c == n - 1 else None)
                    if i >= 2:
                        t, h, k0 = units[i - 2]
                        pe.wait_ge(a_emptied, a0 + i - 1)
                        b, filled = take("v")
                        n = (512 - k0) // P
                        contract(b[:, 0:64], lambda c: PT[:, i % 2, c * P:(c + 1) * P],
                                 lambda c: u[:, k0 // P + c, AV + 64 * (h // 4):AV + 64 * (h // 4) + 64], filled, n)
                    if i < len(units) and i % 4 == 3:
                        fill()
                mark["pv1", l] = k["v"]

            def layer1(l):
                due.extend(MODS[12 * l + NFIRST:12 * l + NFIRST + 12])
                normed([0, 1, 2, 3], 2 * l)
                last_c, w = -1, None
                for c, t, lo, hi, r in in1_jobs(l):
                    if c != last_c:
                        last_c, w = c, weights(("in1", l, c))
                    b, filled = take(r)
                    linear(b[:, 0:hi - lo], lambda i: [x[:, i, t * P:(t + 1) * P] for x in (actT_r, act_lo_r)],
                           lambda i: [x[:, i, lo:hi] for x in w], filled)
                through()
                mark["in1", l] = k["a"]
                emptied("v")
                emptied("a")
                gla(l)
                pooling(l)
                attention1(l)
                emptied("v")
                for j in range(6):
                    b, filled = take("va"[j % 2])
                    for n, t in enumerate(tiles1(l)):
                        tr(b[:, t * P:(t + 1) * P], mixt[:, t, j * P:(j + 1) * P],
                           filled if n == len(tiles1(l)) - 1 else None)
                k["turned"] = 6
                mod_columns()
                for half in range(2):
                    w = weights(("out1", l, half))
                    for t in tiles1(l):
                        b, filled = take("v")
                        linear(b[:, :], lambda i: [x[:, i, t * P:(t + 1) * P] for x in (actT_r, mix_lo_r)],
                               lambda i: [x[:, i, :] for x in w], filled, [2, 3, 4, 5, 6, 7, 0, 1])
                normed(tiles1(l), 2 * l + 1)
                n = P * len(tiles1(l))
                for q in range(4):
                    for c in (2 * q, 2 * q + 1):
                        w = weights(("up1", l, c))
                        for m in range(4):
                            b, filled = take("va"[m % 2])
                            linear(b[:, 0:n], lambda i: [x[:, i, m * P:(m + 1) * P] for x in w],
                                   lambda i: [x[:, i, 0:n] for x in (actT_r, act_lo_r)], filled)
                        if c == 0:
                            mod_columns()
                    for half in range(2):
                        w = weights(("down1", l, 2 * q + half))
                        for t in tiles1(l):
                            b, filled = take("v")
                            for i in range(KT):
                                if t == 0 and half == 0:
                                    pe.wait_ge(hid_ready, nth(hid_ready))
                                three(b[:, :], [hid_hi[:, t, i, :], hid_lo_r[:, t, i, :]],
                                      [x[:, i, :] for x in w], i == 0, i == KT - 1, filled if i == KT - 1 else None)
                through()

            def layer2(l):
                due.extend(MODS[12 * (L + l) + NFIRST:12 * (L + l) + NFIRST + 12])
                normed([0, 1], 2 * (L + l))
                for c, (c0, c1) in enumerate(CH2):
                    w = weights(("in2", l, c))
                    for t in range(TS):
                        b, filled = take("va"[t])
                        linear(b[:, 0:c1 - c0], lambda i: [x[:, i, t * P:(t + 1) * P] for x in (actT_r, act2_lo_r)],
                               lambda i: [x[:, i, :] for x in w], filled)
                through()
                mark["in2", l] = k["a"]
                emptied("v")
                emptied("a")
                pe.wait_ge(par_in, nth(par_in, 16))
                for col in (QM, KM):
                    b, filled = take("a")
                    for hp in range(2):
                        for t in range(TS):
                            tr(b[:, S * hp + t * P:S * hp + (t + 1) * P], u2[:, t, col + P * hp:col + P * (hp + 1)],
                               filled if hp == 1 and t == 1 else None)
                fill()
                pe.wait_ge(lf_ready, nth(lf_ready))
                b, filled = take("v")
                mm(b[:, 0:4], const("up"), lf[:, 0, :])
                mm(b[:, 4:8], ones, lf[:, 0, :], True, False)
                mm(b[:, 4:8], const("up"), lf[:, 1, :], False, True, filled)
                fill()
                pe.wait_ge(lat_ready, nth(lat_ready))
                b, filled = take("v")
                for i in range(2):
                    for t in range(TS):
                        tr(b[:, S * i + t * P:S * i + (t + 1) * P], u2[:, t, CQ + i * P:CQ + (i + 1) * P],
                           filled if i == 1 and t == 1 else None)
                b, filled = take("v")
                for t in range(TS):
                    tr(b[:, t * P:(t + 1) * P], u2[:, t, CKV:KR], filled if t == 1 else None)
                emptied("v")
                wq = par2("w_uq").rearrange("p (k n) -> p k n", k=2)
                wkv = par2("w_ukv")
                for t in range(TS):
                    for n in range(2):
                        b, filled = take("v")
                        contract(b[:, 0:384], lambda i: cqT[:, i, t * P:(t + 1) * P],
                                 lambda i: wq[:, i, 384 * n:384 * (n + 1)], filled, 2)
                    for n in range(2):
                        b, filled = take("a")
                        mm(b[:, :], ckvT[:, t * P:(t + 1) * P], wkv[:, 512 * n:512 * (n + 1)], inc=filled)
                mark["kv", l] = k["a"]
                fill()
                pe.wait_ge(qa_ready, nth(qa_ready))
                for src, n in ((qa, 0), (ka, 1)):
                    for hp in range(2):
                        b, filled = take("va"[n])
                        for e in range(2):
                            for t in range(TS):
                                tr(b[0:66, S * e + t * P:S * e + (t + 1) * P], src[:, 4 * t + 2 * hp + e, :],
                                   filled if e == 1 and t == 1 else None)
                fill()
                pe.wait_ge(heads_ready, nth(heads_ready))
                emptied("a")
                for src, n in ((ql, 0), (kc, 1)):
                    for hp in range(4):
                        b, filled = take("va"[n])
                        for e in range(2):
                            for t in range(TS):
                                h = 2 * hp + e
                                tr(b[0:96, S * e + t * P:S * e + (t + 1) * P], src[:, t, 96 * h:96 * h + 96],
                                   filled if e == 1 and t == 1 else None)
                emptied("v")
                emptied("a")
                s0, a0 = k["s"], k["a"]
                for i in range(len(UNITS2) + 2):
                    if i < len(UNITS2):
                        kind, h, q = UNITS2[i]
                        n = P * (q + 1)
                        b, filled = take("s")
                        if kind == "fox":
                            lhs, rhs = qfT[0:66, h, q * P:(q + 1) * P], kfT[0:66, h, 0:n]
                        elif kind == "moba":
                            po = 64 * (h % 2)
                            lhs, rhs = qmT[po:po + 64, h // 2, q * P:(q + 1) * P], kmT[po:po + 64, h // 2, 0:n]
                        else:
                            lhs, rhs = qcT[0:96, h, q * P:(q + 1) * P], kcT[0:96, h, 0:n]
                        mm(b[:, 0:n], lhs, rhs, inc=filled)
                    if 1 <= i <= len(UNITS2):
                        kind, h, q = UNITS2[i - 1]
                        pe.wait_ge(p2_ready, nth(p2_ready))
                        b, filled = take("a")
                        for c in range(q + 1):
                            tr(b[:, c * P:(c + 1) * P], P2[:, (i - 1) % 2, c * P:(c + 1) * P],
                               filled if c == q else None)
                    if i >= 2:
                        kind, h, q = UNITS2[i - 2]
                        pe.wait_ge(a_emptied, a0 + i - 1)
                        b, filled = take("v")

                        def value(c):
                            if kind == "fox":
                                return u2[:, c, VF + 64 * h:VF + 64 * h + 64]
                            if kind == "moba":
                                return u2[:, c, VM + 64 * h:VM + 64 * h + 64]
                            return vv[:, c, 64 * h:64 * h + 64]
                        contract(b[:, 0:64], lambda c: PT2[:, i % 2, c * P:(c + 1) * P], value, filled, q + 1)
                    if i < len(UNITS2) and i % 4 == 3:
                        fill()
                mark["pv2", l] = k["v"]
                pe.wait_ge(mixt_ready, nth(mixt_ready))
                turn([0, 1], S, lambda ft, t: mix2[:, t, ft * P:(ft + 1) * P])
                k["turned"] = KT
                mod_columns()
                for half in range(2):
                    w = weights(("out2", l, half))
                    for t in range(TS):
                        b, filled = take("v")
                        linear(b[:, :], lambda i: [x[:, i, t * P:(t + 1) * P] for x in (actT_r, act2_lo_r)],
                               lambda i: [x[:, i, :] for x in w], filled)
                normed([0, 1], 2 * (L + l) + 1)
                for c in range(F2 // 256):
                    w = weights(("up2", l, c))
                    for m in range(2):
                        b, filled = take("s")
                        for g in range(2):
                            linear(b[:, S * g:S * (g + 1)],
                                   lambda i: [x[:, i, S * g + m * P:S * g + (m + 1) * P] for x in w],
                                   lambda i: [x[:, i, 0:S] for x in (actT_r, act2_lo_r)], filled if g == 1 else None)
                    if c == 0 and l < L - 1:
                        mod_columns()
                for half in range(2):
                    banks = [take("v") for t in range(TS)]
                    for c, (k0, k1) in enumerate(HC2):
                        w = weights(("down2", l, 3 * half + c))
                        for t, (b, filled) in enumerate(banks):
                            for i in range(k0, k1):
                                if t == 0 and half == 0:
                                    pe.wait_ge(hid_ready, nth(hid_ready))
                                three(b[:, :], [x[:, i, t * P:(t + 1) * P] for x in (hid2_hi, hid2_lo_r)],
                                      [x[:, i - k0, :] for x in w], i == 0, i == 21, filled if i == 21 else None)
                through()

            pe.wait_ge(cons_in, 16 * NCONS)
            pe.wait_ge(cT_ready, 1)
            for h in range(4):
                b, filled = take("v")
                mm(b[:, :], t5col[:, h, :], t5hot, inc=filled)
            due = MODS[:NFIRST]
            for _ in range(NFIRST):
                fill()
            mod_columns()
            for l in range(L):
                layer1(l)
            for l in range(L):
                layer2(l)

        @block.vector
        def _(dve):
            nth = counter()
            v = nc.vector

            def step(ins, signal=v_step):
                ins.then_inc(signal, 1)
                dve.wait_ge(signal, nth(signal))

            def filled(r="v"):
                banks, s = (VB, v_filled) if r == "v" else (SB, s_filled)
                n = nth(s)
                dve.wait_ge(s, n)
                return banks[(n - 1) % len(banks)]

            def emptied(ins, r="v"):
                ins.then_inc(v_emptied if r == "v" else s_emptied, 1)

            def tt(o, x, y, op):
                return v.tensor_tensor(o, x, y, op)

            def minus_abs(x):
                return v.scalar_tensor_tensor(out=x, in0=x, scalar=-1.0, in1=x, op0=ALU.mult, op1=ALU.min)

            def power(ins, at, n):
                ins.then_inc(ms_ready, 1)
                handed.append(("power", at, n))
                dve.wait_ge(rstd_ready, nth(rstd_ready))

            def rstd(parts):
                for i, (at, n, div) in enumerate(parts):
                    ins = v.tensor_scalar(ms[:, at:at + n], ss[:, at:at + n], 1.0 / div, EPS, ALU.mult, ALU.add)
                    if i < len(parts) - 1:
                        step(ins)
                power(ins, parts[0][0], parts[-1][0] + parts[-1][1] - parts[0][0])

            def mod_row():
                if not due:
                    return
                n = MODS.index(due.pop(0))
                m = 2 if n < 12 * L else 1
                dve.wait_ge(row_in[n % 3], 16 * (n // 3 + 1))
                dve.wait_ge(m_filled, n + 1)
                r = row[0:m, n % 3, :]
                step(tt(r, MB[n % 2][0:m, :], r, ALU.add), row_ready)

            def mod_columns(kind, l, part):
                m = 2 if kind == "mod1" else 1
                gain = gcol[:, (0 if kind == "mod1" else 2) + part, l, :]
                b = filled()
                src = b[:, 0:32].rearrange("p (v w k) -> p w k v", v=2, w=2)
                step(v.tensor_copy(modT[:, 0, :, 0:m], src[:, 0, :, 0:m]))
                step(v.scalar_tensor_tensor(out=modT[:, 1, :, 0:m], in0=src[:, 1, :, 0:m], scalar=1.0,
                                            in1=bc(gain, 2, m), op0=ALU.add, op1=ALU.mult), v_emptied)

            def norm_tile(t, n):
                dve.wait_ge(sq_ready, nth(sq_ready))
                rstd([(t, 1, D)])
                step(v.tensor_scalar(normal(n)[:, t, :], X[:, t, :], rs[:, t:t + 1], None, ALU.mult), xn_ready)

            def split(keys):
                for key in keys:
                    if key in P_SPLITS and ("split", key) not in handed:
                        handed.append(("split", key))
                    if key not in V_SPLITS:
                        continue
                    part = slice(0, min(share(key), lower(key).shape[1]))
                    dve.wait_ge(whi_ready, SPLITS.index(key) + 1)
                    step(tt(lower(key)[:, part], extent(slot(key), key)[:, part], upper(key)[:, part].bitcast(f32),
                            ALU.subtract), w_ready)

            def rest(lo, lo_r, hi, signal):
                step(tt(lo_r, lo, hi.bitcast(f32), ALU.subtract), signal)

            def turned(tiles, lo, lo_r):
                n = P * len(tiles)
                for ft in range(KT):
                    if ft % 2 == 0:
                        b = filled()
                        for s in range(len(tiles) // 2):
                            step(v.tensor_scalar(lo[:, ft, S * s:S * s + S], b[:, S * s:S * s + S],
                                                 modT[:, 1, ft, s:s + 1], modT[:, 0, ft, s:s + 1], ALU.mult, ALU.add),
                                 v_emptied if s == len(tiles) // 2 - 1 else v_step)
                        step(v.tensor_copy(actT_r[:, ft, 0:n], lo[:, ft, 0:n]))
                        rest(lo[:, ft, 0:n], lo_r[:, ft, 0:n], actT_r[:, ft, 0:n], act_ready)
                    else:
                        handed.append(("rest", lo_r[:, ft, 0:n], lo[:, ft, 0:n], actT_r[:, ft, 0:n]))

            def turned_mix(fts, n, lo, lo_r):
                for i, ft in enumerate(fts):
                    if i % 2 == 0:
                        b = filled()
                        step(v.tensor_copy(lo[:, ft, 0:n], b[:, 0:n]), v_emptied)
                        step(v.tensor_copy(actT_r[:, ft, 0:n], lo[:, ft, 0:n]))
                        rest(lo[:, ft, 0:n], lo_r[:, ft, 0:n], actT_r[:, ft, 0:n], act_ready)
                    else:
                        handed.append(("rest", lo_r[:, ft, 0:n], lo[:, ft, 0:n], actT_r[:, ft, 0:n]))

            def gla(l):
                dve.wait_ge(par_in, nth(par_in, 16))
                step(v.memset(rT[32:33, :], 1.0))
                b = filled()
                step(v.tensor_copy(rT[0:32, :], b[0:32, :]), v_emptied)
                for t in range(4):
                    b = filled()
                    step(v.tensor_scalar(la[:, t, :], b[:, :], 0.0, None, ALU.min))
                    step(v.scalar_tensor_tensor(out=zt[:, t, :], in0=la[:, t, :], scalar=2.0, in1=b[:, :],
                                                op0=ALU.mult, op1=ALU.subtract), v_emptied)
                aq_sums(l)
                for t in range(4):
                    dve.wait_ge(zlog_ready, nth(zlog_ready))
                    step(tt(la[:, t, :], la[:, t, :], zt[:, t, :], ALU.subtract), la_ready if t == 3 else v_step)
                mod_row()
                for t in range(4):
                    dve.wait_ge(a_emptied, mark["dec", l] + 1 + t)
                    for d in range(2):
                        o = ke4[:, t, 256 * d:256 * (d + 1)]
                        step(tt(o, o, u[:, t, GK:GV], ALU.mult), ke_ready if t == 3 and d == 1 else v_step)
                for n, pair in enumerate(STATES):
                    for d, (t, to) in enumerate(pair):
                        b = filled()
                        for hp in range(2):
                            j = 2 * d + hp
                            o = St[:, to, 64 * j:64 * j + 64]
                            part = b[:, 64 * hp:64 * hp + 64]
                            if n == 0:
                                ins = v.tensor_copy(o, part)
                            else:
                                ins = v.scalar_tensor_tensor(out=o, in0=St[:, t, 64 * j:64 * j + 64],
                                                             scalar=dec[:, 4 * t + j:4 * t + j + 1], in1=part,
                                                             op0=ALU.mult, op1=ALU.add)
                            step(ins, v_emptied if hp == 1 else v_step)
                mod_row()
                dve.wait_ge(rstd_ready, nth(rstd_ready))
                for t in tiles1(l):
                    dve.wait_ge(a_emptied, mark["bT", l, t])
                    for d in range(2):
                        j = slice(2 * d, 2 * d + 2)
                        src = bT[:, j, :]
                        step(tt(qk64[:, j, :], src, bT[:, j, 63 + d:64 + d].broadcast_to([P, 2, P]), ALU.subtract))
                        for dst, n in ((qk32, 64), (qd, 32)):
                            s4 = src.rearrange("p h (b i) -> p h b i", i=n)
                            ref = s4[:, :, :, n // 2 - 1 + d:n // 2 + d].broadcast_to([P, 2, P // n, n])
                            step(tt(dst[:, j, :].rearrange("p h (b i) -> p h b i", i=n), s4, ref, ALU.subtract))
                    step(minus_abs(qk96))
                    step(v.tensor_scalar(qd[:, :, :], qd[:, :, :], 80.0, -80.0, ALU.min, ALU.max), exps_in)
                    aq_norm(l, t)
                    mod_row()
                    aq_rope(t)
                    if l == L - 1:
                        aq_norm(l, t + 2)
                    dve.wait_ge(exps_out, nth(exps_out))
                    q, kk = qgT[:, :, t * P:(t + 1) * P], kgT[:, :, t * P:(t + 1) * P]
                    for d in range(2):
                        j = slice(2 * d, 2 * d + 2)
                        for dst, src in ((qd, q), (kd, kk), (qi, q)):
                            step(tt(dst[:, j, :], dst[:, j, :], src, ALU.mult))
                        for half in range(2):
                            src = q if half != d else kk
                            o = qk64[:, j, 64 * half:64 * half + 64]
                            step(tt(o, o, src[:, :, 64 * half:64 * half + 64], ALU.mult))
                            o = qk32[:, j, :].rearrange("p h (b g i) -> p h b g i", b=2, g=2)[:, :, :, half, :]
                            sv = src.rearrange("p h (b g i) -> p h b g i", b=2, g=2)[:, :, :, half, :]
                            step(tt(o, o, sv, ALU.mult), qk_ready if d == 1 and half == 1 else v_step)
                    for pr in range(2):
                        b = filled("s")
                        main = b[:, 0:256].rearrange("p (h i) -> p h i", h=2)
                        step(tt(AT[:, 2 * pr:2 * pr + 2, :], main, bc(const("mask_f"), 1, 2), ALU.mult))
                        diag = b[:, 256:320].rearrange("p (h i) -> p h i", h=2)
                        step(tt(atb[:, 2 * pr:2 * pr + 2, :], diag, bc(const("mask_b"), 1, 2), ALU.mult), s_emptied)
                    for B in range(0, P, 32):
                        o = AT[B:B + 32, :, B:B + 32]
                        step(tt(o, o, atb[B:B + 32, :, :], ALU.add), AT_ready if B == 96 else v_step)
                    mod_row()
                    for pr in range(2):
                        b = filled()
                        o = mixt[:, t, 0:256].rearrange("p (h e c) -> p h e c", h=2, e=2)[:, :, pr, :]
                        step(v.tensor_copy(o, b[:, 0:128].rearrange("p (h c) -> p h c", h=2)), v_emptied)
                n = len(tiles1(l))
                o = mixt[:, 0:n, 0:256]
                o4 = o.rearrange("p t (h c) -> p t h c", h=4)
                step(tt(gsq[:, 0:n, :], o, o, ALU.mult))
                step(v.tensor_reduce(ss[:, 0:4 * n].rearrange("p (t h) -> p t h", h=4),
                                     gsq[:, 0:n, :].rearrange("p t (h c) -> p t h c", h=4), X_AXIS, ALU.add))
                rstd([(0, 4 * n, 64)])
                mod_row()
                for t in range(n):
                    step(tt(o4[:, t], o4[:, t], bc(rs[:, 4 * t:4 * t + 4], 2, 64), ALU.mult))
                    step(tt(o4[:, t], o4[:, t], bc(par1("g_gla"), 1, 4), ALU.mult))
                g = gexp[:, 0:n, :]
                dve.wait_ge(gexp_ready, nth(gexp_ready))
                step(v.tensor_scalar(g, g, 1.0, None, ALU.add))
                step(v.reciprocal(g, g))
                step(tt(g, g, u[:, 0:n, GG:RF], ALU.mult))
                step(tt(o, o, g, ALU.mult))

            def rope(x1, x2, cos, sin, t1, t2):
                step(tt(t1, x1, sin, ALU.mult))
                step(tt(t2, x2, sin, ALU.mult))
                step(tt(x1, x1, cos, ALU.mult))
                step(tt(x2, x2, cos, ALU.mult))
                step(tt(x1, x1, t2, ALU.subtract))
                step(tt(x2, x2, t1, ALU.add))

            def span(l, t):
                return 0 if t in tiles1(l) else 8

            def aq_sums(l):
                for t in range(4):
                    if span(l, t) == 0:
                        x = u[:, t, AQ:AK].rearrange("p (a n) -> p a n", a=2)
                        step(tt(sqq, x, x, ALU.mult))
                        step(v.tensor_reduce(ss[:, 10 * t:10 * t + 8].rearrange("p (a h) -> p a h", a=2),
                                             sqq.rearrange("p a (h c) -> p a h c", c=64), X_AXIS, ALU.add))
                    x = u[:, t, AK:AV]
                    step(tt(sqk, x, x, ALU.mult))
                    step(v.tensor_reduce(ss[:, 10 * t + 8:10 * t + 10], sqk.rearrange("p (h c) -> p h c", c=64),
                                         X_AXIS, ALU.add))
                step(v.tensor_scalar(ms[:, 0:40], ss[:, 0:40], 1.0 / 64, EPS, ALU.mult, ALU.add), ms_ready)
                handed.append(("power", 0, 40))

            def aq_norm(l, t):
                h0 = span(l, t)
                x = u[:, t, AQ + 64 * h0:AV].rearrange("p (h c) -> p h c", c=64)
                step(tt(x, x, bc(rs[:, 10 * t + h0:10 * t + 10], 2, 64), ALU.mult))
                if h0 == 0:
                    step(tt(x[:, 0:8, :], x[:, 0:8, :], bc(par1("g_q"), 1, 8), ALU.mult))
                xk = x[:, 8 - h0:10 - h0, :]
                step(tt(xk, xk, bc(par1("g_k"), 1, 2), ALU.mult))

            def aq_rope(t):
                if t < TS:
                    table = const("rope1").rearrange("p (t c a f) -> p t c a f", t=2, c=2, a=2)
                    x = u[:, t, AQ:AV].rearrange("p (h a b f) -> p h a b f", a=2, b=2, f=16)
                    for axis in range(2):
                        t1 = mixt[:, 2, 256:416].rearrange("p (h f) -> p h f", f=16)
                        t2 = mixt[:, 3, 256:416].rearrange("p (h f) -> p h f", f=16)
                        rope(x[:, :, axis, 0, :], x[:, :, axis, 1, :], bc(table[:, t, 0, axis, :], 1, 10),
                             bc(table[:, t, 1, axis, :], 1, 10), t1, t2)

            def attention1(l):
                for t in range(4):
                    o = kdup[:, t, :].rearrange("p (g e c) -> p g e c", g=2, e=2)
                    k2 = u[:, t, AK:AV].rearrange("p (g c) -> p g c", g=2)
                    step(v.tensor_copy(o, bc(k2, 2, 2)), aq_ready if t == 3 else v_step)
                mod_row()
                n = P * len(tiles1(l))
                for g in range(2):
                    b = filled()
                    step(v.tensor_scalar(plo[:, g, 0:n], b[:, 0:n], spool[:, l, g:g + 1], None, ALU.mult), v_emptied)
                    step(v.tensor_copy(actT_r[:, g, 0:n], plo[:, g, 0:n]))
                for j in (0, 2):
                    b = filled()
                    step(v.tensor_copy(qT[:, j, 0:n], b[:, 0:n]), v_emptied)
                for g in range(2):
                    b = filled()
                    step(v.tensor_copy(kT[:, g, :], b[:, :]), v_emptied)
                units = units1(l)
                for i in range(len(units) + 2):
                    if i < len(units):
                        t, h, k0 = units[i]
                        if i % 4 == 2 and i > 2:
                            mod_row()
                        b = filled("s")
                        step(v.tensor_reduce(mx[:, i % 2:i % 2 + 1], b[:, 0:512 - k0], X_AXIS, ALU.max))
                        step(v.tensor_scalar(nm[:, i % 2:i % 2 + 1], mx[:, i % 2:i % 2 + 1], -0.125, None, ALU.mult),
                             nm_ready)
                    if i >= 2:
                        t, h, k0 = units[i - 2]
                        b = filled()
                        r = rinv[:, i % 2:i % 2 + 1]
                        step(v.reciprocal(r, rsum[:, (i - 2) % 4:(i - 2) % 4 + 1]))
                        step(v.tensor_scalar(mixt[:, t, 256 + 64 * h:320 + 64 * h], b[:, 0:64], r, None, ALU.mult),
                             v_emptied)
                nth(s_emptied, len(units))
                mod_row()

            def residual1(tiles, half, behind=None):
                c = slice(half * MODC, (half + 1) * MODC)
                for t in tiles:
                    b = filled()
                    step(tt(tmpx[:, t % 2, :], b[:, :], GA[:, t // 2, c], ALU.mult), v_emptied)
                    step(tt(X[:, t, c], X[:, t, c], tmpx[:, t % 2, :], ALU.add), x_ready if behind else v_step)
                    if behind:
                        behind(t)

            def layer1(l):
                due.extend(MODS[12 * l + NFIRST:12 * l + NFIRST + 12])
                if l == 0:
                    dve.wait_ge(t5_in, 16)
                    step(tt(t5[:, :, :], t5[:, :, :], bc(const("causal"), 1, 4), ALU.add))
                if l == 0:
                    split([("in1", 0, 0)])
                turned([0, 1, 2, 3], act_lo, act_lo_r)
                last_c = -1
                for c, t, lo, hi, r in in1_jobs(l):
                    if c != last_c:
                        last_c = c
                        split(after(("in1", l, c)))
                    if r == "v":
                        b = filled()
                        c0 = CH1[c][0]
                        step(v.tensor_copy(u[:, t, c0 + lo:c0 + hi], b[:, 0:hi - lo]), v_emptied)
                dve.wait_ge(a_emptied, mark["in1", l])
                gla(l)
                attention1(l)
                n = P * len(tiles1(l))
                handed.append(("split", ("out1", l, 0)))
                turned_mix(range(2, 8), n, mix_lo, mix_lo_r)
                step(tt(mix_lo_r[:, 0:2, 0:n], plo[:, :, 0:n], actT_r[:, 0:2, 0:n].bitcast(f32), ALU.subtract))
                split([("out1", l, 0)])
                mod_columns("mod1", l, 1)
                dve.wait_ge(ga_in, nth(ga_in, 32))
                for half in range(2):
                    split(after(("out1", l, half)))
                    residual1(tiles1(l), half, (lambda t: norm_tile(t, 2 * l + 1)) if half else None)
                turned(tiles1(l), act_lo, act_lo_r)
                dve.wait_ge(ga_in, nth(ga_in, 32))
                tiles = slice(0, len(tiles1(l)))
                for q in range(4):
                    for c in (2 * q, 2 * q + 1):
                        split(after(("up1", l, c)))
                        for m in range(4):
                            i = 4 * (c % 2) + m
                            low, high = hid_lo[:, tiles, i, :], hid_hi[:, tiles, i, :]
                            if m % 2 == 0:
                                b = filled()
                                step(v.tensor_scalar(low, b[:, 0:n].rearrange("p (t n) -> p t n", n=P), 0.0, None,
                                                     ALU.max), v_emptied)
                                step(tt(low, low, low, ALU.mult))
                                step(v.tensor_copy(high, low))
                            else:
                                dve.wait_ge(hsq_ready, nth(hsq_ready))
                            rest(low, hid_lo_r[:, tiles, i, :], high, hid_ready)
                        if c == 0:
                            mod_columns("mod1" if l < L - 1 else "mod2", (l + 1) % L, 0)
                    for half in range(2):
                        split(after(("down1", l, 2 * q + half)))
                        behind = None
                        if q == 3 and half == 1:
                            behind = (lambda t: norm_tile(t, 2 * l + 2)) if l < L - 1 else last_norm
                        residual1(tiles1(l), half, behind)

            def last_norm(t):
                dve.wait_ge(sq_ready, nth(sq_ready))
                rstd([(t, 1, D)])
                dve.wait_ge(gf_in, 16)
                step(v.scalar_tensor_tensor(out=X[:, t, :], in0=X[:, t, :], scalar=rs[:, t:t + 1], in1=gf,
                                            op0=ALU.mult, op1=ALU.mult), x_ready)
                norm_tile(t, 2 * L)

            def squares(o, src, at):
                step(v.tensor_tensor_reduce(out=o, in0=src, in1=src, scale=1.0, scalar=0.0, op0=ALU.mult,
                                            op1=ALU.add, accum_out=ss[:, at:at + 1]))

            def residual2(keys, behind):
                dve.wait_ge(ga_in, nth(ga_in, 32))
                step(tt(GA[:, 0, :], GA[:, 0, :], post, ALU.mult))
                for half in range(2):
                    c = slice(half * MODC, (half + 1) * MODC)
                    for key in keys[half]:
                        split(after(key))
                    for t in range(TS):
                        b = filled()
                        y = y2[:, t, c]
                        step(v.tensor_copy(y, b[:, :]), v_emptied)
                        squares(junk2, y, t)
                        mean = ms[:, t:t + 1]
                        if half == 0:
                            step(v.tensor_scalar(mean, ss[:, t:t + 1], 1.0 / D, EPS, ALU.mult, ALU.add))
                            step(tt(y, y, GA[:, 0, c], ALU.mult))
                        else:
                            v.scalar_tensor_tensor(out=mean, in0=ss[:, t:t + 1], scalar=1.0 / D, in1=mean,
                                                   op0=ALU.mult, op1=ALU.add).then_inc(ms_ready, 1)
                            handed.append(("power", t, 1))
                            step(tt(y, y, GA[:, 0, c], ALU.mult))
                for t in range(TS):
                    dve.wait_ge(rstd_ready, nth(rstd_ready))
                    step(v.scalar_tensor_tensor(out=X[:, t, :], in0=y2[:, t, :], scalar=rs[:, t:t + 1],
                                                in1=X[:, t, :], op0=ALU.mult, op1=ALU.add), x_ready)
                for t in range(TS):
                    behind(t)

            def layer2(l):
                due.extend(MODS[12 * (L + l) + NFIRST:12 * (L + l) + NFIRST + 12])
                turned([0, 1], act2_lo, act2_lo_r)
                for c, (c0, c1) in enumerate(CH2):
                    split(after(("in2", l, c)))
                    b = filled()
                    step(v.tensor_copy(u2[:, 0, c0:c1], b[:, 0:c1 - c0]), v_emptied)
                dve.wait_ge(a_emptied, mark["in2", l])
                dve.wait_ge(par_in, nth(par_in, 16))
                for t in range(TS):
                    step(tt(lft[:, t, :], u2[:, t, FL:QM], par2("b_forget"), ALU.add))
                step(v.tensor_scalar(lf[:, :, :], lft[:, :, :], 0.0, None, ALU.min))
                step(minus_abs(lft[:, :, :]), fneg_ready)
                for t in range(TS):
                    squares(tmp2[:, 0:256], u2[:, t, CQ:CKV], t)
                    squares(tmp2[:, 0:128], u2[:, t, CKV:KR], 2 + t)
                dve.wait_ge(flog_ready, nth(flog_ready))
                step(tt(lf[:, :, :], lf[:, :, :], lft[:, :, :], ALU.subtract), lf_ready)
                mod_row()
                rstd([(0, 2, 256), (2, 2, 128)])
                for t in range(TS):
                    for i, (c0, c1, g) in enumerate(((CQ, CKV, "g_q_lat"), (CKV, KR, "g_kv_lat"))):
                        x = u2[:, t, c0:c1]
                        step(v.scalar_tensor_tensor(out=x, in0=x, scalar=rs[:, 2 * i + t:2 * i + t + 1],
                                                    in1=par2(g), op0=ALU.mult, op1=ALU.mult),
                             lat_ready if t == 1 and i == 1 else v_step)
                b = filled()
                step(v.tensor_copy(Fc[:, :, :], b[:, 0:8].rearrange("p (t h) -> p t h", h=4)), v_emptied)
                mod_row()
                b = filled()
                step(v.tensor_copy(cqT[:, :, :], b[:, :].rearrange("p (k n) -> p k n", k=2)), v_emptied)
                b = filled()
                step(v.tensor_copy(ckvT, b[:, 0:S]), v_emptied)
                for t in range(TS):
                    h4 = slice(4 * t, 4 * t + 4)
                    step(v.tensor_scalar(qa[:, h4, 0:64], u2[:, t, QF:KF].rearrange("p (h c) -> p h c", h=4), 0.125,
                                         None, ALU.mult))
                    step(v.tensor_copy(ka[:, h4, 0:64], u2[:, t, KF:VF].rearrange("p (h c) -> p h c", h=4)))
                    step(v.tensor_copy(qa[:, h4, 65:66], bc(Fc[:, t, :], 2, 1)))
                    step(v.tensor_scalar(ka[:, h4, 64:65], bc(Fc[:, t, :], 2, 1), -1.0, None, ALU.mult))
                step(v.memset(qa[:, :, 64:65], 1.0))
                step(v.memset(ka[:, :, 65:66], 1.0), qa_ready)
                for t in range(TS):
                    for n in range(2):
                        b = filled()
                        step(v.tensor_copy(ql[:, t, 384 * n:384 * n + 384], b[:, 0:384]), v_emptied)
                mod_row()
                table = const("rope2").rearrange("p (t c f) -> p t c f", t=2, c=2)
                for t in range(TS):
                    q8 = ql[:, t, :].rearrange("p (h c) -> p h c", h=8)
                    t1 = tmp2[:, 0:128].rearrange("p (h f) -> p h f", f=16)
                    t2 = tmp2[:, 128:256].rearrange("p (h f) -> p h f", f=16)
                    rope(q8[:, :, 64:80], q8[:, :, 80:96], bc(table[:, t, 0, :], 1, 8), bc(table[:, t, 1, :], 1, 8),
                         t1, t2)
                    kr = u2[:, t, KR:IN2]
                    rope(kr[:, 0:16], kr[:, 16:32], table[:, t, 0, :], table[:, t, 1, :], tmp2[:, 0:16],
                         tmp2[:, 16:32])
                    k8 = kc[:, t, :].rearrange("p (h c) -> p h c", h=8)
                    step(v.tensor_copy(k8[:, :, 64:96], bc(kr, 1, 8)), heads_ready if t == 1 else v_step)
                for hp in range(2):
                    b = filled()
                    step(v.tensor_copy(qfT[0:66, 2 * hp:2 * hp + 2, :], b[0:66, :].rearrange("p (h n) -> p h n", h=2)),
                         v_emptied)
                for hp in range(4):
                    b = filled()
                    step(v.tensor_copy(qcT[0:96, 2 * hp:2 * hp + 2, :], b[0:96, :].rearrange("p (h n) -> p h n", h=2)),
                         v_emptied)
                mod_row()
                for i in range(len(UNITS2) + 2):
                    if i < len(UNITS2):
                        kind, h, q = UNITS2[i]
                        if i % 4 == 2 and i > 2:
                            mod_row()
                        n = P * (q + 1)
                        mask = (t5[:, h, :] if kind == "moba" else const("causal"))[:, S - n:S]
                        b = filled("s")
                        step(v.tensor_tensor_reduce(out=S2[:, i % 2, 0:n], in0=b[:, 0:n], in1=mask, scale=1.0,
                                                    scalar=-3.0e38, op0=ALU.add, op1=ALU.max,
                                                    accum_out=mx[:, i % 2:i % 2 + 1]), s_emptied)
                        step(v.tensor_scalar(nm[:, i % 2:i % 2 + 1], mx[:, i % 2:i % 2 + 1], -SCALE2[kind], None,
                                             ALU.mult), nm_ready)
                    if i >= 2:
                        kind, h, q = UNITS2[i - 2]
                        c0 = {"fox": 0, "moba": 256, "mla": 512}[kind] + 64 * h
                        b = filled()
                        r = rinv[:, i % 2:i % 2 + 1]
                        step(v.reciprocal(r, rsum[:, (i - 2) % 4:(i - 2) % 4 + 1]))
                        step(v.tensor_scalar(mix2[:, q, c0:c0 + 64], b[:, 0:64], r, None, ALU.mult), v_emptied)
                mod_row()
                groups = ((0, 256), (256, 512), (512, 1024))
                for g, (c0, c1) in enumerate(groups):
                    for t in range(TS):
                        squares(params[:, 0:c1 - c0], mix2[:, t, c0:c1], 2 * g + t)
                rstd([(0, 4, 256), (4, 2, 512)])
                split([("out2", l, 0)])
                for g, (c0, c1) in enumerate(groups):
                    for t in range(TS):
                        x = mix2[:, t, c0:c1]
                        step(v.scalar_tensor_tensor(out=x, in0=x, scalar=rs[:, 2 * g + t:2 * g + t + 1],
                                                    in1=par2("g_group")[:, c0:c1], op0=ALU.mult, op1=ALU.mult),
                             mixt_ready if g == 2 and t == 1 else v_step)
                turned_mix(range(KT), S, act2_lo, act2_lo_r)
                mod_columns("mod2", l, 1)
                residual2([[("out2", l, 0)], [("out2", l, 1)]], lambda t: norm_tile(t, 2 * (L + l) + 1))
                turned([0, 1], act2_lo, act2_lo_r)
                for m in range(F2 // P):
                    if m % 2 == 0:
                        split(after(("up2", l, m // 2)))
                    dve.wait_ge(sg_ready, nth(sg_ready))
                    b = filled("s")
                    g = sg2[:, m % 2, :]
                    step(v.tensor_scalar(g, g, 1.0, None, ALU.add))
                    step(v.reciprocal(g, g))
                    step(tt(g, g, b[:, 0:S], ALU.mult))
                    step(tt(hid2_lo[:, m, :], g, b[:, S:512], ALU.mult), s_emptied)
                    step(v.tensor_copy(hid2_hi[:, m, :], hid2_lo[:, m, :]))
                    rest(hid2_lo[:, m, :], hid2_lo_r[:, m, :], hid2_hi[:, m, :], hid_ready)
                    if m == 1 and l < L - 1:
                        mod_columns("mod2", l + 1, 0)
                residual2([[("down2", l, 3 * half + c) for c in range(3)] for half in range(2)],
                          lambda t: norm_tile(t, 2 * (L + l) + 2) if l < L - 1 else None)

            step(v.memset(ss[:, :], 0.0))
            dve.wait_ge(cons_in, 16 * NCONS)
            step(v.tensor_copy(t5col, bc(t5tab, 2, P)))
            dve.wait_ge(cexp_ready, 1)
            step(v.tensor_scalar(csig[:, :], csig[:, :], 1.0, None, ALU.add))
            step(v.reciprocal(csig[:, :], csig[:, :]))
            step(tt(cT[:, :, :].rearrange("p a k -> p (a k)"), cols[:, 0:24], csig[:, :], ALU.mult), cT_ready)
            for h in range(4):
                b = filled()
                step(v.tensor_scalar(t5rows[:, h, :], b[:, :], 8.0, None, ALU.mult), v_emptied)
            due = MODS[:NFIRST]
            for _ in range(NFIRST):
                mod_row()
            mod_columns("mod1", 0, 0)
            for t in range(4):
                norm_tile(t, 0)
            for l in range(L):
                layer1(l)
            for l in range(L):
                layer2(l)

        @block.scalar
        def _(act):
            nth = counter()

            def step(ins, signal=a_step):
                ins.then_inc(signal, 1)
                act.wait_ge(signal, nth(signal))

            def filled(r="a"):
                banks, s = (AB, a_filled) if r == "a" else (SB, s_filled)
                n = nth(s)
                act.wait_ge(s, n)
                return banks[(n - 1) % len(banks)]

            def f(o, x, func, **kw):
                return nc.scalar.activation(o, x, func, **kw)

            def stored(m0, m1):
                for m in range(m0, m1):
                    act.wait_ge(row_out[m % 3], 16 * (m // 3 + 1))

            def mod_loads(n):
                stored(6 * n + 1, 6 * n + 4)
                i, part = n // 2, n % 2
                for vec in range(2):
                    src = a["mods"][i, vec, 3 * D * part:3 * D * part + 2 * D].rearrange("(k p) -> k p", p=P)
                    act.dma_start(modrow[16 * vec:16 * vec + 16, :], src).then_inc(modrow_in, 16)

            def gate_loads(n):
                stored(6 * n + 3, 6 * n + 6)
                i, part = n // 2, n % 2
                gates = a["mods"][i:i + 1, :, 3 * D * part + 2 * D:3 * D * part + 3 * D]
                act.dma_start(GA[:, 0, :], gates[:, 0, :].partition_broadcast(P)).then_inc(ga_in, 16)
                if i < L:
                    src = gates[:, 1, :]
                else:
                    src = a["g_mix_post_2" if part == 0 else "g_ffn_post_2"][i - L:i - L + 1, :]
                act.dma_start(GA[:, 1, :], src.partition_broadcast(P)).then_inc(ga_in, 16)

            def normed(tiles, n):
                for t in tiles:
                    for _ in range(2 if n == 2 * L else 1):
                        if n:
                            act.wait_ge(x_ready, nth(x_ready))
                        step(f(normal(n)[:, t, :], X[:, t, :], ACT.Square, accum_out=ss[:, t:t + 1]), sq_ready)
                gate_loads(n)
                lo = act_lo if n < 2 * L else act2_lo
                n = P * len(tiles)
                for ft in range(1, KT, 2):
                    b = filled()
                    for s in range(len(tiles) // 2):
                        last = s == len(tiles) // 2 - 1
                        step(f(lo[:, ft, S * s:S * s + S], b[:, S * s:S * s + S], ACT.Identity,
                               scale=modT[:, 1, ft, s:s + 1], bias=modT[:, 0, ft, s:s + 1]),
                             a_emptied if last else a_step)
                    step(f(actT_r[:, ft, 0:n], lo[:, ft, 0:n], ACT.Copy), acth_ready)

            def split(keys):
                for key in keys:
                    slot_wait(act, key)
                    i = SPLITS.index(key)
                    if i >= 2:
                        act.wait_ge(slot_read, i - 1)
                    if key[0] == "out1" and key[2] == 1:
                        act.wait_ge(w_ready, V_SPLITS.index(SPLITS[i - 1]) + 1)
                    step(f(upper(key), extent(slot(key), key), ACT.Copy), whi_ready)

            def turned_mix(fts, n, lo):
                for ft in fts:
                    b = filled()
                    step(f(lo[:, ft, 0:n], b[:, 0:n], ACT.Copy), a_emptied)
                    step(f(actT_r[:, ft, 0:n], lo[:, ft, 0:n], ACT.Copy), acth_ready)

            def softplus(x, out_):
                step(f(x, x, ACT.Exp))
                step(f(x, x, ACT.Ln, bias=1.0), out_)

            def layer1(l):
                n = P * len(tiles1(l))
                if l == 0:
                    split([("in1", 0, 0)])
                normed([0, 1, 2, 3], 2 * l)
                last_c = -1
                for c, t, lo, hi, r in in1_jobs(l):
                    if c != last_c:
                        last_c = c
                        split(after(("in1", l, c)))
                    if r == "a":
                        b = filled()
                        c0 = CH1[c][0]
                        step(f(u[:, t, c0 + lo:c0 + hi], b[:, 0:hi - lo], ACT.Copy), a_emptied)
                for t in range(4):
                    act.wait_ge(v_emptied, mark["z", l, t])
                    step(f(zt[:, t, :], zt[:, t, :], ACT.Exp))
                for t in range(4):
                    step(f(zt[:, t, :], zt[:, t, :], ACT.Ln, bias=1.0), zlog_ready)
                for dst, scale in ((qgT, 0.125), (kgT, 1.0)):
                    for hp in range(2):
                        b = filled()
                        step(f(dst[:, hp, 0:n], b[:, 0:n], ACT.Copy, scale=scale), a_emptied)
                b = filled()
                step(f(dec, b[:, 0:16], ACT.Exp), a_emptied)
                for t in range(4):
                    b = filled()
                    step(f(ke4[:, t, :], b[:, :], ACT.Exp), a_emptied)
                for t in tiles1(l):
                    b = filled()
                    step(f(bT[:, :, :], b[:, :].rearrange("p (j n) -> p j n", j=4), ACT.Copy), a_emptied)
                    act.wait_ge(exps_in, nth(exps_in))
                    step(f(qk96, qk96, ACT.Exp))
                    step(f(kd[:, :, :], qd[:, :, :], ACT.Exp, scale=-1.0))
                    step(f(qd[:, :, :], qd[:, :, :], ACT.Exp))
                    step(f(qi[:, :, :], bT[:, :, :], ACT.Exp), exps_out)
                    act.wait_ge(qk_ready, nth(qk_ready))
                step(f(gexp[:, 0:len(tiles1(l)), :], u[:, 0:len(tiles1(l)), GG:RF], ACT.Exp, scale=-1.0), gexp_ready)
                for g in range(2):
                    b = filled()
                    step(f(mT[:, g, 0:n], b[:, 0:n], ACT.Copy), a_emptied)
                for sem_ in (s_filled, s_emptied):
                    nth(sem_, 2 * len(tiles1(l)))
                for j in (1, 3):
                    b = filled()
                    step(f(qT[:, j, 0:n], b[:, 0:n], ACT.Copy), a_emptied)
                units = units1(l)
                for i in range(len(units) + 1):
                    if i < len(units):
                        k0 = units[i][2]
                        act.wait_ge(nm_ready, nth(nm_ready))
                        b = filled("s")
                        step(f(Pr[:, i % 2, 0:512 - k0], b[:, 0:512 - k0], ACT.Exp, bias=nm[:, i % 2:i % 2 + 1],
                               scale=0.125, accum_out=rsum[:, i % 4:i % 4 + 1]), s_emptied)
                    if i >= 1:
                        k0 = units[i - 1][2]
                        b = filled()
                        step(f(PT[:, (i - 1) % 2, 0:512 - k0], b[:, 0:512 - k0], ACT.Copy), a_emptied)
                mod_loads(2 * l + 1)
                act.wait_ge(v_filled, mark["pv1", l])
                split([("out1", l, 0)])
                turned_mix((3, 5, 7), n, mix_lo)
                if l == L - 1:
                    act.dma_start(gf, a["g_final"].partition_broadcast(P)).then_inc(gf_in, 16)
                for half in range(2):
                    split(after(("out1", l, half)))
                normed(tiles1(l), 2 * l + 1)
                mod_loads(2 * l + 2)
                tiles = slice(0, len(tiles1(l)))
                for q in range(4):
                    for c in (2 * q, 2 * q + 1):
                        split(after(("up1", l, c)))
                        for m in (1, 3):
                            i = 4 * (c % 2) + m
                            b = filled()
                            low = hid_lo[:, tiles, i, :]
                            step(f(low, b[:, 0:n].rearrange("p (t n) -> p t n", n=P), ACT.Relu), a_emptied)
                            step(f(low, low, ACT.Square))
                            step(f(hid_hi[:, tiles, i, :], low, ACT.Copy), hsq_ready)
                    for half in range(2):
                        split(after(("down1", l, 2 * q + half)))

            def layer2(l):
                normed([0, 1], 2 * (L + l))
                for c, (c0, c1) in enumerate(CH2):
                    split(after(("in2", l, c)))
                    b = filled()
                    step(f(u2[:, 1, c0:c1], b[:, 0:c1 - c0], ACT.Copy), a_emptied)
                for dst in (qmT, kmT):
                    b = filled()
                    step(f(dst[:, :, :], b[:, :].rearrange("p (h n) -> p h n", h=2), ACT.Copy), a_emptied)
                act.wait_ge(fneg_ready, nth(fneg_ready))
                softplus(lft[:, :, :], flog_ready)
                for t in range(TS):
                    for n in range(2):
                        b = filled()
                        kv = b[:, :].rearrange("p (h e c) -> p h e c", h=4, e=2)
                        k8 = kc[:, t, :].rearrange("p (h c) -> p h c", h=8)
                        step(f(k8[:, 4 * n:4 * n + 4, 0:64], kv[:, :, 0, :], ACT.Copy))
                        step(f(vv[:, t, 256 * n:256 * n + 256].rearrange("p (h c) -> p h c", h=4), kv[:, :, 1, :],
                               ACT.Copy), a_emptied)
                for hp in range(2):
                    b = filled()
                    step(f(kfT[0:66, 2 * hp:2 * hp + 2, :], b[0:66, :].rearrange("p (h n) -> p h n", h=2), ACT.Copy),
                         a_emptied)
                for hp in range(4):
                    b = filled()
                    step(f(kcT[0:96, 2 * hp:2 * hp + 2, :], b[0:96, :].rearrange("p (h n) -> p h n", h=2), ACT.Copy),
                         a_emptied)
                for i in range(len(UNITS2) + 1):
                    if i < len(UNITS2):
                        kind, h, q = UNITS2[i]
                        n = P * (q + 1)
                        act.wait_ge(nm_ready, nth(nm_ready))
                        step(f(P2[:, i % 2, 0:n], S2[:, i % 2, 0:n], ACT.Exp, bias=nm[:, i % 2:i % 2 + 1],
                               scale=SCALE2[kind], accum_out=rsum[:, i % 4:i % 4 + 1]), p2_ready)
                    if i >= 1:
                        n = P * (UNITS2[i - 1][2] + 1)
                        b = filled()
                        step(f(PT2[:, (i - 1) % 2, 0:n], b[:, 0:n], ACT.Copy), a_emptied)
                mod_loads(2 * (L + l) + 1)
                act.wait_ge(v_filled, mark["pv2", l])
                split([("out2", l, 0)])
                turned_mix((1, 3, 5, 7), S, act2_lo)
                nth(s_filled, len(UNITS2))
                for half in range(2):
                    split(after(("out2", l, half)))
                normed([0, 1], 2 * (L + l) + 1)
                if l < L - 1:
                    mod_loads(2 * (L + l) + 2)
                for m in range(F2 // P):
                    if m % 2 == 0:
                        split(after(("up2", l, m // 2)))
                    b = filled("s")
                    step(f(sg2[:, m % 2, :], b[:, 0:S], ACT.Exp, scale=-1.0), sg_ready)
                for c in range(2 * len(HC2)):
                    split(after(("down2", l, c)))

            act.dma_start(cons[:, :], a["cons"]).then_inc(cons_in, 16)
            act.dma_start(cols[:, :], a["cols"]).then_inc(cons_in, 16)
            act.dma_start(t5tab, a["t5_table_2"]).then_inc(cons_in, 16)
            act.dma_start(t5hot, a["t5hot"]).then_inc(cons_in, 16)
            act.dma_start(X[:, 0:2, :], a["x"][0].rearrange("(t p) d -> p t d", p=P)).then_inc(x_in, 16)
            act.dma_start(X[:, 2:4, :], a["ctx"][0].rearrange("(t p) d -> p t d", p=P)).then_inc(x_in, 16)
            act.wait_ge(cons_in, 16 * NCONS)
            step(f(csig[:, :], cols[:, 0:24], ACT.Exp, scale=-1.0), cexp_ready)
            act.wait_ge(x_in, 32)
            act.wait_ge(cT_ready, 1)
            mod_loads(0)
            for l in range(L):
                layer1(l)
            for l in range(L):
                layer2(l)

        @block.gpsimd
        def _(pool):
            nc.gpsimd.memset(neghalf[:, :], -0.5).then_inc(pool_ready, 1)
            pool.wait_ge(v_emptied, 4)
            pool.dma_start(a["t5_rows"], t5rows).then_inc(t5_stored, 16)
            pool.wait_ge(t5_stored, 16)
            band_src = bass.AP(tensor=a["t5_rows"].tensor, offset=P - 1, ap=[[4 * 512 - 1, P], [512, 4], [1, S]])
            pool.dma_start(t5[:, :, :], band_src).then_inc(t5_in, 16)
            pool.wait_ge(pool_ready, 1)
            nth = counter()
            for kind, *what in handed:
                if kind == "power":
                    at, n = what
                    pool.wait_ge(ms_ready, nth(ms_ready))
                    nc.gpsimd.tensor_tensor(rs[:, at:at + n], ms[:, at:at + n], neghalf[:, at:at + n], ALU.pow)\
                      .then_inc(rstd_ready, 1)
                elif kind == "rest":
                    low, value, high = what
                    pool.wait_ge(acth_ready, nth(acth_ready))
                    nc.gpsimd.tensor_tensor(low, value, high.bitcast(f32), ALU.subtract).then_inc(actp_ready, 1)
                else:
                    key = what[0]
                    pool.wait_ge(whi_ready, SPLITS.index(key) + 1)
                    part = slice(share(key), KT)
                    nc.gpsimd.tensor_tensor(lower(key)[:, part], extent(slot(key), key)[:, part],
                                            upper(key)[:, part].bitcast(f32), ALU.subtract).then_inc(wp_ready, 1)


def bucket(dist):
    n = np.maximum(dist, 0)
    nf = np.maximum(n, 16).astype(np.float32)
    large = 16 + (np.log(nf / np.float32(16)) / np.float32(math.log(8)) * np.float32(16)).astype(np.int32)
    return np.where(n < 16, n, np.minimum(large, 31))


def constants():
    i = np.arange(P)
    t, j = i[:, None], i[None, :]
    out = {}
    out["ident"] = t == j
    out["up16"] = (t <= j) / 16.0
    out["lo16"] = (t >= j) / 16.0
    out["after16"] = (t > j) / 16.0
    out["before16"] = (t < j) / 16.0
    out["up"] = t <= j
    out["ones"] = np.ones((P, P))
    out["mask_f"] = (t // 32 != j // 32) | (t <= j)
    out["mask_b"] = (t % 32) > np.arange(32)[None, :]
    out["causal"] = np.concatenate([np.zeros((P, P)), np.where(j <= t, 0.0, NEG)], 1)
    inv1 = np.float32(10000.0) ** (-np.arange(0, 32, 2, dtype=np.float32) / np.float32(32))
    tok = np.arange(S)
    axes = np.stack([tok // 64, tok % 64], 1).astype(np.float32)
    ang = axes[:, :, None] * inv1
    r1 = np.stack([np.cos(ang), np.sin(ang)], 1)
    out["rope1"] = r1.reshape(TS, P, 64).transpose(1, 0, 2).reshape(P, 128)
    inv2 = np.float32(1.0) / (np.float32(10000.0) ** (np.arange(16, dtype=np.float32) / np.float32(16)))
    ang = tok.astype(np.float32)[:, None] * inv2
    r2 = np.stack([np.cos(ang), np.sin(ang)], 1)
    out["rope2"] = r2.reshape(TS, P, 32).transpose(1, 0, 2).reshape(P, 64)
    cons = np.concatenate([out[n].astype(np.float32) for n, _ in CONST], 1)
    hot = np.zeros((32, 512), np.float32)
    e = np.arange(256)
    hot[bucket(255 - e), e] = 1
    band = np.zeros((4, S, S), np.float32)
    for g, w in enumerate((2, 4, 8, 16)):
        lo, hi = np.clip(tok - w // 2, 0, S - 1), np.clip(tok + w // 2 - 1, 0, S - 1)
        inside = (tok[:, None] >= lo[None, :]) & (tok[:, None] <= hi[None, :])
        band[g] = inside / (hi - lo + 1)[None, :].astype(np.float32) - np.eye(S)
    band = band.reshape(4, TS, P, S).transpose(2, 1, 0, 3).reshape(P, 2048)
    return cons, hot, band


def kernel(**inputs):
    import concourse.bacc as _bacc
    from concourse import mybir as _mybir
    from concourse.bass_utils import run_bass_kernel_spmd as _run

    x = {k: np.ascontiguousarray(v) for k, v in inputs.items()}
    cons, hot, band = constants()

    def columns(w):
        return w.reshape(-1, P).T

    cols = np.concatenate([columns(x[n]) for n in ("c", "c_ctx", "c_2", "g_mix", "g_mlp", "g_mix_pre_2",
                                                   "g_ffn_pre_2", "s_pool")], 1)
    par1 = np.zeros((L, P, sum(n for _, n in PAR1)), np.float32)
    par2 = np.zeros((L, P, sum(n for _, n in PAR2)), np.float32)
    at1, at2 = offsets(PAR1)[0], offsets(PAR2)[0]

    def put(dst, at, name, value):
        s, n = at[name]
        dst[:, s:s + n] = value

    for l in range(L):
        put(par1[l], at1, "band", band)
        wg = np.zeros((P, 512), np.float32)
        wg[0:16, 0:256], wg[16:32, 256:512] = x["w_gate"][l, 0], x["w_gate"][l, 1]
        wg[32, 0:256], wg[32, 256:512] = x["b_gate"][l, 0], x["b_gate"][l, 1]
        put(par1[l], at1, "wg", wg)
        wp = np.zeros((P, 2, P), np.float32)
        for g in range(4):
            o = 64 * (g % 2)
            wp[o:o + 64, g // 2, o:o + 64] = x["w_pool"][l, g]
        put(par1[l], at1, "wpool", wp.reshape(P, 256))
        for n in ("g_q", "g_k", "g_gla"):
            put(par1[l], at1, n, x[n][l][None, :])
        put(par2[l], at2, "w_uq", x["w_uq_2"][l].reshape(2, P, 768).transpose(1, 0, 2).reshape(P, 1536))
        put(par2[l], at2, "w_ukv", x["w_ukv_2"][l])
        for n in ("g_q_lat", "g_kv_lat", "g_group", "b_forget"):
            put(par2[l], at2, n, x[n + "_2"][l][None, :])
    arrays = {"cons": cons, "cols": cols, "t5hot": hot, "par1": par1, "par2": par2}
    for n in ("x", "ctx", "w_mod", "b_mod", "w_in", "w_out", "w_up", "w_down", "g_final", "t5_table_2", "w_ada_2",
              "b_ada_2", "g_mix_post_2", "w_in_2", "w_out_2", "g_ffn_post_2", "w_gate_up_2", "w_down_2"):
        arrays[n] = x[n]
    arrays["g_final"] = x["g_final"].reshape(1, D)

    nc = _bacc.Bacc("TRN2", target_bir_lowering=False, num_devices=1)
    feed, aps = {}, {}
    for n, v in arrays.items():
        v = np.ascontiguousarray(v)
        feed[f"in_{n}"] = v
        aps[n] = nc.dram_tensor(f"in_{n}", v.shape, _mybir.dt.from_np(v.dtype), kind="ExternalInput").ap()
    aps["mods"] = nc.dram_tensor("mods", [2 * L, 2, 6 * D], _mybir.dt.float32, kind="Internal").ap()
    aps["t5_rows"] = nc.dram_tensor("t5_rows", [P, 4, 512], _mybir.dt.float32, kind="Internal").ap()
    out = nc.dram_tensor("out", (1, S, D), _mybir.dt.float32, kind="ExternalOutput").ap()
    trunks(nc, aps, out)
    r = _run(nc, [feed], core_ids=[0])
    return r.results[0]["out"]
```
